# Optimizing a Trainium2 kernel written in Bass

```python
import jax, jax.numpy as jnp
from jax import lax
import numpy as np
import math

D_MODEL = 1024
BATCH = 1
SEQ = 256
DEPTH = 2

CHUNK = 64
N_MIXERS = 2
N_LAYERS_A = (DEPTH + 1) // 2
N_LAYERS_B = DEPTH // 2
SGU_BLOCK = 128
SGU_WIDTH = 2 * D_MODEL
SGU_GROUPS = 16
SGU_GROUP_DIM = SGU_WIDTH // SGU_GROUPS
RWKV_HEAD_DIM = 64
RWKV_HEADS = D_MODEL // RWKV_HEAD_DIM
DECAY_LORA = 64
AAA_LORA = 64
MV_LORA = 32
GATE_LORA = 128
FFN_HIDDEN = 4 * D_MODEL
RMS_EPS = 1e-6
LN_EPS = 1e-5
GN_EPS = 64e-5


def _rmsnorm(x, g):
    xf = x.astype(jnp.float32)
    y = xf * lax.rsqrt(jnp.mean(xf * xf, axis=-1, keepdims=True) + RMS_EPS)
    return (y * g.astype(jnp.float32)).astype(x.dtype)

def _layernorm(x, g, b, eps):
    xf = x.astype(jnp.float32)
    mu = jnp.mean(xf, axis=-1, keepdims=True)
    var = jnp.mean(jnp.square(xf - mu), axis=-1, keepdims=True)
    y = (xf - mu) * lax.rsqrt(var + eps)
    return (y * g.astype(jnp.float32) + b.astype(jnp.float32)).astype(x.dtype)

def _sgu_mask():
    chunk_id = jnp.arange(SGU_BLOCK) // CHUNK
    return chunk_id[None, :] <= chunk_id[:, None]

def _spatial_gating_mixer(h, w_in, b_in, ln_g, ln_b, w_s, b_s, w_out):
    bsz, seq, _ = h.shape
    z = jax.nn.gelu(h @ w_in + b_in, approximate=False)
    u, v = jnp.split(z, 2, axis=-1)
    v = _layernorm(v, ln_g, ln_b, LN_EPS)
    v = v.reshape(bsz, seq // SGU_BLOCK, SGU_BLOCK, SGU_GROUPS, SGU_GROUP_DIM)
    w_s = w_s * _sgu_mask()[None].astype(w_s.dtype)
    s = jnp.einsum('gij,bnjgc->bnigc', w_s, v) + b_s.T[None, None, :, :, None]
    y = u * s.reshape(bsz, seq, SGU_WIDTH)
    return y @ w_out

def _wkv7_scan(r, w, k, v, kk, kka):
    bsz, _, nh, n = r.shape
    xs = tuple(jnp.moveaxis(t, 1, 0) for t in (r, w, k, v, kk, kka))

    def step(S, inp):
        r_t, w_t, k_t, v_t, kk_t, kka_t = inp
        sa = jnp.einsum('bhvk,bhk->bhv', S, -kk_t)
        S = (S * w_t[:, :, None, :] + sa[..., None] * kka_t[:, :, None, :]
             + v_t[..., None] * k_t[:, :, None, :])
        y = jnp.einsum('bhvk,bhk->bhv', S, r_t)
        return S, y

    S0 = jnp.zeros((bsz, nh, n, n), jnp.float32)
    _, y = lax.scan(step, S0, xs)
    return jnp.moveaxis(y, 0, 1)

def _rwkv7_mixer(h, mu, w_rkv, w0, w_la, w_lb, a0, a_la, a_lb, g_la, g_lb,
                 k_k, k_a, r_k, ln_g, ln_b, w_o, v_first, v_mix):
    bsz, seq, d = h.shape
    f32 = jnp.float32

    def heads(t):
        return t.reshape(bsz, seq, RWKV_HEADS, RWKV_HEAD_DIM)

    xx = jnp.pad(h, ((0, 0), (1, 0), (0, 0)))[:, :-1] - h
    xs = h[None] + xx[None] * mu[:, None, None, :]
    rkv = jnp.einsum('pbtd,pde->pbte', xs[:3], w_rkv)
    r, k, v = rkv[0], rkv[1], rkv[2]
    xv, xw, xa, xg = xs[2], xs[3], xs[4], xs[5]
    log_w = -jax.nn.softplus(-(w0 + jnp.tanh(xw @ w_la) @ w_lb)) - 0.5
    decay = jnp.exp(-jnp.exp(log_w.astype(f32)))
    if v_mix is None:
        v_first = v
    else:
        v0, v_la, v_lb = v_mix
        v = v + (v_first - v) * jax.nn.sigmoid(v0 + (xv @ v_la) @ v_lb)
    a = jax.nn.sigmoid(a0 + (xa @ a_la) @ a_lb)
    g = jax.nn.sigmoid(xg @ g_la) @ g_lb
    kk = heads(k * k_k).astype(f32)
    kk = kk / jnp.maximum(jnp.sqrt(jnp.sum(kk * kk, axis=-1, keepdims=True)), 1e-12)
    k = k * (1.0 + (a - 1.0) * k_a)
    r_h, k_h, v_h = heads(r).astype(f32), heads(k).astype(f32), heads(v).astype(f32)
    y = _wkv7_scan(r_h, heads(decay), k_h, v_h, kk, kk * heads(a).astype(f32))
    mu_y = jnp.mean(y, axis=-1, keepdims=True)
    var_y = jnp.mean(jnp.square(y - mu_y), axis=-1, keepdims=True)
    y = ((y - mu_y) * lax.rsqrt(var_y + GN_EPS)).reshape(bsz, seq, d)
    y = y * ln_g.astype(f32) + ln_b.astype(f32)
    bonus = jnp.sum(r_h * k_h * r_k.astype(f32), axis=-1, keepdims=True) * v_h
    y = (y + bonus.reshape(bsz, seq, d)) * g.astype(f32)
    return y.astype(h.dtype) @ w_o, v_first

def _squared_relu_mlp(h, w1, w2):
    return jnp.square(jax.nn.relu(h @ w1)) @ w2

def first_inputs(seed: int = 0) -> dict:
    key = jax.random.key(seed)
    ks = jax.random.split(key, 32)
    f32 = jnp.float32
    D, E, G, H, N = D_MODEL, SGU_WIDTH, SGU_GROUPS, RWKV_HEADS, RWKV_HEAD_DIM
    nA, nB = N_LAYERS_A, N_LAYERS_B

    def nrm(k, shape, scale):
        return jax.random.normal(k, shape, f32) * scale

    return {
        "x": nrm(ks[0], (BATCH, SEQ, D), 1.0),
        "norm_mix_g": 1.0 + nrm(ks[1], (DEPTH, D), 0.05),
        "norm_ffn_g": 1.0 + nrm(ks[2], (DEPTH, D), 0.05),
        "final_norm_g": 1.0 + nrm(ks[3], (D,), 0.05),
        "ffn_w1": nrm(ks[4], (DEPTH, D, FFN_HIDDEN), D ** -0.5),
        "ffn_w2": nrm(ks[5], (DEPTH, FFN_HIDDEN, D), 0.5 * FFN_HIDDEN ** -0.5),
        "sgu_w_in": nrm(ks[6], (nA, D, 2 * E), D ** -0.5),
        "sgu_b_in": nrm(ks[7], (nA, 2 * E), 0.02),
        "sgu_ln_g": 1.0 + nrm(ks[8], (nA, E), 0.05),
        "sgu_ln_b": nrm(ks[9], (nA, E), 0.02),
        "sgu_w_s": nrm(ks[10], (nA, G, SGU_BLOCK, SGU_BLOCK), SGU_BLOCK ** -0.5),
        "sgu_b_s": 1.0 + nrm(ks[11], (nA, G, SGU_BLOCK), 0.1),
        "sgu_w_out": nrm(ks[12], (nA, E, D), 0.5 * E ** -0.5),
        "rwkv_mu": jax.random.uniform(ks[13], (nB, 6, D), f32),
        "rwkv_w_rkv": nrm(ks[14], (nB, 3, D, D), D ** -0.5),
        "rwkv_w0": jax.random.uniform(ks[15], (nB, D), f32, -6.0, 0.5),
        "rwkv_w_lora_a": nrm(ks[16], (nB, D, DECAY_LORA), D ** -0.5),
        "rwkv_w_lora_b": nrm(ks[17], (nB, DECAY_LORA, D), 0.3 * DECAY_LORA ** -0.5),
        "rwkv_a0": nrm(ks[18], (nB, D), 0.1),
        "rwkv_a_lora_a": nrm(ks[19], (nB, D, AAA_LORA), D ** -0.5),
        "rwkv_a_lora_b": nrm(ks[20], (nB, AAA_LORA, D), 0.3 * AAA_LORA ** -0.5),
        "rwkv_v0": 0.5 + nrm(ks[21], (nB - 1, D), 0.1),
        "rwkv_v_lora_a": nrm(ks[22], (nB - 1, D, MV_LORA), D ** -0.5),
        "rwkv_v_lora_b": nrm(ks[23], (nB - 1, MV_LORA, D), 0.3 * MV_LORA ** -0.5),
        "rwkv_g_lora_a": nrm(ks[24], (nB, D, GATE_LORA), D ** -0.5),
        "rwkv_g_lora_b": nrm(ks[25], (nB, GATE_LORA, D), GATE_LORA ** -0.5),
        "rwkv_k_k": 0.85 + nrm(ks[26], (nB, D), 0.05),
        "rwkv_k_a": 1.0 + nrm(ks[27], (nB, D), 0.05),
        "rwkv_r_k": nrm(ks[28], (nB, H, N), 0.1),
        "rwkv_ln_g": 1.0 + nrm(ks[29], (nB, D), 0.05),
        "rwkv_ln_b": nrm(ks[30], (nB, D), 0.02),
        "rwkv_w_o": nrm(ks[31], (nB, D, D), 0.5 * D ** -0.5),
    }

def first_block(x, norm_mix_g, norm_ffn_g, final_norm_g, ffn_w1, ffn_w2,
              sgu_w_in, sgu_b_in, sgu_ln_g, sgu_ln_b, sgu_w_s, sgu_b_s, sgu_w_out,
              rwkv_mu, rwkv_w_rkv, rwkv_w0, rwkv_w_lora_a, rwkv_w_lora_b,
              rwkv_a0, rwkv_a_lora_a, rwkv_a_lora_b,
              rwkv_v0, rwkv_v_lora_a, rwkv_v_lora_b,
              rwkv_g_lora_a, rwkv_g_lora_b, rwkv_k_k, rwkv_k_a, rwkv_r_k,
              rwkv_ln_g, rwkv_ln_b, rwkv_w_o):
    v_first = None
    for i in range(DEPTH):
        h = _rmsnorm(x, norm_mix_g[i])
        j = i // N_MIXERS
        if i % N_MIXERS == 0:
            y = _spatial_gating_mixer(h, sgu_w_in[j], sgu_b_in[j], sgu_ln_g[j], sgu_ln_b[j],
                                      sgu_w_s[j], sgu_b_s[j], sgu_w_out[j])
        else:
            v_mix = None if j == 0 else (rwkv_v0[j - 1], rwkv_v_lora_a[j - 1], rwkv_v_lora_b[j - 1])
            y, v_first = _rwkv7_mixer(h, rwkv_mu[j], rwkv_w_rkv[j], rwkv_w0[j],
                                      rwkv_w_lora_a[j], rwkv_w_lora_b[j],
                                      rwkv_a0[j], rwkv_a_lora_a[j], rwkv_a_lora_b[j],
                                      rwkv_g_lora_a[j], rwkv_g_lora_b[j],
                                      rwkv_k_k[j], rwkv_k_a[j], rwkv_r_k[j],
                                      rwkv_ln_g[j], rwkv_ln_b[j], rwkv_w_o[j],
                                      v_first, v_mix)
        x = x + y
        x = x + _squared_relu_mlp(_rmsnorm(x, norm_ffn_g[i]), ffn_w1[i], ffn_w2[i])
    return _rmsnorm(x, final_norm_g)


DEPTH_2 = 1

ATTN_HEADS = 8
HEAD_DIM = 64
ATTN_WIDTH = ATTN_HEADS * HEAD_DIM
Q_BLOCK = 128
POOL_WINDOWS = (2, 4, 8, 16)
POOL_GROUPS = len(POOL_WINDOWS)
POOL_WIDTH = D_MODEL - ATTN_WIDTH
POOL_GROUP_DIM = POOL_WIDTH // POOL_GROUPS
IN_WIDTH = 3 * ATTN_WIDTH + ATTN_HEADS + POOL_WIDTH
N_EXPERT_GROUPS = 4
EXPERTS_PER_GROUP = 8
TOP_K_EXPERT = 2
D_EXPERT = 256
N_MOD = 6
EPS = 1e-6
NEG_INF = -1e30
FGATE_BIAS_INIT = 3.0


def rmsnorm(x, g):
    xf = x.astype(jnp.float32)
    y = xf * lax.rsqrt(jnp.mean(xf * xf, axis=-1, keepdims=True) + EPS)
    return (y * g.astype(jnp.float32)).astype(x.dtype)

def modulate(h, shift, scale):
    return h * (1.0 + scale[:, None, :]) + shift[:, None, :]

def forgetting_attention(q, k, v, log_f):
    B, S, H, dh = q.shape
    nb = S // Q_BLOCK
    qh = q.transpose(0, 2, 1, 3)
    kh = k.transpose(0, 2, 1, 3)
    vh = v.transpose(0, 2, 1, 3)
    F = jnp.cumsum(log_f, axis=1).transpose(0, 2, 1)
    q_blocks = qh.reshape(B, H, nb, Q_BLOCK, dh).transpose(2, 0, 1, 3, 4)
    fq_blocks = F.reshape(B, H, nb, Q_BLOCK).transpose(2, 0, 1, 3)
    starts = jnp.arange(nb, dtype=jnp.int32) * Q_BLOCK
    key_pos = jnp.arange(S, dtype=jnp.int32)
    scale = 1.0 / math.sqrt(dh)

    def one_block(args):
        qb, fqb, start = args
        s = jnp.einsum('bhqd,bhkd->bhqk', qb, kh).astype(jnp.float32) * scale
        s = s + fqb[..., None] - F[:, :, None, :]
        qpos = start + jnp.arange(Q_BLOCK, dtype=jnp.int32)
        causal = key_pos[None, :] <= qpos[:, None]
        s = jnp.where(causal[None, None], s, NEG_INF)
        p = jax.nn.softmax(s, axis=-1).astype(vh.dtype)
        return jnp.einsum('bhqk,bhkd->bhqd', p, vh)

    out = lax.map(one_block, (q_blocks, fq_blocks, starts))
    return out.transpose(1, 0, 3, 2, 4).reshape(B, S, H * dh)

def trailing_mean(cs, w):
    S = cs.shape[1]
    prev = jnp.pad(cs[:, :S - w], ((0, 0), (w, 0), (0, 0)))
    cnt = jnp.minimum(jnp.arange(1, S + 1), w).astype(jnp.float32)
    return (cs - prev) / cnt[None, :, None]

def multiscale_pool(u, w_pool, pool_scale):
    B, S, _ = u.shape
    ug = u.reshape(B, S, POOL_GROUPS, POOL_GROUP_DIM)
    cs = jnp.cumsum(ug.astype(jnp.float32), axis=1)
    pooled = jnp.stack(
        [trailing_mean(cs[:, :, g, :], w) for g, w in enumerate(POOL_WINDOWS)], axis=2)
    diff = (pooled - ug.astype(jnp.float32)).astype(u.dtype)
    mixed = jnp.einsum('bsgc,gcd->bsgd', diff, w_pool)
    return mixed.reshape(B, S, POOL_WIDTH) * pool_scale

def hierarchical_moe(h, w_rg, b_rg, w_re, b_re, w_gate, w_up, w_down):
    lg = jnp.matmul(h, w_rg).astype(jnp.float32) + b_rg
    pg = jax.nn.softmax(lg, axis=-1)
    top_p, top_g = lax.top_k(pg, 1)
    le = jnp.einsum('td,gde->tge', h, w_re).astype(jnp.float32) + b_re
    le_sel = jnp.take_along_axis(le, top_g[:, :, None], axis=1)[:, 0]
    ev, ei = lax.top_k(le_sel, TOP_K_EXPERT)
    ew = jax.nn.softmax(ev, axis=-1)
    e_comb = jnp.sum(jax.nn.one_hot(ei, EXPERTS_PER_GROUP, dtype=jnp.float32) * ew[..., None], axis=1)
    g_comb = jax.nn.one_hot(top_g[:, 0], N_EXPERT_GROUPS, dtype=jnp.float32) * top_p
    comb = (g_comb[:, :, None] * e_comb[:, None, :]).astype(h.dtype)
    y = jnp.zeros_like(h)
    for g in range(N_EXPERT_GROUPS):
        a = jnp.einsum('td,edf->tef', h, w_gate[g])
        b = jnp.einsum('td,edf->tef', h, w_up[g])
        act = jax.nn.silu(a) * b * comb[:, g, :, None]
        y = y + jnp.einsum('tef,efd->td', act, w_down[g])
    return y

def second_inputs(seed: int = 0) -> dict:
    key = jax.random.key(seed)
    ks = jax.random.split(key, 20)
    f32 = jnp.float32
    D, L = D_MODEL, DEPTH_2
    G, E, F = N_EXPERT_GROUPS, EXPERTS_PER_GROUP, D_EXPERT

    def nrm(k, shape, scale):
        return jax.random.normal(k, shape, f32) * scale

    return {
        "x": nrm(ks[0], (BATCH, SEQ, D), 1.0),
        "c": nrm(ks[1], (BATCH, D), 1.0),
        "norm_mix_g": 1.0 + nrm(ks[2], (L, D), 0.02),
        "norm_ffn_g": 1.0 + nrm(ks[3], (L, D), 0.02),
        "norm_final_g": 1.0 + nrm(ks[4], (D,), 0.02),
        "w_ada": nrm(ks[5], (L, D, N_MOD * D), 0.5 * D ** -0.5),
        "b_ada": nrm(ks[6], (L, N_MOD * D), 0.02),
        "w_in": nrm(ks[7], (L, D, IN_WIDTH), D ** -0.5),
        "b_fgate": FGATE_BIAS_INIT + nrm(ks[8], (L, ATTN_HEADS), 0.1),
        "w_pool": nrm(ks[9], (L, POOL_GROUPS, POOL_GROUP_DIM, POOL_GROUP_DIM), POOL_GROUP_DIM ** -0.5),
        "pool_scale": 1.0 + nrm(ks[10], (L, POOL_WIDTH), 0.1),
        "w_out": nrm(ks[11], (L, D, D), D ** -0.5),
        "w_router_group": nrm(ks[12], (L, D, G), D ** -0.5),
        "b_router_group": nrm(ks[13], (L, G), 0.01),
        "w_router_expert": nrm(ks[14], (L, G, D, E), D ** -0.5),
        "b_router_expert": nrm(ks[15], (L, G, E), 0.01),
        "w_expert_gate": nrm(ks[16], (L, G, E, D, F), D ** -0.5),
        "w_expert_up": nrm(ks[17], (L, G, E, D, F), D ** -0.5),
        "w_expert_down": nrm(ks[18], (L, G, E, F, D), F ** -0.5),
    }

def second_block(x, c, norm_mix_g, norm_ffn_g, norm_final_g, w_ada, b_ada, w_in, b_fgate,
              w_pool, pool_scale, w_out, w_router_group, b_router_group, w_router_expert,
              b_router_expert, w_expert_gate, w_expert_up, w_expert_down):
    B, S, D = x.shape
    split_pts = [ATTN_WIDTH, 2 * ATTN_WIDTH, 3 * ATTN_WIDTH, 3 * ATTN_WIDTH + ATTN_HEADS]
    c_act = jax.nn.silu(c)
    for l in range(DEPTH_2):
        mod = jnp.matmul(c_act, w_ada[l]) + b_ada[l]
        sh_m, sc_m, gt_m, sh_f, sc_f, gt_f = jnp.split(mod, N_MOD, axis=-1)

        h = modulate(rmsnorm(x, norm_mix_g[l]), sh_m, sc_m)
        proj = jnp.matmul(h, w_in[l])
        q, k, v, f_logit, u = jnp.split(proj, split_pts, axis=-1)
        q = q.reshape(B, S, ATTN_HEADS, HEAD_DIM)
        k = k.reshape(B, S, ATTN_HEADS, HEAD_DIM)
        v = v.reshape(B, S, ATTN_HEADS, HEAD_DIM)
        log_f = jax.nn.log_sigmoid(f_logit.astype(jnp.float32) + b_fgate[l].astype(jnp.float32))
        attn_out = forgetting_attention(q, k, v, log_f)
        pool_out = multiscale_pool(u, w_pool[l], pool_scale[l])
        mix = jnp.matmul(jnp.concatenate([attn_out, pool_out.astype(attn_out.dtype)], axis=-1), w_out[l])
        x = x + gt_m[:, None, :] * mix

        h = modulate(rmsnorm(x, norm_ffn_g[l]), sh_f, sc_f)
        ffn = hierarchical_moe(h.reshape(B * S, D), w_router_group[l], b_router_group[l],
                               w_router_expert[l], b_router_expert[l], w_expert_gate[l],
                               w_expert_up[l], w_expert_down[l])
        x = x + gt_f[:, None, :] * ffn.reshape(B, S, D)
    return rmsnorm(x, norm_final_g)


def setup_inputs(seed=0):
    out = dict(first_inputs(seed))
    for name, value in second_inputs(seed + 1).items():
        if name != "x":
            out[name + "_2"] = value
    return out


def reference(
    x, norm_mix_g, norm_ffn_g, final_norm_g, ffn_w1, ffn_w2, sgu_w_in, sgu_b_in, sgu_ln_g,
    sgu_ln_b, sgu_w_s, sgu_b_s, sgu_w_out, rwkv_mu, rwkv_w_rkv, rwkv_w0, rwkv_w_lora_a,
    rwkv_w_lora_b, rwkv_a0, rwkv_a_lora_a, rwkv_a_lora_b, rwkv_v0, rwkv_v_lora_a, rwkv_v_lora_b,
    rwkv_g_lora_a, rwkv_g_lora_b, rwkv_k_k, rwkv_k_a, rwkv_r_k, rwkv_ln_g, rwkv_ln_b, rwkv_w_o,
    c_2, norm_mix_g_2, norm_ffn_g_2, norm_final_g_2, w_ada_2, b_ada_2, w_in_2, b_fgate_2,
    w_pool_2, pool_scale_2, w_out_2, w_router_group_2, b_router_group_2, w_router_expert_2,
    b_router_expert_2, w_expert_gate_2, w_expert_up_2, w_expert_down_2,
):
    x = first_block(
        x, norm_mix_g, norm_ffn_g, final_norm_g, ffn_w1, ffn_w2, sgu_w_in, sgu_b_in, sgu_ln_g,
        sgu_ln_b, sgu_w_s, sgu_b_s, sgu_w_out, rwkv_mu, rwkv_w_rkv, rwkv_w0, rwkv_w_lora_a,
        rwkv_w_lora_b, rwkv_a0, rwkv_a_lora_a, rwkv_a_lora_b, rwkv_v0, rwkv_v_lora_a,
        rwkv_v_lora_b, rwkv_g_lora_a, rwkv_g_lora_b, rwkv_k_k, rwkv_k_a, rwkv_r_k, rwkv_ln_g,
        rwkv_ln_b, rwkv_w_o,
    )
    return second_block(
        x, c_2, norm_mix_g_2, norm_ffn_g_2, norm_final_g_2, w_ada_2, b_ada_2, w_in_2, b_fgate_2,
        w_pool_2, pool_scale_2, w_out_2, w_router_group_2, b_router_group_2, w_router_expert_2,
        b_router_expert_2, w_expert_gate_2, w_expert_up_2, w_expert_down_2,
    )


_drawn_inputs = setup_inputs


def setup_inputs(seed=0):
    import zlib

    import numpy as np

    out = dict(_drawn_inputs(seed))
    spreads = {}
    factors = {'sgu_b_in': 4.034,
     'sgu_ln_g': 3.485,
     'sgu_ln_b': 6.029,
     'rwkv_w_lora_a': 8.0,
     'rwkv_w_lora_b': 8.0,
     'rwkv_a0': 3.892,
     'rwkv_k_k': 4.035,
     'rwkv_k_a': 3.482,
     'rwkv_ln_g': 4.721,
     'rwkv_ln_b': 7.67,
     'norm_mix_g_2': 8.0,
     'norm_ffn_g_2': 4.723,
     'norm_final_g_2': 8.534,
     'b_fgate_2': 37.508,
     'pool_scale_2': 2.828,
     'b_router_group_2': 8.0,
     'b_router_expert_2': 8.0}
    for name, (base, spread) in spreads.items():
        noise = np.random.default_rng([zlib.crc32(name.encode()), seed]).standard_normal(out[name].shape)
        drawn = base * np.exp(spread * noise) if base else spread * noise
        out[name] = __import__('jax').numpy.asarray(drawn.astype(out[name].dtype))
    for name, factor in factors.items():
        out[name] = (out[name] * factor).astype(out[name].dtype)
    return out
```

```python
from contextlib import ExitStack

import numpy as np
import concourse.bass as bass
from concourse import mybir

F32 = mybir.dt.float32
F32R = mybir.dt.float32r
ALU = mybir.AluOpType
ACT = mybir.ActivationFunctionType
AX = mybir.AxisListType

P = 128
SEQ, D = 256, 1024
TT = SEQ // P
KT = D // P
SGU = 2 * D
SG = SGU // P
FFN = 4 * D
HEADS, HD = 16, 64
CH = 64
NCH = SEQ // CH
AH = 8
AW = AH * HD
PG = 4
WINDOWS = (2, 4, 8, 16)
NORMS = [0, 1, 2, 3, "f", 4, 5, "g"]
NG, NE = 4, 8
EXPERTS = NG * NE
DE = 256
NMOD = 6
EPS, LN_EPS, GN_EPS = 1e-6, 1e-5, 64e-5
KAPPA = float(np.exp(-0.5))
NEG = -1e30
RING = 4
AHEAD = 3
SLOT = 2048

STAGES = [("sgu_v", 8), ("sgu_u", 8), ("sgu_out", 8), ("ffn0", 32), ("rwkv_k", 4), ("rwkv_r", 4),
          ("rwkv_v", 4), ("rwkv_o", 4), ("ffn1", 32), ("in2", 8), ("out2", 4), ("moe", 96)]
FIRST, PIECES = {}, 0
for _name, _count in STAGES:
    FIRST[_name] = PIECES
    PIECES += _count

COLS = [("norm_mix0", 8), ("norm_mix1", 8), ("norm_ffn0", 8), ("norm_ffn1", 8), ("b_in_u", 16),
        ("sgu_ln_g", 16), ("sgu_ln_b", 16), ("mu", 48), ("w0", 8), ("a0", 8), ("k_k", 8),
        ("k_a", 8), ("r_k", 8), ("norm_mix2", 8), ("norm_ffn2", 8), ("pool_scale", 4), ("c", 8), ("b_ada", 48)]
COL, NCOL = {}, 0
for _name, _count in COLS:
    COL[_name] = NCOL
    NCOL += _count

CONSTS = [("ident", 128), ("ones", 128), ("strict_lower", 64), ("strict_upper", 64),
          ("incl_upper", 64), ("level1_lower", 64), ("level_upper", 6 * 64), ("ident64", 64),
          ("not_chunk_start", 256), ("head2", 2), ("head16", 30), ("descending", 8)]
CST, NCST = {}, 0
for _name, _count in CONSTS:
    CST[_name] = NCST
    NCST += _count
CST_WIDTH = dict(CONSTS)


def shape_constants():
    c = np.zeros((P, NCST), np.float32)

    def put(name, value):
        c[:, CST[name]:CST[name] + value.shape[1]] = value

    put("ident", np.eye(P))
    put("ones", np.ones((P, P)))
    t = np.arange(P)[:, None] % CH
    s = np.arange(CH)[None, :]
    put("strict_lower", (t > s) * 1.0)
    put("strict_upper", (t < s) * 1.0)
    put("incl_upper", (t <= s) * 1.0)
    put("ident64", (t == s) * 1.0)
    put("level1_lower", ((t // 2 == s // 2) & (t > s)) * 1.0)
    levels = []
    for n in range(6):
        m = 2 ** n
        levels.append(((t // (2 * m) == s // (2 * m)) & (t // m % 2 == 0) & (s // m % 2 == 1)) * 1.0)
    put("level_upper", np.concatenate(levels, 1))
    put("not_chunk_start", np.broadcast_to((np.arange(SEQ) % CH != 0) * 1.0, (P, SEQ)))
    half = np.arange(P)[:, None] // HD
    put("head2", (np.arange(2)[None, :] == half) * 1.0)
    put("descending", np.broadcast_to(np.arange(8, 0, -1.0), (P, 8)))
    put("head16", (np.arange(30)[None, :] == 14 + half) * 1.0)
    return c


def head_rows():
    return (np.arange(HEADS)[:, None] == np.arange(D)[None, :] // HD).astype(np.float32)


def pool_matrices():
    out = np.zeros((PG, SEQ, SEQ), np.float32)
    for g, w in enumerate(WINDOWS):
        for t in range(SEQ):
            lo = max(0, t - w + 1)
            out[g, lo:t + 1, t] = 1.0 / min(t + 1, w)
            out[g, t, t] -= 1.0
    return np.ascontiguousarray(out.reshape(PG, TT, P, SEQ).transpose(2, 1, 0, 3))


def attention_constants():
    t, s = np.arange(P)[:, None], np.arange(P)[None, :]
    diag = np.where(s <= t, 0.0, NEG)
    mask = np.concatenate([diag, np.zeros((P, P)), diag], 1)
    cum = (np.arange(SEQ)[:, None] <= np.arange(SEQ)[None, :]) * 1.0
    cum = cum.reshape(TT, P, SEQ).transpose(1, 0, 2).reshape(P, TT * SEQ)
    rows = np.zeros((P, 2 + AH))
    rows[AH:2 * AH, 0] = 1.0
    rows[0:AH, 1] = 1.0
    for h in range(AH):
        rows[h, 2 + h] = rows[AH + h, 2 + h] = 1.0
    return np.concatenate([mask, cum, rows], 1).astype(np.float32)


ATTC = 3 * P + TT * SEQ + 2 + AH


DIRECT = ["x", "ffn_w1", "ffn_w2", "sgu_w_in", "sgu_b_in", "sgu_b_s", "sgu_w_out", "rwkv_w_rkv",
          "rwkv_w_o", "w_ada_2", "w_in_2", "w_out_2", "w_expert_gate_2", "w_expert_up_2",
          "w_expert_down_2", "rwkv_w_lora_a", "rwkv_w_lora_b", "rwkv_a_lora_a", "rwkv_a_lora_b",
          "rwkv_g_lora_a", "rwkv_g_lora_b", "rwkv_ln_g", "rwkv_ln_b", "final_norm_g", "norm_final_g_2",
          "b_ada_2"]


def build(nc, a, out):
    with ExitStack() as ctx:
        sems = {}

        def sem(name):
            if name not in sems:
                sems[name] = ctx.enter_context(nc.semaphore(name))
            return sems[name]

        where = [(nc.sbuf_base + 31) // 32 * 32]

        def sb(name, cols, dt=F32, at=None):
            offset = where[0] if at is None else at
            t = nc.alloc_sbuf_tensor_at(name, [P, cols], dt, offset=offset)
            if at is None:
                where[0] = offset + (4 * cols + 31) // 32 * 32
            return t

        raw = [sb(f"raw{i}", SLOT) for i in range(RING)]
        whi = [sb(f"whi{i}", SLOT, F32R) for i in range(RING)]
        wlo = [sb(f"wlo{i}", SLOT, F32R) for i in range(RING)]
        X = sb("X", TT * D)
        arena_at = where[0]
        arena = sb("arena", 11 * SLOT + SLOT // 2)
        cst = sb("cst", NCST)
        col = sb("col", NCOL)
        small = sb("small", 640)
        zeros_bf = nc.alloc_sbuf_tensor_at("zeros_bf", [P, P], mybir.dt.bfloat16, offset=where[0])
        where[0] += 2 * P
        zeros, zero_cols = zeros_bf[:, :], zeros_bf[:, 0:1].to_broadcast([P, 512])
        assert where[0] <= nc.sbuf_usable_end, where[0]

        Xv = X[:, :].rearrange("p (t d) -> p t d", t=TT)

        def slot(i, n=1):
            return arena[:, i * SLOT:(i + n) * SLOT]

        def slot_r(name, i, cols, skip=0):
            return sb(name, cols, F32R, at=arena_at + 4 * (i * SLOT + skip))

        def tiles(ap, k=KT):
            return ap.rearrange("p (k t) -> p k t", k=k)

        def cc(name, lo=0, n=None):
            n = CST_WIDTH[name] if n is None else n
            return cst[:, CST[name] + lo:CST[name] + lo + n]

        def colv(name, j):
            return col[:, COL[name] + j:COL[name] + j + 1]

        ident = cc("ident")
        ss = small[:, 0:2]
        rec = small[:, 2:4]
        rstd = small[:, 4:6]
        bns = small[:, 8:8 + 48]
        bna = small[:, 56:60]
        wend = small[:, 64:96]
        bonus = small[:, 96:128]
        gst = small[:, 128:224]
        scr = small[:, 224:384]
        gsig = small[:, 384:640]

        Hh = slot_r("Hh", 2, SLOT)
        Hl = slot_r("Hl", 3, SLOT)
        HhT, HlT = tiles(Hh[:, :]), tiles(Hl[:, :])
        Ah = slot_r("Ah", 0, 1024)
        Al = slot_r("Al", 0, 1024, 1024)
        Ch = slot_r("Ch", 5, SLOT)
        Cl = slot_r("Cl", 6, SLOT)
        ChT, ClT = tiles(Ch[:, :]), tiles(Cl[:, :])
        Fh = slot_r("Fh", 0, 1024)
        Fl = slot_r("Fl", 0, 1024, 1024)

        r_h, r_xx, r_xs = tiles(slot(0)), tiles(slot(1)), tiles(slot(4))
        r_xsa, r_xsg = tiles(slot(9)), tiles(slot(10))
        r_la = slot(8).rearrange("p (k n) -> p k n", k=KT)
        r_lb = arena[:, 11 * SLOT:11 * SLOT + D]
        r_mid = slot(3)[:, 0:SEQ]
        r_sg, r_cum, r_a = tiles(slot(5)), tiles(slot(6)), tiles(slot(7))
        r_k, r_kk, r_r = tiles(slot(9)), tiles(slot(10)), tiles(slot(7))
        r_tmp, r_prod = tiles(slot(4)), tiles(slot(1))
        r_headrows = slot(8)[0:HEADS, 0:D]
        r_norm = arena[0:HEADS, 11 * SLOT:11 * SLOT + SEQ]
        r_v = tiles(slot(0), TT)
        r_at, r_rt, r_kt, r_bt = tiles(slot(5)), tiles(slot(7)), tiles(slot(9)), tiles(slot(10))

        def heads(i):
            return slot(i).rearrange("p (t h s) -> p t h s", t=TT, h=HEADS)

        r_M, r_Y, r_Aak, r_Arb, r_Ark, r_X = heads(1), heads(2), heads(3), heads(4), heads(6), heads(9)
        r_btm, r_ktm = heads(8), heads(10)
        r_Q = arena[:, 11 * SLOT:11 * SLOT + D].rearrange("p (b h s) -> p b h s", b=2, h=8)
        r_U = heads(9)
        r_RS = slot(1).rearrange("p (w h s) -> p w h s", w=2, h=HEADS)
        r_Z = arena[:, 11 * SLOT:11 * SLOT + D].rearrange("p (b j v) -> p b j v", b=2, j=KT)
        r_y, r_y2 = heads(3), heads(2)
        r_lnrow = slot(4).rearrange("p (w d) -> p w d", w=2)
        r_gb = slot(8)[:, 0:D]
        MATRICES = [("M", r_at, r_bt, "strict_lower"), ("N", r_bt, r_at, "strict_upper"),
                    ("Arb", r_bt, r_rt, "incl_upper"), ("Aak", r_kt, r_at, "strict_upper"),
                    ("Ark", r_kt, r_rt, "incl_upper")]
        MATRIX_OUT = {"M": r_M, "N": r_Y, "Arb": r_Arb, "Aak": r_Aak, "Ark": r_Ark}

        NR = NG + EXPERTS
        W_SMALL = KT * AH + KT * NR + PG * P
        B_SMALL = AH + NR
        s_w = slot(1)[:, 0:W_SMALL]
        s_b = slot(1)[:, W_SMALL:W_SMALL + B_SMALL]
        s_c = slot(1)[:, W_SMALL + B_SMALL:W_SMALL + B_SMALL + ATTC]
        w_f = s_w[:, 0:KT * AH].rearrange("p (k n) -> p k n", k=KT)
        w_r = s_w[:, KT * AH:KT * (AH + NR)].rearrange("p (k n) -> p k n", k=KT)
        w_pool = s_w[:, KT * (AH + NR):].rearrange("p (g n) -> p g n", g=PG)
        causal = s_c[:, 0:3 * P]
        cum = s_c[:, 3 * P:3 * P + TT * SEQ].rearrange("p (t n) -> p t n", t=TT)
        f_cols = s_c[:, 3 * P + TT * SEQ:]
        cact = scr[:, 8:16]
        modcol = scr[:, 16:64]
        gain2 = scr[:, 64:80]
        macc = slot(5, 3)
        gates = slot(10).rearrange("p (m d) -> p m d", m=2)
        finrow = slot(7)[:, 0:D]
        qT, kT = tiles(slot(5)[:, 0:1024], 4), tiles(slot(5)[:, 1024:2048], 4)
        vtm, utm = tiles(slot(6)[:, 0:1024], TT), tiles(slot(6)[:, 1024:2048], TT)
        poolm = slot(7).rearrange("p (t g n) -> p t g n", t=TT, g=PG)
        lf2 = arena[:, 11 * SLOT:11 * SLOT + 64].rearrange("p (t n) -> p t n", t=TT)
        f_tmp = arena[:, 11 * SLOT + 64:11 * SLOT + 128]
        f_a = arena[0:2 * AH, 11 * SLOT + 128:11 * SLOT + 384]
        f_b = arena[0:2 * AH, 11 * SLOT + 384:11 * SLOT + 640]
        f_bh = tiles(slot(4), AH)[0:2 * AH]
        prob = slot(2)[:, 0:6 * P].rearrange("p (b n) -> p b n", b=2)
        probT = slot(3)[:, 0:6 * P].rearrange("p (b n) -> p b n", b=2)
        pdiff = slot(2)[:, 1024:1536].rearrange("p (b n) -> p b n", b=2)
        pmix = slot(3)[:, 1024:1536].rearrange("p (b n) -> p b n", b=2)
        att_stat = gst[:, 0:8].rearrange("p (b n) -> p b n", b=2)
        C2h, C2l = slot_r("C2h", 8, SLOT), slot_r("C2l", 9, SLOT)
        C2hT, C2lT = tiles(C2h[:, :]), tiles(C2l[:, :])
        Eh, El = slot_r("Eh", 0, 512), slot_r("El", 0, 512, 512)
        e_silu, e_tmp = slot(9)[:, 0:512], slot(9)[:, 512:1024]
        combB = slot(5, 4).rearrange("p (e t) -> p e t", e=EXPERTS)
        combT = slot(4)[0:EXPERTS, 0:SEQ]
        ro = arena[:, 11 * SLOT:11 * SLOT + D]

        ps = ctx.enter_context(nc.psum_tensor("ps", [P, 8, 512], F32))

        x_ready = sem("x_ready")

        def nth(m):
            return NORMS.index(m) + 1

        def splits_before(m):
            return 4 * (m - (1 if m > 2 else 0))

        raw_in = [sem(f"raw_in{i}") for i in range(RING)]
        hi_done, lo_done, used = sem("hi_done"), sem("lo_done"), sem("pieces_done")

        def piece(ring, n, k):
            return ring[n % RING][:, :].rearrange("p (k n) -> p k n", k=k)

        block = ctx.enter_context(nc.Block())

        def krows(w):
            return w.rearrange("(k p) n -> p k n", p=P)

        ffn_w1 = [krows(a["ffn_w1"][i]) for i in range(2)]
        ffn_w2 = [krows(a["ffn_w2"][i]) for i in range(2)]
        w_down = a["w_expert_down_2"][0].rearrange("g e (k p) n -> p (g e k) n", p=P)
        w_gate = a["w_expert_gate_2"][0].rearrange("g e (k p) n -> p (g e k) n", p=P)
        w_up = a["w_expert_up_2"][0].rearrange("g e (k p) n -> p (g e k) n", p=P)

        @block.sync
        def _(sp):
            def load(n, src, i=None, k=KT, per=0):
                if i is not None:
                    sp.wait_ge(lo_done, i * per + (n - RING + 1))
                elif n >= RING:
                    sp.wait_ge(lo_done, n - RING + 1)
                sp.dma_start(piece(raw, n, k), src).then_inc(raw_in[n % RING], 16)

            sp.dma_start(Xv, a["x"][0].rearrange("(t p) d -> p t d", p=P)).then_inc(sem("x_in"), 16)
            sp.dma_start(cst[:, :], a["consts"]).then_inc(sem("cst_in"), 16)
            sp.dma_start(col[:, :], a["cols"]).then_inc(sem("col_in"), 16)
            w = krows(a["sgu_w_in"][0])
            for c in range(8):
                load(FIRST["sgu_v"] + c, w[:, :, SGU + 256 * c:SGU + 256 * (c + 1)])
            for c in range(8):
                load(FIRST["sgu_u"] + c, w[:, :, 256 * c:256 * (c + 1)])
            w = krows(a["sgu_w_out"][0])
            for c in range(8):
                load(FIRST["sgu_out"] + c, w[:, 2 * c:2 * c + 2, :], k=2)

            def ffn_loads(layer, n):
                with sp.Fori(0, FFN // 512) as i:
                    for j in range(2):
                        load(n + j, ffn_w1[layer][:, :, bass.ds(i * 512 + 256 * j, 256)], i, per=4)
                    for j in range(2):
                        load(n + 2 + j, ffn_w2[layer][:, bass.ds(i * 4 + 2 * j, 2), :], i, k=2, per=4)
                    if layer == 1:
                        for j in range(3):
                            sp.wait_ge(sem("ada_used"), i * 3 + (j + 1))
                            sp.dma_start(tiles(slot(8 + j)),
                                         krows(a["w_ada_2"][0])[:, :, bass.ds(i * 768 + 256 * j, 256)]
                                         ).then_inc(sem(f"ada_in{j}"), 16)

            ffn_loads(0, FIRST["ffn0"])
            for name, which in (("rwkv_k", 1), ("rwkv_r", 0), ("rwkv_v", 2)):
                w = krows(a["rwkv_w_rkv"][0, which])
                for c in range(4):
                    load(FIRST[name] + c, w[:, :, 256 * c:256 * (c + 1)])
            w = krows(a["rwkv_w_o"][0])
            for c in range(4):
                load(FIRST["rwkv_o"] + c, w[:, 2 * c:2 * c + 2, :], k=2)
            ffn_loads(1, FIRST["ffn1"])
            w = krows(a["w_in_2"][0])
            for c in range(8):
                at = 256 * c if c < 6 else 256 * c + AH
                load(FIRST["in2"] + c, w[:, :, at:at + 256])
            w = krows(a["w_out_2"][0])
            for c in range(4):
                load(FIRST["out2"] + c, w[:, 2 * c:2 * c + 2, :], k=2)
            with sp.Fori(0, EXPERTS // 4) as i:
                for e in range(4):
                    n = FIRST["moe"] + 3 * e
                    load(n, w_gate[:, bass.ds(i * 32 + 8 * e, 8), :], i, per=12)
                    load(n + 1, w_up[:, bass.ds(i * 32 + 8 * e, 8), :], i, per=12)
                    load(n + 2, w_down[:, bass.ds(i * 8 + 2 * e, 2), :], i, k=2, per=12)
            sp.wait_ge(sem("out_ready"), 1)
            sp.dma_start(out[0].rearrange("(t p) d -> p t d", p=P), Xv).then_inc(sem("out_done"), 16)
            sp.wait_ge(sem("out_done"), 16)

        @block.gpsimd
        def _(pool):
            def lo(n, i=None):
                pool.wait_ge(hi_done, n + 1 if i is None else i * RING + (n + 1))
                pool.tensor_tensor(wlo[n % RING][:, :], raw[n % RING][:, :],
                                   whi[n % RING][:, :].bitcast(F32), ALU.subtract).then_inc(lo_done, 1)
            with pool.Fori(0, PIECES // RING) as i:
                for n in range(RING):
                    lo(n, i)

        @block.scalar
        def _(act):
            def hi(n, i=0, per=0):
                if isinstance(i, int):
                    n += per * i
                    if n >= PIECES:
                        return
                    act.wait_ge(raw_in[n % RING], 16 * (n // RING + 1))
                    if n >= RING:
                        act.wait_ge(used, n - RING + 1)
                else:
                    act.wait_ge(raw_in[n % RING], i * (16 * per // RING) + 16 * (n // RING + 1))
                    act.wait_ge(used, i * per + (n - RING + 1))
                act.activation(whi[n % RING][:, :], raw[n % RING][:, :], ACT.Copy).then_inc(hi_done, 1)

            def norm(m, x_ready, x_count):
                act.wait_ge(x_ready, x_count)
                for t in range(TT):
                    ins = act.activation(tiles(slot(4), 2)[:, t, :], Xv[:, t, :], ACT.Square,
                                         accum_out=ss[:, t:t + 1])
                ins.then_inc(sem("norm_ss"), 1)
                act.wait_ge(sem("norm_rec"), nth(m))
                act.activation(rstd, rec, ACT.Sqrt).then_inc(sem("norm_rstd"), 1)

            for n in range(AHEAD):
                hi(n)
            act.dma_start(slot(7), a["sgu_b_in"][:, SGU:2 * SGU].to_broadcast([P, SGU])
                          ).then_inc(sem("bin_in"), 16)
            act.dma_start(slot(10), a["sgu_w_sT"]).then_inc(sem("ws_in"), 16)
            act.dma_start(slot(1), a["sgu_b_s"].rearrange("n g i -> n (g i)").to_broadcast([P, SGU])
                          ).then_inc(sem("bs_in"), 16)
            norm(0, sem("x_in"), 16)
            v = slot(5, 2).rearrange("p (t d) -> p t d", t=TT)
            uT = tiles(slot(8, 2), SG)
            for c in range(8):
                act.wait_ge(sem("v_biased"), c + 1)
                act.activation(v[:, :, 256 * c:256 * (c + 1)], v[:, :, 256 * c:256 * (c + 1)],
                               ACT.Gelu).then_inc(sem("v_gelu"), 1)
                hi(FIRST["sgu_v"] + c + AHEAD)
            act.wait_ge(sem("col_in"), 16)
            for c in range(8):
                act.wait_ge(used, FIRST["sgu_u"] + c + 1)
                for f in range(2):
                    ins = act.activation(uT[:, 2 * c + f, :], ps[:, 4 + c % 4, 256 * f:256 * (f + 1)],
                                         ACT.Gelu, bias=colv("b_in_u", 2 * c + f))
                ins.then_inc(sem("u_gelu"), 1)
                hi(FIRST["sgu_u"] + c + AHEAD)
            act.wait_ge(sem("v_rec"), 1)
            act.activation(rstd, rec, ACT.Sqrt).then_inc(sem("v_rstd"), 1)
            for c in range(8):
                hi(FIRST["sgu_out"] + c + AHEAD)

            def ffn(layer, n):
                m = 1 if layer == 0 else 3
                norm(m, x_ready, m)
                if layer == 1:
                    act.activation(cact, col[:, COL["c"]:COL["c"] + KT], ACT.Sigmoid).then_inc(sem("c_sigmoid"), 1)
                if layer == 0:
                    for at, w, name in ((0, 64, "w"), (64, 64, "a"), (128, 128, "g")):
                        act.dma_start(r_la[:, :, at:at + w], krows(a[f"rwkv_{name}_lora_a"][0])
                                      ).then_inc(sem("lora_in"), 16)
                    act.dma_start(r_lb[0:64, :], a["rwkv_w_lora_b"][0]).then_inc(sem("lora_in"), 16)
                    act.dma_start(r_lb[64:128, :], a["rwkv_a_lora_b"][0]).then_inc(sem("lora_in"), 16)

                def step(i):
                    for j in range(4):
                        if j < 2:
                            act.wait_ge(used, i * 4 + (n + j + 1))
                            act.activation(slot(4)[:, 512 * j:512 * (j + 1)], ps[:, 4 + j, :],
                                           ACT.Relu).then_inc(sem("ffn_relu"), 1)
                        hi(n + j + AHEAD, i, per=4)
                with act.Fori(0, FFN // 512 - 1) as i:
                    step(i)
                step(FFN // 512 - 1)

            def rwkv():
                norm(2, x_ready, 2)
                act.wait_ge(sem("lora_mm"), 1)
                act.activation(r_mid[0:64, :], ps[0:64, 0, 0:SEQ], ACT.Tanh).then_inc(sem("lora_mid"), 1)
                act.wait_ge(sem("lora_mm"), 2)
                act.activation(r_mid[64:128, :], ps[64:128, 1, 0:SEQ], ACT.Copy).then_inc(sem("lora_mid"), 1)
                act.wait_ge(sem("lora_mm"), 3)
                act.activation(gsig, ps[:, 2, 0:SEQ], ACT.Sigmoid).then_inc(sem("g_sigmoid"), 1)
                act.dma_start(r_headrows, a["head_rows"]).then_inc(sem("headrows_in"), 16)
                for what, dst, bias in (("w", r_sg, "w0"), ("a", r_a, "a0")):
                    for q in range(4):
                        act.wait_ge(sem("lora2_mm"), (4 if what == "a" else 0) + q + 1)
                        for j in (2 * q, 2 * q + 1):
                            ins = act.activation(dst[:, j, :], ps[:, 4 + q, 256 * (j % 2):256 * (j % 2 + 1)],
                                                 ACT.Sigmoid, bias=colv(bias, j))
                        ins.then_inc(sem("lora_sigmoid"), 1)

                def copies(name, dst):
                    for c in range(4):
                        act.wait_ge(used, FIRST[name] + c + 1)
                        if name == "rwkv_v":
                            o = dst[:, :, 256 * c:256 * (c + 1)]
                            src = ps[:, 4 + c, :].rearrange("p (t n) -> p t n", t=TT)
                        else:
                            o = dst[:, 2 * c:2 * c + 2, :]
                            src = ps[:, 4 + c, :].rearrange("p (f n) -> p f n", f=2)
                        act.activation(o, src, ACT.Copy).then_inc(sem("rwkv_copied"), 1)
                        hi(FIRST[name] + c + AHEAD)

                copies("rwkv_k", r_k)
                act.wait_ge(sem("kk_sum_mm"), 1)
                act.activation(r_norm, ps[0:HEADS, 3, 0:SEQ], ACT.Sqrt).then_inc(sem("kk_norm"), 1)
                act.wait_ge(sem("cum_excl"), 1)
                act.activation(slot(5), slot(5), ACT.Exp, scale=-KAPPA).then_inc(sem("W_excl"), 1)
                act.wait_ge(sem("k_new"), 1)
                copies("rwkv_r", r_r)
                copies("rwkv_v", r_v)
                act.wait_ge(sem("tmp_free"), 1)
                act.activation(slot(4), slot(6), ACT.Exp, scale=KAPPA).then_inc(sem("W_inv"), 1)
                act.wait_ge(sem("W_inv"), 1)
                act.activation(slot(6), slot(6), ACT.Exp, scale=-KAPPA).then_inc(sem("W"), 1)
                for m, dst in enumerate((r_btm, r_ktm)):
                    for q in range(4):
                        act.wait_ge(sem("token_major_mm"), 4 * m + q + 1)
                        act.activation(dst[:, q // 2, 8 * (q % 2):8 * (q % 2 + 1), :].rearrange("p h s -> p (h s)"),
                                       ps[:, 4 + q, :], ACT.Copy).then_inc(sem("rwkv_copied"), 1)
                for c in range(1, NCH):
                    rows = slice(CH * (c % 2), CH * (c % 2 + 1))
                    for g in range(2):
                        act.wait_ge(sem("ystate_mm"), 2 * (c - 1) + g + 1)
                        act.activation(r_y[rows, c // 2, g::2, :], ps[rows, g, :].rearrange("p (j s) -> p j s", j=KT),
                                       ACT.Copy).then_inc(sem("y_state"), 1)
                act.wait_ge(sem("y_mm"), 2 * NCH)
                act.dma_start(r_lnrow[:, 0, :], a["rwkv_ln_g"].to_broadcast([P, D])).then_inc(sem("ln_in"), 16)
                act.dma_start(r_lnrow[:, 1, :], a["rwkv_ln_b"].to_broadcast([P, D])).then_inc(sem("ln_in"), 16)
                act.dma_start(r_gb, a["rwkv_g_lora_b"][0]).then_inc(sem("gb_in"), 16)
                act.wait_ge(sem("gn_rec"), 1)
                act.activation(gst[:, 32:64], gst[:, 32:64], ACT.Sqrt).then_inc(sem("gn_rstd"), 1)
                for c in range(4):
                    hi(FIRST["rwkv_o"] + c + AHEAD)

            ffn(0, FIRST["ffn0"])
            def gates_and_mixer():
                act.wait_ge(sem("ada_used"), 27)
                act.dma_start(gates[:, 0, :], a["b_ada_2"][:, 2 * D:3 * D].to_broadcast([P, D])
                              ).then_inc(sem("gate_in"), 16)
                act.dma_start(gates[:, 1, :], a["b_ada_2"][:, 5 * D:6 * D].to_broadcast([P, D])
                              ).then_inc(sem("gate_in"), 16)
                act.dma_start(s_w, a["w_small"]).then_inc(sem("small_in"), 16)
                act.dma_start(s_b, a["b_small"].to_broadcast([P, B_SMALL])).then_inc(sem("small_in"), 16)
                act.dma_start(s_c, a["attention_consts"]).then_inc(sem("small_in"), 16)
                act.wait_ge(sem("gate_mm"), 9)
                act.dma_start(finrow, a["final_norm_g"].unsqueeze(0).to_broadcast([P, D])
                              ).then_inc(sem("fin_in"), 16)
                norm("f", x_ready, 4)
                act.wait_ge(x_ready, 5)
                act.dma_start(slot(7), a["pool_matrices"]).then_inc(sem("pool_in"), 16)
                norm(4, x_ready, 5)
                for c in range(8):
                    act.wait_ge(used, FIRST["in2"] + c + 1)
                    src = ps[:, 4 + c % 4, :].rearrange("p (f n) -> p f n", f=2)
                    if c < 4:
                        o = (qT if c < 2 else kT)[:, 2 * (c % 2):2 * (c % 2) + 2, :]
                    else:
                        o = (vtm if c < 6 else utm)[:, :, 256 * (c % 2):256 * (c % 2 + 1)]
                    act.activation(o, src, ACT.Copy, scale=HD ** -0.5 if c < 2 else 1.0
                                   ).then_inc(sem("in2_copied"), 1)
                    hi(FIRST["in2"] + c + AHEAD)
                    if c == 3:
                        fl = f_tmp[:, 16:32].rearrange("p (t n) -> p t n", t=TT)
                        act.wait_ge(sem("f_negabs"), 1)
                        act.activation(fl, fl, ACT.Exp).then_inc(sem("f_exp"), 1)
                        act.wait_ge(sem("f_exp"), 1)
                        act.activation(fl, fl, ACT.Ln, bias=1.0).then_inc(sem("f_ln"), 1)
                for h in range(AH):
                    st = att_stat[:, h % 2, :]
                    act.wait_ge(sem("att_max"), h + 1)
                    p_ = prob[:, h % 2, :]
                    act.activation(p_[:, 0:P], p_[:, 0:P], ACT.Exp, bias=st[:, 0:1], accum_out=st[:, 2:3])
                    act.activation(p_[:, P:3 * P], p_[:, P:3 * P], ACT.Exp, bias=st[:, 1:2],
                                   accum_out=st[:, 3:4]).then_inc(sem("att_exp"), 1)
                for c in range(4):
                    hi(FIRST["out2"] + c + AHEAD)

            def moe():
                norm(5, x_ready, 6)
                act.wait_ge(sem("ro_group"), 1)
                act.activation(ro[:, 72:80], ro[:, 72:80], ACT.Exp).then_inc(sem("ro_group_exp"), 1)
                act.wait_ge(sem("ro_pair"), 1)
                act.activation(ro[:, 200:202], ro[:, 200:202], ACT.Exp).then_inc(sem("ro_pair_exp"), 1)
                for q in range(EXPERTS // 2):
                    act.wait_ge(sem("comb_mm"), q + 1)
                    act.activation(combB[:, 2 * q:2 * q + 2, :], ps[:, 4 + q % 4, :].rearrange("p (e t) -> p e t", e=2),
                                   ACT.Copy).then_inc(sem("comb_copied"), 1)

                def step(i):
                    for e in range(4):
                        for j in range(3):
                            n = FIRST["moe"] + 3 * e + j
                            if j == 0:
                                act.wait_ge(used, i * 12 + (n + 1))
                                act.activation(e_silu, ps[:, 4, :], ACT.Silu).then_inc(sem("e_silu"), 1)
                            hi(n + AHEAD, i, per=12)
                with act.Fori(0, EXPERTS // 4 - 1) as i:
                    step(i)
                step(EXPERTS // 4 - 1)
                act.wait_ge(x_ready, 7)
                act.dma_start(finrow, a["norm_final_g_2"].unsqueeze(0).to_broadcast([P, D])
                              ).then_inc(sem("fin_in"), 16)
                norm("g", x_ready, 7)

            rwkv()
            ffn(1, FIRST["ffn1"])
            gates_and_mixer()
            moe()

        @block.vector
        def _(dve):
            chained = [0]
            chain = sem("dve_chain")

            def do(ins):
                chained[0] += 1
                ins.then_inc(chain, 1)

            def settle():
                dve.wait_ge(chain, chained[0])

            def norm(m, gain=None, shift=None, split=True):
                dve.wait_ge(sem("norm_ss"), nth(m))
                do(dve.tensor_scalar(rec, ss, 1.0 / D, EPS, ALU.mult, ALU.add))
                settle()
                dve.reciprocal(rec, rec).then_inc(sem("norm_rec"), 1)
                dve.wait_ge(sem("norm_rstd"), nth(m))
                for t in range(TT):
                    dve.tensor_scalar(tiles(slot(4), 2)[:, t, :], Xv[:, t, :], rstd[:, t:t + 1], None,
                                      ALU.mult).then_inc(sem("norm_xn"), 1)
                h = tiles(slot(0))
                for q in range(4):
                    dve.wait_ge(sem("norm_tp"), 4 * m + q + 1)
                    for j in (2 * q, 2 * q + 1):
                        src = ps[:, 4 + q, 256 * (j % 2):256 * (j % 2 + 1)]
                        if shift is None:
                            do(dve.tensor_scalar(h[:, j, :], src, gain(j), None, ALU.mult))
                        else:
                            do(dve.tensor_scalar(h[:, j, :], src, gain(j), shift(j), ALU.mult, ALU.add))
                    settle()
                    if not split:
                        continue
                    both = slice(2 * q, 2 * q + 2)
                    do(dve.tensor_copy(HhT[:, both, :], h[:, both, :]))
                    settle()
                    dve.tensor_tensor(HlT[:, both, :], h[:, both, :], HhT[:, both, :].bitcast(F32),
                                      ALU.subtract).then_inc(sem("norm_h"), 1)

            def add_to_x(done, count, ready):
                dve.wait_ge(done, count)
                for b in range(4):
                    ins = dve.tensor_tensor(Xv[:, b // 2, 512 * (b % 2):512 * (b % 2 + 1)], ps[:, b, :],
                                            Xv[:, b // 2, 512 * (b % 2):512 * (b % 2 + 1)], ALU.add)
                ins.then_inc(ready, 1)

            dve.memset(zeros, 0.0).then_inc(sem("zeros"), 1)
            dve.wait_ge(sem("cst_in"), 16)
            dve.wait_ge(sem("col_in"), 16)
            norm(0, lambda j: colv("norm_mix0", j))
            v = slot(5, 2).rearrange("p (t d) -> p t d", t=TT)
            bin_row = slot(7)
            dve.wait_ge(sem("bin_in"), 16)
            for c in range(8):
                dve.wait_ge(used, FIRST["sgu_v"] + c + 1)
                dve.tensor_tensor(v[:, :, 256 * c:256 * (c + 1)], ps[:, c % 4, :].rearrange("p (t n) -> p t n", t=TT),
                                  bin_row[:, 256 * c:256 * (c + 1)].unsqueeze(1).to_broadcast([P, TT, 256]),
                                  ALU.add).then_inc(sem("v_biased"), 1)
            wsT = slot(10)
            dve.wait_ge(sem("ws_in"), 16)
            dve.memset(tiles(wsT, SG)[CH:P, :, 0:CH], 0.0).then_inc(sem("ws_masked"), 1)
            dve.wait_ge(sem("v_gelu"), 8)
            for t in range(TT):
                for q in range(4):
                    do(dve.bn_stats(bns[:, (4 * t + q) * 6:(4 * t + q + 1) * 6], v[:, t, 512 * q:512 * (q + 1)]))
            settle()
            for t in range(TT):
                do(dve.bn_aggr(bna[:, 2 * t:2 * t + 2], bns[:, 24 * t:24 * t + 24]))
            settle()
            mv = bna.rearrange("p (t s) -> p t s", s=2)
            do(dve.tensor_scalar(rec.unsqueeze(2), mv[:, :, 1:2], LN_EPS, None, ALU.add))
            settle()
            dve.reciprocal(rec, rec).then_inc(sem("v_rec"), 1)
            gate_b = tiles(slot(1), SG)
            dve.wait_ge(sem("bs_in"), 16)
            dve.wait_ge(sem("rowsum_mm"), 1)
            for g in range(SG):
                ins = dve.scalar_tensor_tensor(gate_b[:, g, :], ps[:, g // 4, 128 * (g % 4):128 * (g % 4 + 1)],
                                               colv("sgu_ln_b", g), gate_b[:, g, :], ALU.mult, ALU.add)
            ins.then_inc(sem("gate_b"), 1)
            dve.wait_ge(sem("v_rstd"), 1)
            for t in range(TT):
                dve.tensor_scalar(v[:, t, :], v[:, t, :], bna[:, 2 * t:2 * t + 1], rstd[:, t:t + 1],
                                  ALU.subtract, ALU.mult).then_inc(sem("v_norm"), 1)
            dve.wait_ge(sem("gate_b"), 1)
            dve.wait_ge(sem("u_gelu"), 8)
            uT = slot(8, 2).rearrange("p (g t) -> p g t", g=SG)
            for q in range(8):
                tmp = slot(4)[:, 512 * (q % 2):512 * (q % 2) + 512]
                dve.wait_ge(sem("gate_mm"), q + 1)
                for g in (2 * q, 2 * q + 1):
                    src = ps[:, 4 + q % 4, 256 * (g % 2):256 * (g % 2 + 1)].rearrange("p (n i) -> p n i", n=TT)
                    do(dve.scalar_tensor_tensor(
                        tmp[:, 256 * (g % 2):256 * (g % 2 + 1)].rearrange("p (n i) -> p n i", n=TT), src,
                        colv("sgu_ln_g", g), gate_b[:, g, :].unsqueeze(1).to_broadcast([P, TT, P]),
                        ALU.mult, ALU.add))
                settle()
                two = uT[:, 2 * q:2 * q + 2, :].rearrange("p g t -> p (g t)")
                do(dve.tensor_tensor(tmp, tmp, two, ALU.mult))
                if q >= 2:
                    dve.wait_ge(used, FIRST["sgu_out"] + q - 1)
                settle()
                yh, yl = Ah[:, 512 * (q % 2):512 * (q % 2) + 512], Al[:, 512 * (q % 2):512 * (q % 2) + 512]
                do(dve.tensor_copy(yh, tmp))
                settle()
                dve.tensor_tensor(yl, tmp, yh.bitcast(F32), ALU.subtract).then_inc(sem("gate_y"), 1)
            add_to_x(used, FIRST["ffn0"], x_ready)

            def ffn(layer):
                m = 1 if layer == 0 else 3
                norm(m, lambda j: colv(f"norm_ffn{layer}", j))

                def squared(i, j):
                    r = slot(4)[:, 512 * j:512 * (j + 1)]
                    sq = slot(4)[:, 1024 + 512 * j:1024 + 512 * (j + 1)]
                    fh, fl = Fh[:, 512 * j:512 * (j + 1)], Fl[:, 512 * j:512 * (j + 1)]
                    dve.wait_ge(sem("ffn_relu"), i * 2 + (16 * layer + j + 1))
                    dve.tensor_tensor(sq, r, r, ALU.mult).then_inc(sem("ffn_sq"), 1)
                    dve.wait_ge(sem("ffn_sq"), i * 4 + (32 * layer + 2 * j + 1))
                    dve.tensor_copy(fh, sq).then_inc(sem("ffn_sq"), 1)
                    dve.wait_ge(sem("ffn_sq"), i * 4 + (32 * layer + 2 * j + 2))
                    dve.tensor_tensor(fl, sq, fh.bitcast(F32), ALU.subtract).then_inc(sem("ffn_hid"), 1)

                if layer == 1:
                    dve.memset(scr[:, 0:1], 0.0).then_inc(sem("ada_used"), 3)
                    dve.wait_ge(sem("c_sigmoid"), 1)
                    do(dve.tensor_tensor(cact, cact, col[:, COL["c"]:COL["c"] + KT], ALU.mult))
                    settle()

                def ada(i, j):
                    buf = slot(8 + j)
                    dve.wait_ge(sem(f"ada_in{j}"), i * 16 + 16)
                    dve.tensor_tensor(tiles(buf), tiles(buf), cact.unsqueeze(2).to_broadcast([P, KT, 256]),
                                      ALU.mult).then_inc(sem("ada_prod"), 1)
                    dve.wait_ge(sem("ada_prod"), i * 3 + (j + 1))
                    dve.tensor_reduce(macc[:, bass.ds(i * 768 + 256 * j, 256)], buf.rearrange("p (k n) -> p n k", k=KT),
                                      AX.X, ALU.add).then_inc(sem("ada_used"), 1)

                with dve.Fori(0, FFN // 512) as i:
                    for j in range(2):
                        squared(i, j)
                        if layer == 1:
                            ada(i, j)
                    if layer == 1:
                        ada(i, 2)
                add_to_x(used, FIRST["rwkv_k"] if layer == 0 else FIRST["in2"], x_ready)

            def mixed(dst, p):
                for j in range(KT):
                    ins = dve.scalar_tensor_tensor(dst[:, j, :], r_xx[:, j, :], colv("mu", 8 * p + j),
                                                   r_h[:, j, :], ALU.mult, ALU.add)
                return ins

            def split(src, ready):
                for q in range(4):
                    both = slice(2 * q, 2 * q + 2)
                    do(dve.tensor_copy(HhT[:, both, :], src[:, both, :]))
                    settle()
                    dve.tensor_tensor(HlT[:, both, :], src[:, both, :], HhT[:, both, :].bitcast(F32),
                                      ALU.subtract).then_inc(ready, 1)

            def flat(t):
                return t.rearrange("p k t -> p (k t)")

            def rwkv():
                norm(2, lambda j: colv("norm_mix1", j), split=False)
                do(dve.tensor_tensor(r_xx[:, :, 1:SEQ], r_h[:, :, 0:SEQ - 1], r_h[:, :, 1:SEQ], ALU.subtract))
                do(dve.tensor_scalar(r_xx[:, :, 0:1], r_h[:, :, 0:1], -1.0, None, ALU.mult))
                settle()
                mixed(r_xs, 3).then_inc(sem("xs"), 1)
                mixed(r_xsa, 4).then_inc(sem("xs"), 1)
                mixed(r_xsg, 5).then_inc(sem("xs"), 1)
                dve.wait_ge(sem("lora_mm"), 1)
                do(mixed(r_xs, 1))
                settle()
                dve.wait_ge(sem("lora2_mm"), 8)
                split(r_xs, sem("xs"))
                dve.wait_ge(sem("lora_sigmoid"), 4)
                for j in range(KT):
                    do(dve.tensor_tensor_scan(r_cum[:, j, :], cc("not_chunk_start"), r_sg[:, j, :], 0.0,
                                              ALU.mult, ALU.add))
                settle()
                dve.tensor_tensor(slot(5), slot(6), slot(5), ALU.subtract).then_inc(sem("cum_excl"), 1)
                dve.wait_ge(sem("lora_mm"), 3)
                for c in range(4):
                    dve.wait_ge(sem("rwkv_copied"), c + 1)
                    for j in (2 * c, 2 * c + 1):
                        do(dve.tensor_scalar(r_kk[:, j, :], r_k[:, j, :], colv("k_k", j), None, ALU.mult))
                settle()
                dve.tensor_tensor(slot(4), slot(10), slot(10), ALU.mult).then_inc(sem("kk_sq"), 1)
                dve.wait_ge(sem("kk_norm"), 1)
                do(dve.tensor_scalar(r_norm, r_norm, 1e-12, None, ALU.max))
                settle()
                dve.reciprocal(r_norm, r_norm).then_inc(sem("kk_rinv"), 1)
                do(mixed(r_xs, 0))
                settle()
                dve.wait_ge(used, FIRST["rwkv_r"])
                split(r_xs, sem("xs"))
                for q in range(4):
                    dve.wait_ge(sem("rinv_mm"), q + 1)
                    two = slot(10)[:, 512 * q:512 * (q + 1)]
                    do(dve.tensor_tensor(two, ps[:, q, :], two, ALU.mult))
                dve.wait_ge(sem("lora_sigmoid"), 8)
                settle()
                dve.wait_ge(sem("W_excl"), 1)
                do(dve.scalar_tensor_tensor(slot(5), slot(10), -1.0, slot(5), ALU.mult, ALU.mult))
                settle()
                do(dve.tensor_tensor(slot(10), slot(10), slot(7), ALU.mult))
                settle()
                for j in range(KT):
                    do(dve.tensor_scalar(r_a[:, j, :], r_a[:, j, :], 1.0, colv("k_a", j), ALU.subtract, ALU.mult))
                settle()
                dve.scalar_tensor_tensor(slot(9), slot(7), 1.0, slot(9), ALU.add, ALU.mult
                                         ).then_inc(sem("k_new"), 1)
                do(mixed(r_xs, 2))
                settle()
                dve.wait_ge(used, FIRST["rwkv_v"])
                split(r_xs, sem("xs"))
                dve.wait_ge(sem("xs"), 15)
                dve.memset(scr[:, 0:1], 0.0).then_inc(sem("tmp_free"), 1)
                dve.wait_ge(sem("rwkv_copied"), 8)
                dve.wait_ge(sem("k_new"), 1)
                for j in range(KT):
                    ins = dve.scalar_tensor_tensor(r_prod[:, j, :], r_r[:, j, :], colv("r_k", j), r_k[:, j, :],
                                                   ALU.mult, ALU.mult)
                ins.then_inc(sem("bonus_prod"), 1)
                dve.wait_ge(sem("bonus_prod"), 1)
                dve.wait_ge(sem("W_inv"), 1)
                do(dve.tensor_tensor(slot(10), slot(10), slot(4), ALU.mult))
                do(dve.tensor_tensor(slot(9), slot(9), slot(4), ALU.mult))
                dve.wait_ge(sem("W"), 1)
                do(dve.tensor_copy(wend.rearrange("p (j c) -> p j c", c=NCH), r_cum[:, :, CH - 1:SEQ:CH]))
                do(dve.tensor_tensor(slot(7), slot(7), slot(6), ALU.mult))
                settle()
                dve.memset(scr[:, 1:2], 0.0).then_inc(sem("scaled"), 1)
                dve.wait_ge(sem("bonus_mm"), 1)
                dve.tensor_copy(bonus, ps[:, 3, 0:32]).then_inc(sem("bonus_copied"), 1)
                for m, (name, _, _, mask) in enumerate(MATRICES):
                    for g in range(4):
                        idx = 4 * m + g
                        dve.wait_ge(sem("mat_mm"), idx + 1)
                        dve.tensor_tensor(
                            MATRIX_OUT[name][:, g // 2, g % 2::2, :],
                            ps[:, idx % 4, :].rearrange("p (h s) -> p h s", h=8),
                            cc(mask).unsqueeze(1).to_broadcast([P, 8, CH]), ALU.mult).then_inc(sem("mat_done"), 1)

                def per_head(t, i):
                    return t[:, i // 2, 8 * (i % 2):8 * (i % 2 + 1), :]

                def wide(ap):
                    return ap.unsqueeze(1).to_broadcast([P, 8, CH])
                dve.wait_ge(sem("mat_done"), 20)
                dve.wait_ge(sem("token_major_mm"), 8)
                for g in range(4):
                    do(dve.tensor_tensor(per_head(r_X, g), per_head(r_M, g), wide(cc("level1_lower")), ALU.mult))
                    do(dve.tensor_tensor(per_head(r_Y, g), per_head(r_Y, g), wide(cc("level_upper", 0, CH)), ALU.mult))
                settle()
                for g in range(4):
                    do(dve.tensor_tensor(per_head(r_X, g), per_head(r_X, g), wide(cc("ident64")), ALU.add))
                    do(dve.tensor_tensor(per_head(r_Y, g), per_head(r_Y, g), wide(cc("ident64")), ALU.add))
                settle()
                dve.memset(scr[:, 2:3], 0.0).then_inc(sem("inv_start"), 1)
                for lv in range(1, 6):
                    def q_part(g):
                        dve.wait_ge(sem("invQ_mm"), 4 * (lv - 1) + g + 1)
                        dve.tensor_tensor(r_Q[:, g % 2, :, :], ps[:, g % 2, :].rearrange("p (h s) -> p h s", h=8),
                                          wide(cc("level_upper", CH * lv, CH)), ALU.mult).then_inc(sem("invQ"), 1)

                    def y_part(g):
                        dve.wait_ge(sem("invY_mm"), 4 * (lv - 1) + g + 1)
                        ins = dve.tensor_tensor(per_head(r_Y, g), ps[:, 2 + g % 2, :].rearrange("p (h s) -> p h s", h=8),
                                                per_head(r_Y, g), ALU.add)
                        if lv < 5:
                            ins = dve.tensor_tensor(per_head(r_X, g),
                                                    ps[:, 4 + g % 2, :].rearrange("p (h s) -> p h s", h=8),
                                                    per_head(r_X, g), ALU.add)
                        ins.then_inc(sem("invY"), 1)
                    q_part(0)
                    for g in range(1, 4):
                        q_part(g)
                        y_part(g - 1)
                    y_part(3)

                for g in range(4):
                    dve.wait_ge(sem("U_mm"), g + 1)
                    dve.tensor_copy(per_head(r_U, g), ps[:, 4 + g, :].rearrange("p (h s) -> p h s", h=8)
                                    ).then_inc(sem("U"), 1)
                dve.wait_ge(sem("U"), 4)
                for c in range(NCH):
                    rows, t = slice(CH * (c % 2), CH * (c % 2 + 1)), c // 2

                    def bank(b):
                        return ps[rows, b, :].rearrange("p (j s) -> p j s", j=KT)
                    for g in range(2):
                        if c > 0:
                            dve.wait_ge(sem("R_mm"), 2 * (c - 1) + g + 1)
                            dve.tensor_tensor(r_RS[rows, 0, g::2, :], bank(g), r_U[rows, t, g::2, :],
                                              ALU.add).then_inc(sem("R"), 1)
                    for g in range(2):
                        dve.wait_ge(sem("SA_mm"), 2 * c + g + 1)
                        dve.tensor_copy(r_RS[rows, 1, g::2, :], bank(2 + g)).then_inc(sem("SA"), 1)
                    if c < NCH - 1:
                        dve.wait_ge(sem("Z_mm"), c + 1)
                        new, old = r_Z[:, (c + 1) % 2, :, :], r_Z[:, c % 2, :, :]
                        src = ps[:, 6, :].rearrange("p (j v) -> p j v", j=KT)
                        decay = wend.rearrange("p (j c) -> p j c", c=NCH)[:, :, c:c + 1].to_broadcast([P, KT, HD])
                        if c > 0:
                            do(dve.tensor_tensor(new, src, old, ALU.add))
                            settle()
                            dve.tensor_tensor(new, new, decay, ALU.mult).then_inc(sem("Z"), 1)
                        else:
                            dve.tensor_tensor(new, src, decay, ALU.mult).then_inc(sem("Z"), 1)
                        dve.wait_ge(sem("Z"), c + 1)
                    for g in range(2):
                        dve.wait_ge(sem("y_mm"), 2 * c + g + 1)
                        y = r_y[rows, t, g::2, :]
                        if c > 0:
                            dve.wait_ge(sem("y_state"), 2 * (c - 1) + g + 1)
                            dve.tensor_tensor(y, bank(4 + g), y, ALU.add).then_inc(sem("y_done"), 1)
                        else:
                            dve.tensor_copy(y, bank(4 + g)).then_inc(sem("y_done"), 1)

                y, y2 = slot(3).rearrange("p (g v) -> p g v", v=HD), slot(2).rearrange("p (g v) -> p g v", v=HD)
                mean, var = gst[:, 0:32], gst[:, 32:64]

                def per_group(ap):
                    return ap.unsqueeze(2).to_broadcast([P, 32, HD])
                dve.wait_ge(sem("y_done"), 2 * NCH)
                do(dve.tensor_reduce(mean, y, AX.X, ALU.add))
                settle()
                do(dve.tensor_scalar(mean, mean, 1.0 / HD, None, ALU.mult))
                settle()
                do(dve.tensor_tensor(y, y, per_group(mean), ALU.subtract))
                settle()
                dve.wait_ge(sem("y_mm"), 2 * NCH)
                do(dve.tensor_tensor(y2, y, y, ALU.mult))
                settle()
                do(dve.tensor_reduce(var, y2, AX.X, ALU.add))
                settle()
                do(dve.tensor_scalar(var, var, 1.0 / HD, GN_EPS, ALU.mult, ALU.add))
                settle()
                dve.reciprocal(var, var).then_inc(sem("gn_rec"), 1)
                do(dve.tensor_tensor(y2, slot(0).rearrange("p (g v) -> p g v", v=HD), per_group(bonus), ALU.mult))
                dve.wait_ge(sem("gn_rstd"), 1)
                do(dve.tensor_tensor(y, y, per_group(var), ALU.mult))
                settle()
                dve.wait_ge(sem("ln_in"), 32)
                y3 = tiles(slot(3), TT)
                do(dve.tensor_tensor(y3, y3, r_lnrow[:, 0:1, :].to_broadcast([P, TT, D]), ALU.mult))
                settle()
                do(dve.tensor_tensor(y3, y3, r_lnrow[:, 1:2, :].to_broadcast([P, TT, D]), ALU.add))
                settle()
                do(dve.tensor_tensor(slot(3), slot(3), slot(2), ALU.add))
                settle()
                for t in range(TT):
                    dve.wait_ge(sem("g_mm"), t + 1)
                    for half in range(2):
                        o = y3[:, t, 512 * half:512 * (half + 1)]
                        ins = dve.tensor_tensor(o, ps[:, 2 * t + half, :], o, ALU.mult)
                    ins.then_inc(sem("y_out"), 1)
                transposed_split("rwkv", ChT, ClT)
                add_to_x(used, FIRST["ffn1"], x_ready)

            def ada_columns():
                dve.wait_ge(sem("gate_in"), 32)
                dve.wait_ge(sem("gate_mm"), 9)
                do(dve.tensor_tensor(modcol, ps[:, 7, 0:48], col[:, COL["b_ada"]:COL["b_ada"] + 48], ALU.add))
                for b in range(4):
                    row = gates[:, b // 2, 512 * (b % 2):512 * (b % 2 + 1)]
                    do(dve.tensor_tensor(row, ps[:, b, :], row, ALU.add))
                settle()
                for m, name in enumerate(("norm_mix2", "norm_ffn2")):
                    do(dve.scalar_tensor_tensor(gain2[:, 8 * m:8 * m + 8], modcol[:, 24 * m + 8:24 * m + 16], 1.0,
                                                col[:, COL[name]:COL[name] + 8], ALU.add, ALU.mult))
                settle()
                dve.memset(scr[:, 0:1], 0.0).then_inc(sem("gates_done"), 1)

            def final_norm(m, count, ready):
                dve.wait_ge(sem("norm_ss"), nth(m))
                do(dve.tensor_scalar(rec, ss, 1.0 / D, EPS, ALU.mult, ALU.add))
                settle()
                dve.reciprocal(rec, rec).then_inc(sem("norm_rec"), 1)
                dve.wait_ge(sem("fin_in"), count)
                dve.wait_ge(sem("norm_rstd"), nth(m))
                for t in range(TT):
                    ins = dve.scalar_tensor_tensor(Xv[:, t, :], Xv[:, t, :], rstd[:, t:t + 1], finrow, ALU.mult, ALU.mult)
                ins.then_inc(ready, 1)

            def gated_add(m, done, count, ready):
                dve.wait_ge(done, count)
                tmp = slot(4)
                for b in range(4):
                    do(dve.tensor_tensor(tmp[:, 512 * b:512 * (b + 1)], ps[:, b, :],
                                         gates[:, m, 512 * (b % 2):512 * (b % 2 + 1)], ALU.mult))
                settle()
                dve.tensor_tensor(X[:, :], X[:, :], tmp, ALU.add).then_inc(ready, 1)

            def mixer2():
                ada_columns()
                final_norm("f", 16, x_ready)
                dve.wait_ge(x_ready, 5)
                norm(4, lambda j: gain2[:, j:j + 1], lambda j: modcol[:, j:j + 1])
                z = f_tmp[:, 0:16].rearrange("p (t n) -> p t n", t=TT)
                e = f_tmp[:, 16:32].rearrange("p (t n) -> p t n", t=TT)
                dve.wait_ge(sem("small_in"), 48)
                dve.wait_ge(sem("f_mm"), 1)
                do(dve.memset(lf2, 0.0))
                do(dve.tensor_tensor(z, ps[:, 3, 0:16].rearrange("p (t n) -> p t n", t=TT),
                                     s_b[:, 0:AH].unsqueeze(1).to_broadcast([P, TT, AH]), ALU.add))
                settle()
                do(dve.tensor_scalar(e, z, -1.0, None, ALU.mult))
                settle()
                dve.tensor_tensor(e, e, z, ALU.min).then_inc(sem("f_negabs"), 1)
                do(dve.tensor_scalar(z, z, 0.0, None, ALU.min))
                settle()
                dve.wait_ge(sem("f_ln"), 1)
                do(dve.tensor_tensor(lf2[:, :, 0:AH], z, e, ALU.subtract))
                dve.tensor_tensor(lf2[:, :, 24:32], e, z, ALU.subtract).then_inc(sem("f_log"), 1)
                dve.wait_ge(sem("F_mm"), 1)
                do(dve.tensor_scalar(f_a, ps[0:16, 3, 0:SEQ], f_cols[0:16, 0:1], None, ALU.add))
                do(dve.tensor_scalar(f_b, ps[0:16, 2, 0:SEQ], f_cols[0:16, 1:2], None, ALU.add))
                settle()
                for h in range(AH):
                    ins = dve.tensor_scalar(f_bh[:, h, :], f_b, f_cols[0:16, 2 + h:3 + h], None, ALU.mult)
                ins.then_inc(sem("F_rows"), 1)
                for g in range(PG):
                    dve.wait_ge(sem("pool_mm"), g + 1)
                    if g >= 2:
                        dve.wait_ge(sem("pmix_mm"), g - 1)
                    dve.tensor_copy(pdiff[:, g % 2, :], ps[:, 4 + g % 2, 0:SEQ]).then_inc(sem("pdiff"), 1)
                    dve.wait_ge(sem("pmix_mm"), g + 1)
                    do(dve.tensor_scalar(pmix[:, g % 2, :], ps[:, 6 + g % 2, 0:SEQ], colv("pool_scale", g), None,
                                         ALU.mult))
                    settle()
                    do(dve.tensor_copy(C2hT[:, 4 + g, :], pmix[:, g % 2, :]))
                    settle()
                    dve.tensor_tensor(C2lT[:, 4 + g, :], pmix[:, g % 2, :], C2hT[:, 4 + g, :].bitcast(F32),
                                      ALU.subtract).then_inc(sem("pool_done"), 1)

                def softmax_in(h):
                    p_, st = prob[:, h % 2, :], att_stat[:, h % 2, :]
                    dve.wait_ge(sem("score_mm"), h + 1)
                    if h >= 2:
                        dve.wait_ge(sem("probT_mm"), h - 1)
                    do(dve.tensor_tensor(p_, ps[:, h % 2, 0:3 * P], causal, ALU.add))
                    settle()
                    do(dve.tensor_tensor(p_, ps[:, 2 + h % 2, 0:3 * P], p_, ALU.add))
                    settle()
                    do(dve.tensor_reduce(st[:, 0:1], p_[:, 0:P], AX.X, ALU.max, negate=True))
                    dve.tensor_reduce(st[:, 1:2], p_[:, P:3 * P], AX.X, ALU.max, negate=True
                                      ).then_inc(sem("att_max"), 1)

                def softmax_out(h):
                    p_, st = prob[:, h % 2, :], att_stat[:, h % 2, :]
                    dve.wait_ge(sem("att_exp"), h + 1)
                    do(dve.reciprocal(st[:, 2:4], st[:, 2:4]))
                    settle()
                    do(dve.tensor_scalar(p_[:, 0:P], p_[:, 0:P], st[:, 2:3], None, ALU.mult))
                    dve.tensor_scalar(p_[:, P:3 * P], p_[:, P:3 * P], st[:, 3:4], None, ALU.mult
                                      ).then_inc(sem("prob"), 1)
                    dve.wait_ge(sem("probT_mm"), h + 1)
                    if h >= 2:
                        dve.wait_ge(sem("av_mm"), h - 1)
                    dve.tensor_copy(probT[:, h % 2, :], ps[:, 4 + h % 2, 0:3 * P]).then_inc(sem("probT"), 1)
                    if h % 2:
                        dve.wait_ge(sem("av_mm"), h + 1)
                        j = h // 2
                        src = ps[:, 6 + j % 2, 0:SEQ]
                        do(dve.tensor_copy(C2hT[:, j, :], src))
                        settle()
                        dve.tensor_tensor(C2lT[:, j, :], src, C2hT[:, j, :].bitcast(F32),
                                          ALU.subtract).then_inc(sem("att_done"), 1)
                dve.wait_ge(sem("pool_done"), PG)
                softmax_in(0)
                for h in range(AH):
                    if h + 1 < AH:
                        softmax_in(h + 1)
                    softmax_out(h)
                gated_add(0, used, FIRST["moe"], x_ready)

            def moe():
                norm(5, lambda j: gain2[:, 8 + j:9 + j], lambda j: modcol[:, 24 + j:25 + j])
                logits = ro[:, 0:72].rearrange("p (t n) -> p t n", t=TT)
                lg, le = logits[:, :, 0:NG], logits[:, :, NG:].rearrange("p t (g e) -> p t g e", g=NG)

                def field(at, n):
                    return ro[:, at:at + TT * n].rearrange("p (t n) -> p t n", t=TT)
                gexp, gone, gmax, top = field(72, NG), field(80, NG), field(88, 1), field(90, 1)
                sel, one1, one2, work = field(92, NE), field(108, NE), field(124, NE), field(140, NE)
                m1, m2, e2, w1 = field(156, 1), field(158, 1), field(200, 1), field(204, 1)
                w2, rank = field(206, 1), field(208, 1)
                prod = ro[:, 256:256 + TT * EXPERTS].rearrange("p (t g e) -> p t g e", t=TT, g=NG)
                comb = ro[:, 384:384 + TT * EXPERTS].rearrange("p (t g e) -> p t g e", t=TT, g=NG)

                def spread(ap, n):
                    return ap.to_broadcast([P, TT, n])

                def step(*args, **kw):
                    do(dve.tensor_tensor(*args, **kw))
                    settle()

                def first_max(dst, src, top_value, n):
                    desc = cc("descending", 8 - n, n).unsqueeze(1).to_broadcast([P, TT, n])
                    step(dst, src, spread(top_value, n), ALU.is_equal)
                    step(dst, dst, desc, ALU.mult)
                    do(dve.tensor_reduce(rank, dst, AX.X, ALU.max))
                    settle()
                    step(dst, dst, spread(rank, n), ALU.is_equal)

                dve.wait_ge(sem("ro_mm"), 1)
                step(logits, ps[:, 6, 0:72].rearrange("p (t n) -> p t n", t=TT),
                     s_b[:, AH:].unsqueeze(1).to_broadcast([P, TT, NR]), ALU.add)
                do(dve.tensor_reduce(gmax, lg, AX.X, ALU.max))
                settle()
                dve.tensor_tensor(gexp, lg, spread(gmax, NG), ALU.subtract).then_inc(sem("ro_group"), 1)
                first_max(gone, lg, gmax, NG)
                step(prod, le, gone.unsqueeze(3).to_broadcast([P, TT, NG, NE]), ALU.mult)
                do(dve.tensor_reduce(sel, prod.rearrange("p t g e -> p t e g"), AX.X, ALU.add))
                settle()
                do(dve.tensor_reduce(m1, sel, AX.X, ALU.max))
                settle()
                first_max(one1, sel, m1, NE)
                do(dve.scalar_tensor_tensor(work, one1, NEG, sel, ALU.mult, ALU.add))
                settle()
                do(dve.tensor_reduce(m2, work, AX.X, ALU.max))
                settle()
                dve.tensor_tensor(e2, m2, m1, ALU.subtract).then_inc(sem("ro_pair"), 1)
                first_max(one2, work, m2, NE)
                dve.wait_ge(sem("ro_group_exp"), 1)
                do(dve.tensor_reduce(top, gexp, AX.X, ALU.add))
                settle()
                do(dve.reciprocal(top, top))
                dve.wait_ge(sem("ro_pair_exp"), 1)
                do(dve.tensor_scalar(w1, e2, 1.0, None, ALU.add))
                settle()
                do(dve.reciprocal(w1, w1))
                settle()
                step(w1, w1, top, ALU.mult)
                step(w2, w1, e2, ALU.mult)
                step(one1, one1, spread(w1, NE), ALU.mult)
                step(one2, one2, spread(w2, NE), ALU.mult)
                step(one1, one1, one2, ALU.add)
                do(dve.tensor_copy(comb, gone.unsqueeze(3).to_broadcast([P, TT, NG, NE])))
                settle()
                dve.tensor_tensor(comb, comb, one1.unsqueeze(2).to_broadcast([P, TT, NG, NE]), ALU.mult
                                  ).then_inc(sem("comb"), 1)
                dve.wait_ge(sem("combT_mm"), 1)
                dve.tensor_copy(combT, ps[0:EXPERTS, 7, 0:SEQ]).then_inc(sem("combT"), 1)
                dve.wait_ge(sem("comb_copied"), EXPERTS // 2)
                with dve.Fori(0, EXPERTS) as i:
                    for f in range(2):
                        at = slice(256 * f, 256 * (f + 1))
                        if f == 0:
                            dve.wait_ge(sem("e_silu"), i + 1)
                            dve.wait_ge(sem("up0_mm"), i + 1)
                        else:
                            dve.wait_ge(used, i * 3 + (FIRST["moe"] + 2))
                        dve.tensor_tensor(e_tmp[:, at], ps[:, 5 + f, 0:256], e_silu[:, at], ALU.mult
                                          ).then_inc(sem("e_dve"), 1)
                        dve.wait_ge(sem("e_dve"), i * 6 + (3 * f + 1))
                        dve.tensor_tensor(e_tmp[:, at].unsqueeze(1), e_tmp[:, at].unsqueeze(1),
                                          combB[:, bass.ds(i, 1), :], ALU.mult).then_inc(sem("e_dve"), 1)
                        dve.wait_ge(sem("e_dve"), i * 6 + (3 * f + 2))
                        dve.tensor_copy(Eh[:, at], e_tmp[:, at]).then_inc(sem("e_dve"), 1)
                        dve.wait_ge(sem("e_dve"), i * 6 + (3 * f + 3))
                        dve.tensor_tensor(El[:, at], e_tmp[:, at], Eh[:, at].bitcast(F32), ALU.subtract
                                          ).then_inc(sem("e_hid"), 1)
                gated_add(1, used, PIECES, x_ready)
                final_norm("g", 32, x_ready)

            def transposed_split(name, dh, dl):
                for q in range(4):
                    dve.wait_ge(sem(f"{name}_tp"), q + 1)
                    both = slice(2 * q, 2 * q + 2)
                    src = ps[:, 4 + q, :].rearrange("p (f t) -> p f t", f=2)
                    do(dve.tensor_copy(dh[:, both, :], src))
                    settle()
                    dve.tensor_tensor(dl[:, both, :], src, dh[:, both, :].bitcast(F32),
                                      ALU.subtract).then_inc(sem(f"{name}_T"), 1)

            ffn(0)
            rwkv()
            ffn(1)
            mixer2()
            moe()
            dve.wait_ge(x_ready, 8)
            dve.memset(scr[:, 1:2], 0.0).then_inc(sem("out_ready"), 1)

        @block.tensor
        def _(pe):
            def mm3(o, sh, sl, mh, ml, start, stop):
                pe.matmul(o, sh, mh, start=start, stop=False, skip_group_check=True)
                pe.matmul(o, sh, ml, start=False, stop=False, skip_group_check=True)
                return pe.matmul(o, sl, mh, start=False, stop=stop, skip_group_check=True)

            def have(n, i=None, per=0):
                pe.wait_ge(lo_done, n + 1 if i is None else i * per + (n + 1))
                return n

            def feature_tiles(n, bank, xh, xl, wait_k=None):
                wh, wl = piece(whi, n, KT), piece(wlo, n, KT)
                for f in range(2):
                    for k in range(KT):
                        if wait_k and f == 0:
                            wait_k(k)
                        c = slice(P * f, P * (f + 1))
                        ins = mm3(ps[:, bank, 256 * f:256 * (f + 1)], wh[:, k, c], wl[:, k, c],
                                  xh[:, k, :], xl[:, k, :], k == 0, k == KT - 1)
                return ins

            def token_tiles(n, bank, xh, xl, wait_k=None):
                wh, wl = piece(whi, n, KT), piece(wlo, n, KT)
                for t in range(TT):
                    for k in range(KT):
                        if wait_k and t == 0:
                            wait_k(k)
                        c = slice(P * t, P * (t + 1))
                        ins = mm3(ps[:, bank, 256 * t:256 * (t + 1)], xh[:, k, c], xl[:, k, c],
                                  wh[:, k, :], wl[:, k, :], k == 0, k == KT - 1)
                return ins

            def accumulate(n, xh, xl, first, last, wait_k=None):
                wh, wl = piece(whi, n, 2), piece(wlo, n, 2)
                for k in range(2):
                    if wait_k:
                        wait_k(k)
                    for t in range(TT):
                        for half in range(2):
                            c = slice(P * t, P * (t + 1))
                            w = slice(512 * half, 512 * (half + 1))
                            ins = mm3(ps[:, 2 * t + half, :], xh[:, k, c], xl[:, k, c], wh[:, k, w], wl[:, k, w],
                                      first and k == 0, last and k == 1)
                ins.then_inc(used, 1)

            def norm(m):
                pe.wait_ge(sem("norm_xn"), TT * (m + 1))
                for q in range(4):
                    for j in (2 * q, 2 * q + 1):
                        for t in range(TT):
                            ins = pe.transpose(ps[:, 4 + q, 256 * (j % 2) + P * t:256 * (j % 2) + P * (t + 1)],
                                               tiles(slot(4), 2)[:, t, P * j:P * (j + 1)], ident)
                    ins.then_inc(sem("norm_tp"), 1)
                return lambda k: pe.wait_ge(sem("norm_h"), splits_before(m) + k // 2 + 1) if k % 2 == 0 else None

            pe.wait_ge(sem("cst_in"), 16)
            pe.wait_ge(sem("zeros"), 1)
            h_ready = norm(0)
            for c in range(8):
                n = have(FIRST["sgu_v"] + c)
                if c >= 4:
                    pe.wait_ge(sem("v_biased"), c - 3)
                token_tiles(n, c % 4, HhT, HlT, h_ready if c == 0 else None).then_inc(used, 1)
            for c in range(8):
                n = have(FIRST["sgu_u"] + c)
                if c >= 4:
                    pe.wait_ge(sem("u_gelu"), c - 3)
                feature_tiles(n, 4 + c % 4, HhT, HlT).then_inc(used, 1)
            pe.wait_ge(sem("ws_masked"), 1)
            pe.wait_ge(sem("v_biased"), 8)
            for q in range(4):
                ins = pe.matmul(ps[:, q, :], cc("ones"), slot(10)[:, 512 * q:512 * (q + 1)], start=True, stop=True)
            ins.then_inc(sem("rowsum_mm"), 1)
            v = slot(5, 2).rearrange("p (t d) -> p t d", t=TT)

            def gate(q):
                for g in (2 * q, 2 * q + 1):
                    for t in range(TT):
                        o = ps[:, 4 + q % 4, 256 * (g % 2) + P * t:256 * (g % 2) + P * (t + 1)]
                        ins = pe.matmul(o, v[:, t, P * g:P * (g + 1)], slot(10)[:, P * g:P * (g + 1)],
                                        start=True, stop=True)
                ins.then_inc(sem("gate_mm"), 1)
            pe.wait_ge(sem("v_norm"), TT)
            pe.wait_ge(sem("u_gelu"), 8)
            for q in range(4):
                gate(q)
            pe.wait_ge(sem("gate_b"), 1)
            for q in range(8):
                n = have(FIRST["sgu_out"] + q)
                pe.wait_ge(sem("gate_y"), q + 1)
                at = slice(512 * (q % 2), 512 * (q % 2) + 512)
                accumulate(n, tiles(Ah[:, at], 2), tiles(Al[:, at], 2), q == 0, q == 7)
                if q + 4 < 8:
                    gate(q + 4)

            def ffn(layer, base):
                m = 1 if layer == 0 else 3
                h_ready = norm(m)
                for b in range(4):
                    pe.matmul(ps[:, b, :], zeros, zero_cols, start=True, stop=False, skip_group_check=True)
                for k in range(0, KT, 2):
                    h_ready(k)
                with pe.Fori(0, FFN // 512) as i:
                    for j in range(2):
                        n = have(base + j, i, 4)
                        feature_tiles(n, 4 + j, HhT, HlT).then_inc(used, 1)
                    for j in range(2):
                        n = have(base + 2 + j, i, 4)
                        pe.wait_ge(sem("ffn_hid"), i * 2 + (16 * layer + j + 1))
                        at = slice(512 * j, 512 * (j + 1))
                        accumulate(n, tiles(Fh[:, at], 2), tiles(Fl[:, at], 2), False, False)

            def transposes(name, src):
                for q in range(4):
                    for j in (2 * q, 2 * q + 1):
                        for t in range(TT):
                            ins = pe.transpose(ps[:, 4 + q, 256 * (j % 2) + P * t:256 * (j % 2) + P * (t + 1)],
                                               src[:, t, P * j:P * (j + 1)], ident)
                    ins.then_inc(sem(f"{name}_tp"), 1)

            def fp32_k(o, w, x, k_tiles=KT):
                for k in range(k_tiles):
                    ins = pe.matmul(o, w[:, k, :], x[:, k, :], start=k == 0, stop=k == k_tiles - 1)
                return ins

            def rwkv():
                norm(2)
                pe.wait_ge(sem("lora_in"), 80)
                pe.wait_ge(sem("xs"), 1)
                fp32_k(ps[0:64, 0, 0:SEQ], r_la[:, :, 0:64], r_xs).then_inc(sem("lora_mm"), 1)
                pe.wait_ge(sem("xs"), 2)
                fp32_k(ps[64:128, 1, 0:SEQ], r_la[:, :, 64:128], r_xsa).then_inc(sem("lora_mm"), 1)
                pe.wait_ge(sem("xs"), 3)
                fp32_k(ps[:, 2, 0:SEQ], r_la[:, :, 128:256], r_xsg).then_inc(sem("lora_mm"), 1)
                for m, what in enumerate("wa"):
                    rows = slice(64 * m, 64 * (m + 1))
                    pe.wait_ge(sem("lora_mid"), m + 1)
                    for q in range(4):
                        if m:
                            pe.wait_ge(sem("lora_sigmoid"), q + 1)
                        for j in (2 * q, 2 * q + 1):
                            ins = pe.matmul(ps[:, 4 + q, 256 * (j % 2):256 * (j % 2 + 1)],
                                            r_lb[rows, P * j:P * (j + 1)], r_mid[rows, :], start=True, stop=True)
                        ins.then_inc(sem("lora2_mm"), 1)

                def xs_ready(before):
                    return lambda k: pe.wait_ge(sem("xs"), before + k // 2 + 1) if k % 2 == 0 else None
                for c in range(4):
                    n = have(FIRST["rwkv_k"] + c)
                    pe.wait_ge(sem("lora_sigmoid"), 4 + c + 1)
                    feature_tiles(n, 4 + c, HhT, HlT, xs_ready(3) if c == 0 else None).then_inc(used, 1)
                pe.wait_ge(sem("kk_sq"), 1)
                for j in range(KT):
                    ins = pe.matmul(ps[0:HEADS, 3, 0:SEQ], cc("head16", 14 - 2 * j, HEADS), r_tmp[:, j, :],
                                    start=j == 0, stop=j == KT - 1)
                ins.then_inc(sem("kk_sum_mm"), 1)
                pe.wait_ge(sem("headrows_in"), 16)
                pe.wait_ge(sem("kk_rinv"), 1)
                for q in range(4):
                    for j in (2 * q, 2 * q + 1):
                        ins = pe.matmul(ps[:, q, 256 * (j % 2):256 * (j % 2 + 1)], r_headrows[:, P * j:P * (j + 1)],
                                        r_norm, start=True, stop=True)
                    ins.then_inc(sem("rinv_mm"), 1)
                for c in range(4):
                    n = have(FIRST["rwkv_r"] + c)
                    pe.wait_ge(sem("rwkv_copied"), c + 1)
                    feature_tiles(n, 4 + c, HhT, HlT, xs_ready(7) if c == 0 else None).then_inc(used, 1)
                for c in range(4):
                    n = have(FIRST["rwkv_v"] + c)
                    pe.wait_ge(sem("rwkv_copied"), 4 + c + 1)
                    token_tiles(n, 4 + c, HhT, HlT, xs_ready(11) if c == 0 else None).then_inc(used, 1)
                pe.wait_ge(sem("bonus_prod"), 1)
                for j in range(KT):
                    for t in range(TT):
                        ins = pe.matmul(ps[:, 3, 16 * t + 2 * j:16 * t + 2 * j + 2], r_prod[:, j, P * t:P * (t + 1)],
                                        cc("head2"), start=True, stop=True)
                ins.then_inc(sem("bonus_mm"), 1)

                pe.wait_ge(sem("scaled"), 1)

                def matrix(idx):
                    _, left, right, _ = MATRICES[idx // 4]
                    t, g = idx % 4 // 2, idx % 2
                    if idx == 3:
                        pe.wait_ge(sem("bonus_copied"), 1)
                    if idx >= 4:
                        pe.wait_ge(sem("mat_done"), idx - 3)
                    f = slice(HD * g, HD * (g + 1))
                    for j in range(KT):
                        for c in (2 * t, 2 * t + 1):
                            tok = slice(CH * c, CH * (c + 1))
                            ins = pe.matmul(ps[CH * (c % 2):CH * (c % 2 + 1), idx % 4, CH * j:CH * (j + 1)],
                                            left[f, j, tok], right[f, j, tok], start=True, stop=True)
                    ins.then_inc(sem("mat_mm"), 1)

                def token_major(src, before):
                    for q in range(4):
                        pe.wait_ge(sem("rwkv_copied"), before + q + 1)
                        for j in range(4 * (q % 2), 4 * (q % 2) + 4):
                            ins = pe.transpose(ps[:, 4 + q, P * (j % 4):P * (j % 4 + 1)],
                                               src[:, j, P * (q // 2):P * (q // 2 + 1)], ident)
                        ins.then_inc(sem("token_major_mm"), 1)
                for idx in range(12):
                    matrix(idx)
                token_major(r_bt, 8)
                for idx in range(12, 20):
                    matrix(idx)
                token_major(r_kt, 12)

                def units(g):
                    for h in range(8 * (g % 2), 8 * (g % 2) + 8):
                        for half in range(2):
                            yield h, slice(CH * half, CH * (half + 1)), slice(CH * (h % 8), CH * (h % 8 + 1))
                pe.wait_ge(sem("inv_start"), 1)
                pe.wait_ge(sem("rwkv_copied"), 20)
                for lv in range(1, 6):
                    def q_part(g):
                        if lv > 1:
                            pe.wait_ge(sem("invY"), 4 * (lv - 2) + g + 1)
                        for h, rows, at in units(g):
                            ins = pe.matmul(ps[rows, g % 2, at], r_M[rows, g // 2, h, :], r_Y[rows, g // 2, h, :],
                                            start=True, stop=True)
                        ins.then_inc(sem("invQ_mm"), 1)

                    def y_part(g):
                        pe.wait_ge(sem("invQ"), 4 * (lv - 1) + g + 1)
                        if lv > 1 or g >= 2:
                            pe.wait_ge(sem("invY"), 4 * (lv - 1) + g - 1)
                        for h, rows, at in units(g):
                            ins = pe.matmul(ps[rows, 2 + g % 2, at], r_X[rows, g // 2, h, :], r_Q[rows, g % 2, h % 8, :],
                                            start=True, stop=True)
                        if lv < 5:
                            for h, rows, at in units(g):
                                ins = pe.matmul(ps[rows, 4 + g % 2, at], r_Q[rows, g % 2, h % 8, :],
                                                r_X[rows, g // 2, h, :], start=True, stop=True)
                        ins.then_inc(sem("invY_mm"), 1)
                    q_part(0)
                    for g in range(1, 4):
                        q_part(g)
                        y_part(g - 1)
                    y_part(3)

                pe.wait_ge(sem("invY"), 20)
                for g in range(4):
                    for h, rows, at in units(g):
                        ins = pe.matmul(ps[rows, 4 + g, at], r_Aak[rows, g // 2, h, :],
                                        r_v[rows, g // 2, HD * h:HD * (h + 1)], start=True, stop=True)
                    ins.then_inc(sem("U_mm"), 1)

                for c in range(NCH):
                    t, rows, tok = c // 2, slice(CH * (c % 2), CH * (c % 2 + 1)), slice(CH * c, CH * (c + 1))
                    Z = r_Z[:, c % 2, :, :]

                    def bank_heads(g):
                        for j in range(KT):
                            yield 2 * j + g, j, slice(HD * g, HD * (g + 1)), slice(CH * j, CH * (j + 1))
                    if c > 0:
                        pe.wait_ge(sem("Z"), c)
                        pe.wait_ge(sem("y_state"), 2 * (c - 1)) if c > 1 else None
                        for g in range(2):
                            for h, j, f, at in bank_heads(g):
                                ins = pe.matmul(ps[rows, g, at], r_at[f, j, tok], Z[f, j, :], start=True, stop=True)
                            ins.then_inc(sem("R_mm"), 1)
                    for g in range(2):
                        if c > 0:
                            pe.wait_ge(sem("R"), 2 * (c - 1) + g + 1)
                        else:
                            pe.wait_ge(sem("U"), 4)
                        for h, j, f, at in bank_heads(g):
                            R = r_RS[rows, 0, h, :] if c > 0 else r_U[rows, 0, h, :]
                            ins = pe.matmul(ps[rows, 2 + g, at], r_Y[rows, t, h, :], R, start=True, stop=True)
                        ins.then_inc(sem("SA_mm"), 1)
                    if c > 0:
                        for g in range(2):
                            for h, j, f, at in bank_heads(g):
                                ins = pe.matmul(ps[rows, g, at], r_rt[f, j, tok], Z[f, j, :], start=True, stop=True)
                            ins.then_inc(sem("ystate_mm"), 1)
                    pe.wait_ge(sem("SA"), 2 * c + 2)
                    if c < NCH - 1:
                        for h in range(HEADS):
                            f, j = slice(HD * (h % 2), HD * (h % 2 + 1)), h // 2
                            o = ps[f, 6, HD * j:HD * (j + 1)]
                            pe.matmul(o, r_btm[rows, t, h, :], r_RS[rows, 1, h, :], start=True, stop=False)
                            ins = pe.matmul(o, r_ktm[rows, t, h, :], r_v[rows, t, HD * h:HD * (h + 1)],
                                            start=False, stop=True)
                        ins.then_inc(sem("Z_mm"), 1)
                    for g in range(2):
                        if c > 0:
                            pe.wait_ge(sem("y_done"), 2 * (c - 1) + g + 1)
                        for h, j, f, at in bank_heads(g):
                            pe.matmul(ps[rows, 4 + g, at], r_Arb[rows, t, h, :], r_RS[rows, 1, h, :],
                                      start=True, stop=False)
                            ins = pe.matmul(ps[rows, 4 + g, at], r_Ark[rows, t, h, :],
                                            r_v[rows, t, HD * h:HD * (h + 1)], start=False, stop=True)
                        ins.then_inc(sem("y_mm"), 1)
                pe.wait_ge(sem("gb_in"), 16)
                pe.wait_ge(sem("g_sigmoid"), 1)
                pe.wait_ge(sem("y_state"), 2 * (NCH - 1))
                for t in range(TT):
                    for half in range(2):
                        ins = pe.matmul(ps[:, 2 * t + half, :], gsig[:, P * t:P * (t + 1)],
                                        r_gb[:, 512 * half:512 * (half + 1)], start=True, stop=True)
                    ins.then_inc(sem("g_mm"), 1)
                pe.wait_ge(sem("y_out"), TT)
                transposes("rwkv", tiles(slot(3), TT))
                for c in range(4):
                    n = have(FIRST["rwkv_o"] + c)
                    pe.wait_ge(sem("rwkv_T"), c + 1)
                    accumulate(n, ChT[:, 2 * c:2 * c + 2, :], ClT[:, 2 * c:2 * c + 2, :], c == 0, c == 3)

            def mixer2():
                pe.wait_ge(sem("ada_used"), 27)
                ones = cc("ones")
                for j in range(6 * KT):
                    ins = pe.matmul(ps[:, 7, j:j + 1], macc[:, P * j:P * (j + 1)], ones[:, 0:1], start=True, stop=True)
                pe.wait_ge(x_ready, 4)
                for b in range(4):
                    at = (2 if b < 2 else 5) * D + 512 * (b % 2)
                    ins = pe.matmul(ps[:, b, :], ones, macc[:, at:at + 512], start=True, stop=True)
                ins.then_inc(sem("gate_mm"), 1)
                pe.wait_ge(sem("gates_done"), 1)
                h_ready = norm(4)
                pe.wait_ge(sem("small_in"), 48)
                pe.wait_ge(sem("norm_h"), splits_before(4) + 4)
                for t in range(TT):
                    for k in range(KT):
                        ins = pe.matmul(ps[:, 3, AH * t:AH * (t + 1)], r_h[:, k, P * t:P * (t + 1)], w_f[:, k, :],
                                        start=k == 0, stop=k == KT - 1)
                ins.then_inc(sem("f_mm"), 1)
                for c in range(8):
                    n = have(FIRST["in2"] + c)
                    if c >= 4:
                        pe.wait_ge(sem("in2_copied"), c - 3)
                    (feature_tiles if c < 4 else token_tiles)(n, 4 + c % 4, HhT, HlT).then_inc(used, 1)
                    if c == 5:
                        pe.wait_ge(sem("f_log"), 1)
                        for b, at in ((3, 0), (2, 16)):
                            for t in range(TT):
                                ins = pe.matmul(ps[0:16, b, 0:SEQ], lf2[:, t, at:at + 16], cum[:, t, :],
                                                start=t == 0, stop=t == TT - 1)
                        ins.then_inc(sem("F_mm"), 1)
                pe.wait_ge(sem("in2_copied"), 8)
                pe.wait_ge(sem("pool_in"), 16)

                def pool_mean(g):
                    for t in range(TT):
                        ins = pe.matmul(ps[:, 4 + g % 2, 0:SEQ], utm[:, t, P * g:P * (g + 1)], poolm[:, t, g, :],
                                        start=t == 0, stop=t == TT - 1)
                    ins.then_inc(sem("pool_mm"), 1)

                def pool_mix(g):
                    pe.wait_ge(sem("pdiff"), g + 1)
                    pe.matmul(ps[:, 6 + g % 2, 0:SEQ], w_pool[:, g, :], pdiff[:, g % 2, :],
                              start=True, stop=True).then_inc(sem("pmix_mm"), 1)
                pool_mean(0)
                pool_mean(1)
                for g in range(PG):
                    if g >= 2:
                        pe.wait_ge(sem("pool_done"), g - 1)
                    pool_mix(g)
                    if g + 2 < PG:
                        pool_mean(g + 2)
                pe.wait_ge(sem("F_rows"), 1)

                def scores(h):
                    f, j = slice(HD * (h % 2), HD * (h % 2 + 1)), h // 2
                    if h >= 2:
                        pe.wait_ge(sem("att_max"), h - 1)
                    for o, t, s_ in ((slice(0, P), 0, P), (slice(P, 3 * P), 1, SEQ)):
                        tok = slice(P * t, P * (t + 1))
                        pe.matmul(ps[:, h % 2, o], qT[f, j, tok], kT[f, j, 0:s_], start=True, stop=True)
                    for o, t, s_ in ((slice(0, P), 0, P), (slice(P, 3 * P), 1, SEQ)):
                        tok = slice(P * t, P * (t + 1))
                        ins = pe.matmul(ps[:, 2 + h % 2, o], f_a[:, tok], f_bh[:, h, 0:s_], start=True, stop=True)
                    ins.then_inc(sem("score_mm"), 1)
                pe.wait_ge(sem("pool_done"), PG)
                scores(0)
                scores(1)
                for h in range(AH):
                    pe.wait_ge(sem("prob"), h + 1)
                    if h >= 2:
                        pe.wait_ge(sem("probT"), h - 1)
                    for b in range(3):
                        ins = pe.transpose(ps[:, 4 + h % 2, P * b:P * (b + 1)], prob[:, h % 2, P * b:P * (b + 1)], ident)
                    ins.then_inc(sem("probT_mm"), 1)
                    if h + 2 < AH:
                        scores(h + 2)
                    pe.wait_ge(sem("probT"), h + 1)
                    j, f = h // 2, slice(HD * (h % 2), HD * (h % 2 + 1))
                    if j >= 2:
                        pe.wait_ge(sem("att_done"), j - 1)
                    V = [vtm[:, t, HD * h:HD * (h + 1)] for t in range(TT)]
                    o, pT = ps[f, 6 + j % 2, 0:SEQ], probT[:, h % 2, :]
                    pe.matmul(o[:, 0:P], V[0], pT[:, 0:P], start=True, stop=True)
                    pe.matmul(o[:, P:SEQ], V[0], pT[:, P:2 * P], start=True, stop=False)
                    pe.matmul(o[:, P:SEQ], V[1], pT[:, 2 * P:3 * P], start=False, stop=True).then_inc(sem("av_mm"), 1)
                for c in range(4):
                    n = have(FIRST["out2"] + c)
                    if c < 2:
                        pe.wait_ge(sem("att_done"), 4)
                    accumulate(n, C2hT[:, 2 * c:2 * c + 2, :], C2lT[:, 2 * c:2 * c + 2, :], c == 0, c == 3)

            def moe():
                norm(5)
                pe.wait_ge(sem("norm_h"), splits_before(5) + 4)
                for t in range(TT):
                    for k in range(KT):
                        ins = pe.matmul(ps[:, 6, NR * t:NR * (t + 1)], r_h[:, k, P * t:P * (t + 1)], w_r[:, k, :],
                                        start=k == 0, stop=k == KT - 1)
                ins.then_inc(sem("ro_mm"), 1)
                pe.wait_ge(sem("comb"), 1)
                for t in range(TT):
                    ins = pe.transpose(ps[0:EXPERTS, 7, P * t:P * (t + 1)],
                                       ro[:, 384 + EXPERTS * t:384 + EXPERTS * (t + 1)], ident)
                ins.then_inc(sem("combT_mm"), 1)
                pe.wait_ge(sem("combT"), 1)
                for e in range(EXPERTS):
                    if e % 2 == 0 and e >= 8:
                        pe.wait_ge(sem("comb_copied"), e // 2 - 3)
                    ins = pe.matmul(ps[:, 4 + e // 2 % 4, 256 * (e % 2):256 * (e % 2 + 1)],
                                    ident[0:EXPERTS, e:e + 1].to_broadcast([EXPERTS, P]), combT, start=True, stop=True)
                    if e % 2:
                        ins.then_inc(sem("comb_mm"), 1)
                pe.wait_ge(sem("comb_copied"), EXPERTS // 2)
                for b in range(4):
                    pe.matmul(ps[:, b, :], zeros, zero_cols, start=True, stop=False, skip_group_check=True)
                base = FIRST["moe"]
                with pe.Fori(0, EXPERTS // 4) as i:
                    for e in range(4):
                        n = have(base + 3 * e, i, 12)
                        feature_tiles(n, 4, HhT, HlT).then_inc(used, 1)
                        n = have(base + 3 * e + 1, i, 12)
                        wh, wl = piece(whi, n, KT), piece(wlo, n, KT)
                        for f in range(2):
                            for k in range(KT):
                                c = slice(P * f, P * (f + 1))
                                ins = mm3(ps[:, 5 + f, 0:256], wh[:, k, c], wl[:, k, c],
                                          HhT[:, k, :], HlT[:, k, :], k == 0, k == KT - 1)
                            ins.then_inc(sem("up0_mm") if f == 0 else used, 1)
                        n = have(base + 3 * e + 2, i, 12)
                        eh, el = tiles(Eh[:, :], 2), tiles(El[:, :], 2)
                        accumulate(n, eh, el, False, False,
                                   lambda k: pe.wait_ge(sem("e_hid"), i * 8 + (2 * e + k + 1)))

            ffn(0, FIRST["ffn0"])
            rwkv()
            ffn(1, FIRST["ffn1"])
            mixer2()
            moe()


def kernel(**inputs):
    import concourse.bacc as bacc
    from concourse.bass_utils import run_bass_kernel_spmd

    def columns(v):
        return np.asarray(v, np.float32).reshape(-1, P).T

    g = {k: np.asarray(v) for k, v in inputs.items()}
    parts = {"norm_mix0": g["norm_mix_g"][0], "norm_mix1": g["norm_mix_g"][1],
             "norm_ffn0": g["norm_ffn_g"][0], "norm_ffn1": g["norm_ffn_g"][1],
             "b_in_u": g["sgu_b_in"][0, :SGU], "sgu_ln_g": g["sgu_ln_g"], "sgu_ln_b": g["sgu_ln_b"],
             "mu": g["rwkv_mu"], "w0": g["rwkv_w0"], "a0": g["rwkv_a0"], "k_k": g["rwkv_k_k"],
             "k_a": g["rwkv_k_a"], "r_k": g["rwkv_r_k"], "norm_mix2": g["norm_mix_g_2"],
             "norm_ffn2": g["norm_ffn_g_2"], "pool_scale": g["pool_scale_2"], "c": g["c_2"], "b_ada": g["b_ada_2"]}
    arrays = {name: np.ascontiguousarray(g[name]) for name in DIRECT}
    arrays["cols"] = np.ascontiguousarray(np.concatenate([columns(parts[name]) for name, _ in COLS], 1))
    arrays["consts"] = shape_constants()
    arrays["head_rows"] = head_rows()
    arrays["attention_consts"] = attention_constants()
    arrays["pool_matrices"] = pool_matrices().reshape(P, TT * PG * SEQ)

    def rows(w):
        return w.reshape(KT, P, -1).transpose(1, 0, 2)
    router = np.concatenate([g["w_router_group_2"][0], *g["w_router_expert_2"][0]], 1)
    arrays["w_small"] = np.ascontiguousarray(np.concatenate(
        [rows(g["w_in_2"][0][:, 3 * AW:3 * AW + AH]).reshape(P, -1), rows(router).reshape(P, -1),
         g["w_pool_2"][0].transpose(1, 0, 2).reshape(P, -1)], 1))
    arrays["b_small"] = np.concatenate([g["b_fgate_2"].reshape(1, -1), g["b_router_group_2"].reshape(1, -1),
                                        g["b_router_expert_2"].reshape(1, -1)], 1)
    arrays["sgu_w_sT"] = np.ascontiguousarray(g["sgu_w_s"][0].transpose(2, 0, 1).reshape(P, SG * P))

    nc = bacc.Bacc("TRN2", target_bir_lowering=False, num_devices=1)
    dram = {name: nc.dram_tensor(f"in_{name}", v.shape, mybir.dt.from_np(v.dtype), kind="ExternalInput").ap()
            for name, v in arrays.items()}
    out = nc.dram_tensor("out", (1, SEQ, D), F32, kind="ExternalOutput").ap()
    build(nc, dram, out)
    r = run_bass_kernel_spmd(nc, [{f"in_{name}": v for name, v in arrays.items()}], core_ids=[0])
    return r.results[0]["out"]
```

```python
from contextlib import ExitStack

import numpy as np
import concourse.bass as bass
from concourse import mybir

F32 = mybir.dt.float32
F32R = mybir.dt.float32r
ALU = mybir.AluOpType
ACT = mybir.ActivationFunctionType
AX = mybir.AxisListType

P = 128
SEQ, D = 256, 1024
TT = SEQ // P
KT = D // P
SGU = 2 * D
SG = SGU // P
FFN = 4 * D
HEADS, HD = 16, 64
CH = 64
NCH = SEQ // CH
AH = 8
AW = AH * HD
PG = 4
WINDOWS = (2, 4, 8, 16)
NORMS = [0, 1, 2, 3, "f", 4, 5, "g"]
NG, NE = 4, 8
EXPERTS = NG * NE
DE = 256
NMOD = 6
CAP = 64
QUAD = 4 * CAP
EXTRA = 8
EPS, LN_EPS, GN_EPS = 1e-6, 1e-5, 64e-5
KAPPA = float(np.exp(-0.5))
NEG = -1e30
RING = 4
AHEAD = 3
SLOT = 2048

STAGES = [("sgu_v", 8), ("sgu_u", 8), ("sgu_out", 8), ("ffn0", 32), ("rwkv_k", 4), ("rwkv_r", 4),
          ("rwkv_v", 4), ("rwkv_o", 4), ("ffn1", 32), ("in2", 8), ("out2", 4)]
FIRST, PIECES = {}, 0
for _name, _count in STAGES:
    FIRST[_name] = PIECES
    PIECES += _count

COLS = [("norm_mix0", 8), ("norm_mix1", 8), ("norm_ffn0", 8), ("norm_ffn1", 8), ("b_in_u", 16),
        ("sgu_ln_g", 16), ("sgu_ln_b", 16), ("mu", 48), ("w0", 8), ("a0", 8), ("k_k", 8),
        ("k_a", 8), ("r_k", 8), ("norm_mix2", 8), ("norm_ffn2", 8), ("pool_scale", 4), ("c", 8), ("b_ada", 48)]
COL, NCOL = {}, 0
for _name, _count in COLS:
    COL[_name] = NCOL
    NCOL += _count

CONSTS = [("ident", 128), ("ones", 128), ("strict_lower", 64), ("strict_upper", 64),
          ("incl_upper", 64), ("level1_lower", 64), ("level_upper", 6 * 64), ("ident64", 64),
          ("not_chunk_start", 256), ("head2", 2), ("head16", 30), ("descending", 8)]
CST, NCST = {}, 0
for _name, _count in CONSTS:
    CST[_name] = NCST
    NCST += _count
CST_WIDTH = dict(CONSTS)


def shape_constants():
    c = np.zeros((P, NCST), np.float32)

    def put(name, value):
        c[:, CST[name]:CST[name] + value.shape[1]] = value

    put("ident", np.eye(P))
    put("ones", np.ones((P, P)))
    t = np.arange(P)[:, None] % CH
    s = np.arange(CH)[None, :]
    put("strict_lower", (t > s) * 1.0)
    put("strict_upper", (t < s) * 1.0)
    put("incl_upper", (t <= s) * 1.0)
    put("ident64", (t == s) * 1.0)
    put("level1_lower", ((t // 2 == s // 2) & (t > s)) * 1.0)
    levels = []
    for n in range(6):
        m = 2 ** n
        levels.append(((t // (2 * m) == s // (2 * m)) & (t // m % 2 == 0) & (s // m % 2 == 1)) * 1.0)
    put("level_upper", np.concatenate(levels, 1))
    put("not_chunk_start", np.broadcast_to((np.arange(SEQ) % CH != 0) * 1.0, (P, SEQ)))
    half = np.arange(P)[:, None] // HD
    put("head2", (np.arange(2)[None, :] == half) * 1.0)
    put("descending", np.broadcast_to(np.arange(8, 0, -1.0), (P, 8)))
    put("head16", (np.arange(30)[None, :] == 14 + half) * 1.0)
    return c


def head_rows():
    return (np.arange(HEADS)[:, None] == np.arange(D)[None, :] // HD).astype(np.float32)


def pool_matrices():
    out = np.zeros((PG, SEQ, SEQ), np.float32)
    for g, w in enumerate(WINDOWS):
        for t in range(SEQ):
            lo = max(0, t - w + 1)
            out[g, lo:t + 1, t] = 1.0 / min(t + 1, w)
            out[g, t, t] -= 1.0
    return np.ascontiguousarray(out.reshape(PG, TT, P, SEQ).transpose(2, 1, 0, 3))


def attention_constants():
    t, s = np.arange(P)[:, None], np.arange(P)[None, :]
    diag = np.where(s <= t, 0.0, NEG)
    mask = np.concatenate([diag, np.zeros((P, P)), diag], 1)
    cum = (np.arange(SEQ)[:, None] <= np.arange(SEQ)[None, :]) * 1.0
    cum = cum.reshape(TT, P, SEQ).transpose(1, 0, 2).reshape(P, TT * SEQ)
    rows = np.zeros((P, 2 + AH))
    rows[AH:2 * AH, 0] = 1.0
    rows[0:AH, 1] = 1.0
    for h in range(AH):
        rows[h, 2 + h] = rows[AH + h, 2 + h] = 1.0
    return np.concatenate([mask, cum, rows], 1).astype(np.float32)


ATTC = 3 * P + TT * SEQ + 2 + AH


DIRECT = ["x", "ffn_w1", "ffn_w2", "sgu_w_in", "sgu_b_in", "sgu_b_s", "sgu_w_out", "rwkv_w_rkv",
          "rwkv_w_o", "w_ada_2", "w_in_2", "w_out_2", "w_expert_gate_2", "w_expert_up_2",
          "w_expert_down_2", "rwkv_w_lora_a", "rwkv_w_lora_b", "rwkv_a_lora_a", "rwkv_a_lora_b",
          "rwkv_g_lora_a", "rwkv_g_lora_b", "rwkv_ln_g", "rwkv_ln_b", "final_norm_g", "norm_final_g_2",
          "b_ada_2"]


def build(nc, a, out):
    with ExitStack() as ctx:
        sems = {}

        def sem(name):
            if name not in sems:
                sems[name] = ctx.enter_context(nc.semaphore(name))
            return sems[name]

        where = [(nc.sbuf_base + 31) // 32 * 32]

        def sb(name, cols, dt=F32, at=None):
            offset = where[0] if at is None else at
            t = nc.alloc_sbuf_tensor_at(name, [P, cols], dt, offset=offset)
            if at is None:
                where[0] = offset + (4 * cols + 31) // 32 * 32
            return t

        raw = [sb(f"raw{i}", SLOT) for i in range(RING)]
        whi = [sb(f"whi{i}", SLOT, F32R) for i in range(RING)]
        wlo = [sb(f"wlo{i}", SLOT, F32R) for i in range(RING)]
        X = sb("X", TT * D)
        arena_at = where[0]
        arena = sb("arena", 11 * SLOT + SLOT // 2)
        cst = sb("cst", NCST)
        col = sb("col", NCOL)
        small = sb("small", 640)
        zeros_bf = nc.alloc_sbuf_tensor_at("zeros_bf", [P, P], mybir.dt.bfloat16, offset=where[0])
        where[0] += 2 * P
        zeros, zero_cols = zeros_bf[:, :], zeros_bf[:, 0:1].to_broadcast([P, 512])
        assert where[0] <= nc.sbuf_usable_end, where[0]

        Xv = X[:, :].rearrange("p (t d) -> p t d", t=TT)

        def slot(i, n=1):
            return arena[:, i * SLOT:(i + n) * SLOT]

        def slot_r(name, i, cols, skip=0):
            return sb(name, cols, F32R, at=arena_at + 4 * (i * SLOT + skip))

        def tiles(ap, k=KT):
            return ap.rearrange("p (k t) -> p k t", k=k)

        def cc(name, lo=0, n=None):
            n = CST_WIDTH[name] if n is None else n
            return cst[:, CST[name] + lo:CST[name] + lo + n]

        def colv(name, j):
            return col[:, COL[name] + j:COL[name] + j + 1]

        ident = cc("ident")
        ss = small[:, 0:2]
        rec = small[:, 2:4]
        rstd = small[:, 4:6]
        bns = small[:, 8:8 + 48]
        bna = small[:, 56:60]
        wend = small[:, 64:96]
        bonus = small[:, 96:128]
        gst = small[:, 128:224]
        scr = small[:, 224:384]
        gsig = small[:, 384:640]

        Hh = slot_r("Hh", 2, SLOT)
        Hl = slot_r("Hl", 3, SLOT)
        HhT, HlT = tiles(Hh[:, :]), tiles(Hl[:, :])
        Ah = slot_r("Ah", 0, 1024)
        Al = slot_r("Al", 0, 1024, 1024)
        Ch = slot_r("Ch", 5, SLOT)
        Cl = slot_r("Cl", 6, SLOT)
        ChT, ClT = tiles(Ch[:, :]), tiles(Cl[:, :])
        Fh = slot_r("Fh", 0, 1024)
        Fl = slot_r("Fl", 0, 1024, 1024)

        r_h, r_xx, r_xs = tiles(slot(0)), tiles(slot(1)), tiles(slot(4))
        r_xsa, r_xsg = tiles(slot(9)), tiles(slot(10))
        r_la = slot(8).rearrange("p (k n) -> p k n", k=KT)
        r_lb = arena[:, 11 * SLOT:11 * SLOT + D]
        r_mid = slot(3)[:, 0:SEQ]
        r_sg, r_cum, r_a = tiles(slot(5)), tiles(slot(6)), tiles(slot(7))
        r_k, r_kk, r_r = tiles(slot(9)), tiles(slot(10)), tiles(slot(7))
        r_tmp, r_prod = tiles(slot(4)), tiles(slot(1))
        r_headrows = slot(8)[0:HEADS, 0:D]
        r_norm = arena[0:HEADS, 11 * SLOT:11 * SLOT + SEQ]
        r_v = tiles(slot(0), TT)
        r_at, r_rt, r_kt, r_bt = tiles(slot(5)), tiles(slot(7)), tiles(slot(9)), tiles(slot(10))

        def heads(i):
            return slot(i).rearrange("p (t h s) -> p t h s", t=TT, h=HEADS)

        r_M, r_Y, r_Aak, r_Arb, r_Ark, r_X = heads(1), heads(2), heads(3), heads(4), heads(6), heads(9)
        r_btm, r_ktm = heads(8), heads(10)
        r_Q = arena[:, 11 * SLOT:11 * SLOT + D].rearrange("p (b h s) -> p b h s", b=2, h=8)
        r_U = heads(9)
        r_RS = slot(1).rearrange("p (w h s) -> p w h s", w=2, h=HEADS)
        r_Z = arena[:, 11 * SLOT:11 * SLOT + D].rearrange("p (b j v) -> p b j v", b=2, j=KT)
        r_y, r_y2 = heads(3), heads(2)
        r_lnrow = slot(4).rearrange("p (w d) -> p w d", w=2)
        r_gb = slot(8)[:, 0:D]
        MATRICES = [("M", r_at, r_bt, "strict_lower"), ("N", r_bt, r_at, "strict_upper"),
                    ("Arb", r_bt, r_rt, "incl_upper"), ("Aak", r_kt, r_at, "strict_upper"),
                    ("Ark", r_kt, r_rt, "incl_upper")]
        MATRIX_OUT = {"M": r_M, "N": r_Y, "Arb": r_Arb, "Aak": r_Aak, "Ark": r_Ark}

        NR = NG + EXPERTS
        W_SMALL = KT * AH + KT * NR + PG * P
        B_SMALL = AH + NR
        s_w = slot(1)[:, 0:W_SMALL]
        s_b = slot(1)[:, W_SMALL:W_SMALL + B_SMALL]
        s_c = slot(1)[:, W_SMALL + B_SMALL:W_SMALL + B_SMALL + ATTC]
        w_f = s_w[:, 0:KT * AH].rearrange("p (k n) -> p k n", k=KT)
        w_r = s_w[:, KT * AH:KT * (AH + NR)].rearrange("p (k n) -> p k n", k=KT)
        w_pool = s_w[:, KT * (AH + NR):].rearrange("p (g n) -> p g n", g=PG)
        causal = s_c[:, 0:3 * P]
        cum = s_c[:, 3 * P:3 * P + TT * SEQ].rearrange("p (t n) -> p t n", t=TT)
        f_cols = s_c[:, 3 * P + TT * SEQ:]
        cact = scr[:, 8:16]
        modcol = scr[:, 16:64]
        gain2 = scr[:, 64:80]
        macc = slot(5, 3)
        gates = slot(10).rearrange("p (m d) -> p m d", m=2)
        finrow_first, finrow = slot(8)[:, 0:D], slot(7)[:, 0:D]
        qT, kT = tiles(slot(5)[:, 0:1024], 4), tiles(slot(5)[:, 1024:2048], 4)
        vtm, utm = tiles(slot(6)[:, 0:1024], TT), tiles(slot(6)[:, 1024:2048], TT)
        poolm = slot(7).rearrange("p (t g n) -> p t g n", t=TT, g=PG)
        lf2 = arena[:, 11 * SLOT:11 * SLOT + 64].rearrange("p (t n) -> p t n", t=TT)
        f_tmp = arena[:, 11 * SLOT + 64:11 * SLOT + 128]
        f_a = arena[0:2 * AH, 11 * SLOT + 128:11 * SLOT + 384]
        f_b = arena[0:2 * AH, 11 * SLOT + 384:11 * SLOT + 640]
        f_bh = tiles(slot(4), AH)[0:2 * AH]
        prob = slot(2)[:, 0:6 * P].rearrange("p (b n) -> p b n", b=2)
        probT = slot(3)[:, 0:6 * P].rearrange("p (b n) -> p b n", b=2)
        pdiff = slot(2)[:, 1024:1536].rearrange("p (b n) -> p b n", b=2)
        pmix = slot(3)[:, 1024:1536].rearrange("p (b n) -> p b n", b=2)
        att_stat = gst[:, 0:8].rearrange("p (b n) -> p b n", b=2)
        moe_index = nc.alloc_sbuf_tensor_at("moe_index", [P, EXTRA + 1], mybir.dt.int32, offset=where[0])
        where[0] += 64
        assert where[0] <= nc.sbuf_usable_end, where[0]
        iota = small[:, 384:640]
        slots12 = scr[:, 0:4].rearrange("p (w t) -> p w t", w=2)
        wslot = scr[:, 128:132].rearrange("p (b n) -> p b n", b=2)
        G12 = slot(8)[:, 0:4 * QUAD].rearrange("p (w t n) -> p w t n", w=2, t=TT)
        e_silu, e_hid = (slot(8)[:, 4 * QUAD + 2 * CAP * n:4 * QUAD + 2 * CAP * (n + 1)] for n in range(2))
        e_parts = slot(8)[:, 5 * QUAD:5 * QUAD + 2 * DE]
        Gr = slot_r("Gr", 9, TT * QUAD)
        GrT = tiles(Gr[:, :], TT)
        scatter = [slot_r(f"scatter{b}", 9, TT * QUAD, TT * QUAD * (b + 1)) for b in range(2)]
        ring_at = (nc.sbuf_base + 31) // 32 * 32
        picked = []
        for b, places in enumerate(((arena_at + 4 * 5 * SLOT, arena_at + 4 * 6 * SLOT),
                                    (arena_at + 4 * 4 * SLOT, ring_at + 4 * 11 * SLOT))):
            picked.append([sb(f"picked{b}{n}", SLOT, F32R, at=place)[:, :].rearrange(
                "p (k e s n) -> p k e s n", k=4, e=4, s=2) for n, place in enumerate(places)])
        picked_raw = sb("picked_raw", 2 * QUAD, at=ring_at + 4 * 10 * SLOT)
        w_down_in = [sb(f"w_down_in{b}", SLOT, at=ring_at + 4 * (6 + b) * SLOT) for b in range(2)]
        Yh, Yl = slot_r("Yh", 0, D), slot_r("Yl", 0, D, D)
        XhT, XlT = tiles(Hh[:, :], TT), tiles(Hl[:, :], TT)
        C2h, C2l = slot_r("C2h", 8, SLOT), slot_r("C2l", 9, SLOT)
        C2hT, C2lT = tiles(C2h[:, :]), tiles(C2l[:, :])
        ro = arena[:, 11 * SLOT:11 * SLOT + D]

        ps = ctx.enter_context(nc.psum_tensor("ps", [P, 8, 512], F32))

        x_ready = sem("x_ready")

        def nth(m):
            return NORMS.index(m) + 1

        raw_in = [sem(f"raw_in{i}") for i in range(RING)]
        hi_done, lo_done, used = sem("hi_done"), sem("lo_done"), sem("pieces_done")

        def piece(ring, n, k):
            return ring[n % RING][:, :].rearrange("p (k n) -> p k n", k=k)

        block = ctx.enter_context(nc.Block())

        def krows(w):
            return w.rearrange("(k p) n -> p k n", p=P)

        ffn_w1 = [krows(a["ffn_w1"][i]) for i in range(2)]
        ffn_w2 = [krows(a["ffn_w2"][i]) for i in range(2)]
        w_down = a["w_expert_down_2"][0].rearrange("g e (k p) n -> p (g e k) n", p=P)
        w_gate = a["w_expert_gate_2"][0].rearrange("g e (k p) n -> p (g e k) n", p=P)
        w_up = a["w_expert_up_2"][0].rearrange("g e (k p) n -> p (g e k) n", p=P)

        @block.sync
        def _(sp):
            def load(n, src, i=None, k=KT, per=0):
                if i is not None:
                    sp.wait_ge(lo_done, i * per + (n - RING + 1))
                elif n >= RING:
                    sp.wait_ge(lo_done, n - RING + 1)
                sp.dma_start(piece(raw, n, k), src).then_inc(raw_in[n % RING], 16)

            sp.dma_start(Xv, a["x"][0].rearrange("(t p) d -> p t d", p=P)).then_inc(sem("x_in"), 16)
            sp.dma_start(cst[:, :], a["consts"]).then_inc(sem("cst_in"), 16)
            sp.dma_start(col[:, :], a["cols"]).then_inc(sem("col_in"), 16)
            w = krows(a["sgu_w_in"][0])
            for c in range(8):
                load(FIRST["sgu_v"] + c, w[:, :, SGU + 256 * c:SGU + 256 * (c + 1)])
            for c in range(8):
                load(FIRST["sgu_u"] + c, w[:, :, 256 * c:256 * (c + 1)])
            w = krows(a["sgu_w_out"][0])
            for c in range(8):
                load(FIRST["sgu_out"] + c, w[:, 2 * c:2 * c + 2, :], k=2)

            def ffn_loads(layer, n):
                with sp.Fori(0, FFN // 512) as i:
                    for j in range(2):
                        load(n + j, ffn_w1[layer][:, :, bass.ds(i * 512 + 256 * j, 256)], i, per=4)
                    for j in range(2):
                        load(n + 2 + j, ffn_w2[layer][:, bass.ds(i * 4 + 2 * j, 2), :], i, k=2, per=4)
                    if layer == 1:
                        for j in range(3):
                            sp.wait_ge(sem("ada_used"), i * 3 + (j + 1))
                            sp.dma_start(tiles(slot(8 + j)),
                                         krows(a["w_ada_2"][0])[:, :, bass.ds(i * 768 + 256 * j, 256)]
                                         ).then_inc(sem(f"ada_in{j}"), 16)

            ffn_loads(0, FIRST["ffn0"])
            for name, which in (("rwkv_k", 1), ("rwkv_r", 0), ("rwkv_v", 2)):
                w = krows(a["rwkv_w_rkv"][0, which])
                for c in range(4):
                    load(FIRST[name] + c, w[:, :, 256 * c:256 * (c + 1)])
            w = krows(a["rwkv_w_o"][0])
            for c in range(4):
                load(FIRST["rwkv_o"] + c, w[:, 2 * c:2 * c + 2, :], k=2)
            ffn_loads(1, FIRST["ffn1"])
            w = krows(a["w_in_2"][0])
            for c in range(8):
                at = 256 * c if c < 6 else 256 * c + AH
                load(FIRST["in2"] + c, w[:, :, at:at + 256])
            w = krows(a["w_out_2"][0])
            for c in range(4):
                load(FIRST["out2"] + c, w[:, 2 * c:2 * c + 2, :], k=2)
            def expert_load(e, v, i=None):
                b = e % 2
                for j, (w, n) in enumerate(((w_gate, 8), (w_up, 8), (w_down, 2))):
                    free = sem(("gate_lo", "up_lo", "expert_done")[j])
                    if i is not None:
                        sp.wait_ge(free, i * 2 + (e - 1))
                    elif e >= 2:
                        sp.wait_ge(free, e - 1)
                    dst = w_down_in[b] if j == 2 else raw[2 * b + j]
                    sp.dma_start(dst[:, :].rearrange("p (k n) -> p k n", k=n), w[:, bass.ds(v * n, n), :]
                                 ).then_inc(sem(f"down_in{b}" if j == 2 else f"gate_up_in{b}"), 16)
            sp.wait_ge(used, PIECES)
            expert_load(0, 0)
            expert_load(1, 1)
            with sp.Fori(0, EXPERTS // 2 - 1) as i:
                for e in (2, 3):
                    expert_load(e, i * 2 + e, i)
            sp.wait_ge(sem("moe_index"), 1)
            v = sp.value_load(moe_index[0:1, 0:1], min_val=0, max_val=EXPERTS - 1)
            expert_load(EXPERTS, v)
            more = sp.value_load(moe_index[0:1, EXTRA:EXTRA + 1], min_val=0, max_val=EXTRA)
            with sp.If(more > 0):
                for o in range(1, EXTRA + 1):
                    at = min(o, EXTRA - 1)
                    v = sp.value_load(moe_index[0:1, at:at + 1], min_val=0, max_val=EXPERTS - 1)
                    expert_load(EXPERTS + o, v)
            sp.wait_ge(sem("out_ready"), 1)
            sp.dma_start(out[0].rearrange("(t p) d -> p t d", p=P), Xv).then_inc(sem("out_done"), 16)
            sp.wait_ge(sem("out_done"), 16)

        @block.gpsimd
        def _(pool):
            def lo(n, i=None):
                pool.wait_ge(hi_done, n + 1 if i is None else i * RING + (n + 1))
                pool.tensor_tensor(wlo[n % RING][:, :], raw[n % RING][:, :],
                                   whi[n % RING][:, :].bitcast(F32), ALU.subtract).then_inc(lo_done, 1)
            with pool.Fori(0, PIECES // RING) as i:
                for n in range(RING):
                    lo(n, i)
            def gate_lo(e, i=None):
                pool.wait_ge(sem("expert_hi"), 2 * e + 1 if i is None else i * 4 + (2 * e + 1))
                pool.tensor_tensor(wlo[0][:, :], raw[2 * (e % 2)][:, :], whi[0][:, :].bitcast(F32),
                                   ALU.subtract).then_inc(sem("gate_lo"), 1)
            gate_lo(0)
            with pool.Fori(0, EXPERTS // 2) as i:
                gate_lo(1, i)
                gate_lo(2, i)
            pool.wait_ge(sem("moe_index"), 1)
            more = pool.value_load(moe_index[0:1, EXTRA:EXTRA + 1], min_val=0, max_val=EXTRA)
            with pool.If(more > 0):
                with pool.Fori(EXPERTS // 2, (EXPERTS + EXTRA) // 2) as i:
                    gate_lo(1, i)
                    gate_lo(2, i)

        @block.scalar
        def _(act):
            def hi(n, i=0, per=0):
                if isinstance(i, int):
                    n += per * i
                    if n >= PIECES:
                        return
                    act.wait_ge(raw_in[n % RING], 16 * (n // RING + 1))
                    if n >= RING:
                        act.wait_ge(used, n - RING + 1)
                else:
                    act.wait_ge(raw_in[n % RING], i * (16 * per // RING) + 16 * (n // RING + 1))
                    act.wait_ge(used, i * per + (n - RING + 1))
                act.activation(whi[n % RING][:, :], raw[n % RING][:, :], ACT.Copy).then_inc(hi_done, 1)

            def norm(m, version):
                for t in range(TT):
                    if version == 0:
                        act.wait_ge(sem("x_in"), 16)
                    else:
                        act.wait_ge(x_ready, TT * (version - 1) + t + 1)
                    ins = act.activation(tiles(slot(4), 2)[:, t, :], Xv[:, t, :], ACT.Square,
                                         accum_out=ss[:, t:t + 1])
                ins.then_inc(sem("norm_ss"), 1)
                act.wait_ge(sem("norm_rec"), nth(m))
                act.activation(rstd, rec, ACT.Sqrt).then_inc(sem("norm_rstd"), 1)

            act.dma_start(slot(7), a["sgu_b_in"][:, SGU:2 * SGU].to_broadcast([P, SGU])
                          ).then_inc(sem("bin_in"), 16)
            act.dma_start(slot(10), a["sgu_w_sT"]).then_inc(sem("ws_in"), 16)
            act.dma_start(slot(1), a["sgu_b_s"].rearrange("n g i -> n (g i)").to_broadcast([P, SGU])
                          ).then_inc(sem("bs_in"), 16)
            norm(0, 0)
            for n in range(AHEAD):
                hi(n)
            v = slot(5, 2).rearrange("p (t d) -> p t d", t=TT)
            uT = tiles(slot(8, 2), SG)
            for c in range(8):
                act.wait_ge(sem("v_biased"), c + 1)
                act.activation(v[:, :, 256 * c:256 * (c + 1)], v[:, :, 256 * c:256 * (c + 1)],
                               ACT.Gelu).then_inc(sem("v_gelu"), 1)
                hi(FIRST["sgu_v"] + c + AHEAD)
            act.wait_ge(sem("col_in"), 16)
            for c in range(8):
                act.wait_ge(used, FIRST["sgu_u"] + c + 1)
                for f in range(2):
                    ins = act.activation(uT[:, 2 * c + f, :], ps[:, 4 + c % 4, 256 * f:256 * (f + 1)],
                                         ACT.Gelu, bias=colv("b_in_u", 2 * c + f))
                ins.then_inc(sem("u_gelu"), 1)
                hi(FIRST["sgu_u"] + c + AHEAD)
            act.wait_ge(sem("v_rec"), 1)
            act.activation(rstd, rec, ACT.Sqrt).then_inc(sem("v_rstd"), 1)
            for c in range(8):
                hi(FIRST["sgu_out"] + c + AHEAD)

            def ffn(layer, n):
                m = 1 if layer == 0 else 3
                norm(m, m)
                if layer == 1:
                    act.activation(cact, col[:, COL["c"]:COL["c"] + KT], ACT.Sigmoid).then_inc(sem("c_sigmoid"), 1)
                if layer == 0:
                    for at, w, name in ((0, 64, "w"), (64, 64, "a"), (128, 128, "g")):
                        act.dma_start(r_la[:, :, at:at + w], krows(a[f"rwkv_{name}_lora_a"][0])
                                      ).then_inc(sem("lora_in"), 16)
                    act.dma_start(r_lb[0:64, :], a["rwkv_w_lora_b"][0]).then_inc(sem("lora_in"), 16)
                    act.dma_start(r_lb[64:128, :], a["rwkv_a_lora_b"][0]).then_inc(sem("lora_in"), 16)

                def step(i):
                    for j in range(4):
                        if j < 2:
                            act.wait_ge(used, i * 4 + (n + j + 1))
                            act.activation(slot(4)[:, 512 * j:512 * (j + 1)], ps[:, 4 + j, :],
                                           ACT.Relu).then_inc(sem("ffn_relu"), 1)
                        hi(n + j + AHEAD, i, per=4)
                with act.Fori(0, FFN // 512 - 1) as i:
                    step(i)
                step(FFN // 512 - 1)

            def rwkv():
                norm(2, 2)
                act.wait_ge(sem("lora_mm"), 1)
                act.activation(r_mid[0:64, :], ps[0:64, 0, 0:SEQ], ACT.Tanh).then_inc(sem("lora_mid"), 1)
                act.wait_ge(sem("lora_mm"), 2)
                act.activation(r_mid[64:128, :], ps[64:128, 1, 0:SEQ], ACT.Copy).then_inc(sem("lora_mid"), 1)
                act.wait_ge(sem("lora_mm"), 3)
                act.activation(gsig, ps[:, 2, 0:SEQ], ACT.Sigmoid).then_inc(sem("g_sigmoid"), 1)
                act.dma_start(r_headrows, a["head_rows"]).then_inc(sem("headrows_in"), 16)
                for what, dst, bias in (("w", r_sg, "w0"), ("a", r_a, "a0")):
                    for q in range(4):
                        act.wait_ge(sem("lora2_mm"), (4 if what == "a" else 0) + q + 1)
                        for j in (2 * q, 2 * q + 1):
                            ins = act.activation(dst[:, j, :], ps[:, 4 + q, 256 * (j % 2):256 * (j % 2 + 1)],
                                                 ACT.Sigmoid, bias=colv(bias, j))
                        ins.then_inc(sem("lora_sigmoid"), 1)

                def copies(name, dst):
                    for c in range(4):
                        act.wait_ge(used, FIRST[name] + c + 1)
                        if name == "rwkv_v":
                            o = dst[:, :, 256 * c:256 * (c + 1)]
                            src = ps[:, 4 + c, :].rearrange("p (t n) -> p t n", t=TT)
                        else:
                            o = dst[:, 2 * c:2 * c + 2, :]
                            src = ps[:, 4 + c, :].rearrange("p (f n) -> p f n", f=2)
                        act.activation(o, src, ACT.Copy).then_inc(sem("rwkv_copied"), 1)
                        hi(FIRST[name] + c + AHEAD)

                copies("rwkv_k", r_k)
                act.wait_ge(sem("kk_sum_mm"), 1)
                act.activation(r_norm, ps[0:HEADS, 3, 0:SEQ], ACT.Sqrt).then_inc(sem("kk_norm"), 1)
                act.wait_ge(sem("cum_excl"), 1)
                act.activation(slot(5), slot(5), ACT.Exp, scale=-KAPPA).then_inc(sem("W_excl"), 1)
                act.wait_ge(sem("k_new"), 1)
                copies("rwkv_r", r_r)
                copies("rwkv_v", r_v)
                act.wait_ge(sem("tmp_free"), 1)
                act.activation(slot(4), slot(6), ACT.Exp, scale=KAPPA).then_inc(sem("W_inv"), 1)
                act.wait_ge(sem("W_inv"), 1)
                act.activation(slot(6), slot(6), ACT.Exp, scale=-KAPPA).then_inc(sem("W"), 1)
                for m, dst in enumerate((r_btm, r_ktm)):
                    for q in range(4):
                        act.wait_ge(sem("token_major_mm"), 4 * m + q + 1)
                        act.activation(dst[:, q // 2, 8 * (q % 2):8 * (q % 2 + 1), :].rearrange("p h s -> p (h s)"),
                                       ps[:, 4 + q, :], ACT.Copy).then_inc(sem("rwkv_copied"), 1)
                for c in range(1, NCH):
                    rows = slice(CH * (c % 2), CH * (c % 2 + 1))
                    for g in range(2):
                        act.wait_ge(sem("ystate_mm"), 2 * (c - 1) + g + 1)
                        act.activation(r_y[rows, c // 2, g::2, :], ps[rows, g, :].rearrange("p (j s) -> p j s", j=KT),
                                       ACT.Copy).then_inc(sem("y_state"), 1)
                act.wait_ge(sem("y_mm"), 2 * NCH)
                act.dma_start(r_lnrow[:, 0, :], a["rwkv_ln_g"].to_broadcast([P, D])).then_inc(sem("ln_in"), 16)
                act.dma_start(r_lnrow[:, 1, :], a["rwkv_ln_b"].to_broadcast([P, D])).then_inc(sem("ln_in"), 16)
                act.dma_start(r_gb, a["rwkv_g_lora_b"][0]).then_inc(sem("gb_in"), 16)
                act.wait_ge(sem("gn_rec"), 1)
                act.activation(gst[:, 32:64], gst[:, 32:64], ACT.Sqrt).then_inc(sem("gn_rstd"), 1)
                for c in range(4):
                    hi(FIRST["rwkv_o"] + c + AHEAD)

            ffn(0, FIRST["ffn0"])
            def gates_and_mixer():
                act.wait_ge(sem("ada_used"), 27)
                act.dma_start(gates[:, 0, :], a["b_ada_2"][:, 2 * D:3 * D].to_broadcast([P, D])
                              ).then_inc(sem("gate_in"), 16)
                act.dma_start(gates[:, 1, :], a["b_ada_2"][:, 5 * D:6 * D].to_broadcast([P, D])
                              ).then_inc(sem("gate_in"), 16)
                act.dma_start(s_w, a["w_small"]).then_inc(sem("small_in"), 16)
                act.dma_start(s_b, a["b_small"].to_broadcast([P, B_SMALL])).then_inc(sem("small_in"), 16)
                act.dma_start(s_c, a["attention_consts"]).then_inc(sem("small_in"), 16)
                act.dma_start(finrow_first, a["final_norm_g"].unsqueeze(0).to_broadcast([P, D])
                              ).then_inc(sem("fin_in"), 16)
                norm("f", 4)
                norm(4, 5)
                act.wait_ge(sem("gate_mm"), 9)
                act.dma_start(slot(7), a["pool_matrices"]).then_inc(sem("pool_in"), 16)
                for c in range(8):
                    act.wait_ge(used, FIRST["in2"] + c + 1)
                    src = ps[:, 4 + c % 4, :].rearrange("p (f n) -> p f n", f=2)
                    if c < 4:
                        o = (qT if c < 2 else kT)[:, 2 * (c % 2):2 * (c % 2) + 2, :]
                    else:
                        o = (vtm if c < 6 else utm)[:, :, 256 * (c % 2):256 * (c % 2 + 1)]
                    act.activation(o, src, ACT.Copy, scale=HD ** -0.5 if c < 2 else 1.0
                                   ).then_inc(sem("in2_copied"), 1)
                    hi(FIRST["in2"] + c + AHEAD)
                    if c == 3:
                        fl = f_tmp[:, 16:32].rearrange("p (t n) -> p t n", t=TT)
                        act.wait_ge(sem("f_negabs"), 1)
                        act.activation(fl, fl, ACT.Exp).then_inc(sem("f_ln"), 1)
                        act.wait_ge(sem("f_ln"), 1)
                        act.activation(fl, fl, ACT.Ln, bias=1.0).then_inc(sem("f_ln"), 1)
                for h in range(AH):
                    st = att_stat[:, h % 2, :]
                    act.wait_ge(sem("att_max"), h + 1)
                    p_ = prob[:, h % 2, :]
                    act.activation(p_[:, 0:P], p_[:, 0:P], ACT.Exp, bias=st[:, 0:1], accum_out=st[:, 2:3])
                    act.activation(p_[:, P:3 * P], p_[:, P:3 * P], ACT.Exp, bias=st[:, 1:2],
                                   accum_out=st[:, 3:4]).then_inc(sem("att_exp"), 1)
                for c in range(4):
                    hi(FIRST["out2"] + c + AHEAD)

            def moe():
                act.dma_start(iota, a["iota"]).then_inc(sem("iota_in"), 16)
                norm(5, 6)
                act.wait_ge(sem("ro_logits"), 1)
                act.activation(ro[:, 72:80], ro[:, 72:80], ACT.Exp).then_inc(sem("ro_exp"), 1)
                act.wait_ge(sem("ro_logits"), 2)
                act.activation(ro[:, 200:202], ro[:, 200:202], ACT.Exp).then_inc(sem("ro_exp"), 1)

                def split_hi(e, j, i=0):
                    if j == 0:
                        act.wait_ge(sem(f"gate_up_in{e % 2}"), i * 128 + 32 * (e // 2 + 1))
                    act.activation(whi[j][:, :], raw[2 * (e % 2) + j][:, :], ACT.Copy).then_inc(sem("expert_hi"), 1)

                def copy_picked(part, bank):
                    for f in range(2):
                        k = 2 * part + f
                        ins = act.activation(picked_raw[:, QUAD * f:QUAD * (f + 1)], ps[:, bank, QUAD * f:QUAD * (f + 1)],
                                             ACT.Identity, scale=gain2[:, 8 + k:9 + k], bias=modcol[:, 24 + k:25 + k])
                    ins.then_inc(sem("picked_raw"), 1)
                split_hi(0, 0)
                split_hi(0, 1)
                for part in range(4):
                    act.wait_ge(sem("gather_mm"), part + 1)
                    if part > 0:
                        act.wait_ge(sem("picked"), part)
                    copy_picked(part, 4 + part)
                act.wait_ge(sem("scatter_tp"), 1)
                act.activation(scatter[1][:, :], ps[:, 3, :], ACT.Copy)
                act.activation(scatter[0][:, :], ps[:, 3, :], ACT.Copy).then_inc(sem("scatter_copied"), 1)

                def weigh(i, q, pair):
                    act.wait_ge(sem("expert_done"), i * 8 + (4 * q + 2 * pair + 2))
                    for half in range(2):
                        ins = act.activation(Yh[:, 512 * half:512 * (half + 1)], ps[:, 4 + half, :], ACT.Copy,
                                             scale=wslot[:, q, pair:pair + 1])
                    ins.then_inc(sem("Y_hi"), 1)

                def two_quads(i):
                    for q in range(2):
                        for e in range(4):
                            n = 4 * q + e
                            if e == 2:
                                weigh(i, q, 0)
                            act.wait_ge(sem("expert_gate_mm"), i * 8 + (n + 1))
                            split_hi(n + 1, 0, i)
                            act.wait_ge(sem("gate_up_mm"), i * 8 + (n + 1))
                            act.activation(e_parts, ps[:, 6, :], ACT.Copy).then_inc(sem("e_parts"), 1)
                            act.wait_ge(sem("e_sum_mm"), i * 8 + (n + 1))
                            act.activation(e_silu, ps[:, 6, 0:2 * CAP], ACT.Silu).then_inc(sem("e_silu"), 1)
                            act.wait_ge(sem("gather_mm"), i * 8 + (n + 5))
                            act.wait_ge(sem("picked"), i * 8 + (n + 4))
                            copy_picked(e, 7)
                            split_hi(n + 1, 1, i)
                        weigh(i, q, 1)
                        act.wait_ge(sem("scatter_tp"), i * 2 + (q + 2))
                        act.activation(scatter[1 - q][:, :], ps[:, 7, :], ACT.Copy).then_inc(sem("scatter_copied"), 1)
                with act.Fori(0, EXPERTS // 8) as i:
                    two_quads(i)
                act.wait_ge(sem("moe_index"), 1)
                more = act.value_load(moe_index[0:1, EXTRA:EXTRA + 1], min_val=0, max_val=EXTRA)
                with act.If(more > 0):
                    with act.Fori(EXPERTS // 8, (EXPERTS + EXTRA) // 8) as i:
                        two_quads(i)
                act.wait_ge(x_ready, TT * 7)
                act.dma_start(finrow, a["norm_final_g_2"].unsqueeze(0).to_broadcast([P, D])
                              ).then_inc(sem("fin_in"), 16)
                norm("g", 7)

            rwkv()
            ffn(1, FIRST["ffn1"])
            gates_and_mixer()
            moe()

        @block.vector
        def _(dve):
            chained = [0]
            chain = sem("dve_chain")

            def do(ins):
                chained[0] += 1
                ins.then_inc(chain, 1)

            def settle():
                dve.wait_ge(chain, chained[0])

            def norm(m, gain=None, shift=None, split=True, before_gain=None):
                dve.wait_ge(sem("norm_ss"), nth(m))
                do(dve.tensor_scalar(rec, ss, 1.0 / D, EPS, ALU.mult, ALU.add))
                settle()
                dve.reciprocal(rec, rec).then_inc(sem("norm_rec"), 1)
                dve.wait_ge(sem("norm_rstd"), nth(m))
                for t in range(TT):
                    dve.tensor_scalar(tiles(slot(4), 2)[:, t, :], Xv[:, t, :], rstd[:, t:t + 1], None,
                                      ALU.mult).then_inc(sem("norm_xn"), 1)
                if before_gain:
                    before_gain()
                h = tiles(slot(0))
                for q in range(4):
                    dve.wait_ge(sem("norm_tp"), 4 * m + q + 1)
                    for j in (2 * q, 2 * q + 1):
                        src = ps[:, 4 + q, 256 * (j % 2):256 * (j % 2 + 1)]
                        if shift is None:
                            ins = dve.tensor_scalar(h[:, j, :], src, gain(j), None, ALU.mult)
                        else:
                            ins = dve.tensor_scalar(h[:, j, :], src, gain(j), shift(j), ALU.mult, ALU.add)
                        if split or j == 2 * q:
                            do(ins)
                    if not split:
                        ins.then_inc(sem("norm_h"), 1)
                        continue
                    settle()
                    both = slice(2 * q, 2 * q + 2)
                    do(dve.tensor_copy(HhT[:, both, :], h[:, both, :]))
                    settle()
                    dve.tensor_tensor(HlT[:, both, :], h[:, both, :], HhT[:, both, :].bitcast(F32),
                                      ALU.subtract).then_inc(sem("norm_h"), 1)
                dve.wait_ge(sem("norm_h"), 4 * m + 4)

            def add_to_x(done, count, ready):
                dve.wait_ge(done, count)
                for b in range(4):
                    ins = dve.tensor_tensor(Xv[:, b // 2, 512 * (b % 2):512 * (b % 2 + 1)], ps[:, b, :],
                                            Xv[:, b // 2, 512 * (b % 2):512 * (b % 2 + 1)], ALU.add)
                    if b % 2:
                        ins.then_inc(ready, 1)

            dve.memset(zeros, 0.0).then_inc(sem("zeros"), 1)
            dve.wait_ge(sem("cst_in"), 16)
            dve.wait_ge(sem("col_in"), 16)
            norm(0, lambda j: colv("norm_mix0", j))
            v = slot(5, 2).rearrange("p (t d) -> p t d", t=TT)
            bin_row = slot(7)
            dve.wait_ge(sem("bin_in"), 16)
            for c in range(8):
                dve.wait_ge(used, FIRST["sgu_v"] + c + 1)
                dve.tensor_tensor(v[:, :, 256 * c:256 * (c + 1)], ps[:, c % 4, :].rearrange("p (t n) -> p t n", t=TT),
                                  bin_row[:, 256 * c:256 * (c + 1)].unsqueeze(1).to_broadcast([P, TT, 256]),
                                  ALU.add).then_inc(sem("v_biased"), 1)
            wsT = slot(10)
            dve.wait_ge(sem("ws_in"), 16)
            dve.memset(tiles(wsT, SG)[CH:P, :, 0:CH], 0.0).then_inc(sem("ws_masked"), 1)
            dve.wait_ge(sem("v_gelu"), 8)
            for t in range(TT):
                for q in range(4):
                    do(dve.bn_stats(bns[:, (4 * t + q) * 6:(4 * t + q + 1) * 6], v[:, t, 512 * q:512 * (q + 1)]))
            settle()
            for t in range(TT):
                do(dve.bn_aggr(bna[:, 2 * t:2 * t + 2], bns[:, 24 * t:24 * t + 24]))
            settle()
            mv = bna.rearrange("p (t s) -> p t s", s=2)
            do(dve.tensor_scalar(rec.unsqueeze(2), mv[:, :, 1:2], LN_EPS, None, ALU.add))
            settle()
            dve.reciprocal(rec, rec).then_inc(sem("v_rec"), 1)
            gate_b = tiles(slot(1), SG)
            dve.wait_ge(sem("bs_in"), 16)
            dve.wait_ge(sem("rowsum_mm"), 1)
            for g in range(SG):
                ins = dve.scalar_tensor_tensor(gate_b[:, g, :], ps[:, g // 4, 128 * (g % 4):128 * (g % 4 + 1)],
                                               colv("sgu_ln_b", g), gate_b[:, g, :], ALU.mult, ALU.add)
            ins.then_inc(sem("gate_b"), 1)
            dve.wait_ge(sem("v_rstd"), 1)
            for t in range(TT):
                dve.tensor_scalar(v[:, t, :], v[:, t, :], bna[:, 2 * t:2 * t + 1], rstd[:, t:t + 1],
                                  ALU.subtract, ALU.mult).then_inc(sem("v_norm"), 1)
            dve.wait_ge(sem("gate_b"), 1)
            dve.wait_ge(sem("u_gelu"), 8)
            uT = slot(8, 2).rearrange("p (g t) -> p g t", g=SG)
            for q in range(8):
                tmp = slot(4)[:, 512 * (q % 2):512 * (q % 2) + 512]
                dve.wait_ge(sem("gate_mm"), q + 1)
                for g in (2 * q, 2 * q + 1):
                    src = ps[:, 4 + q % 4, 256 * (g % 2):256 * (g % 2 + 1)].rearrange("p (n i) -> p n i", n=TT)
                    do(dve.scalar_tensor_tensor(
                        tmp[:, 256 * (g % 2):256 * (g % 2 + 1)].rearrange("p (n i) -> p n i", n=TT), src,
                        colv("sgu_ln_g", g), gate_b[:, g, :].unsqueeze(1).to_broadcast([P, TT, P]),
                        ALU.mult, ALU.add))
                settle()
                two = uT[:, 2 * q:2 * q + 2, :].rearrange("p g t -> p (g t)")
                do(dve.tensor_tensor(tmp, tmp, two, ALU.mult))
                if q >= 2:
                    dve.wait_ge(used, FIRST["sgu_out"] + q - 1)
                settle()
                yh, yl = Ah[:, 512 * (q % 2):512 * (q % 2) + 512], Al[:, 512 * (q % 2):512 * (q % 2) + 512]
                do(dve.tensor_copy(yh, tmp))
                settle()
                dve.tensor_tensor(yl, tmp, yh.bitcast(F32), ALU.subtract).then_inc(sem("gate_y"), 1)
            add_to_x(used, FIRST["ffn0"], x_ready)

            def ffn(layer):
                m = 1 if layer == 0 else 3
                norm(m, lambda j: colv(f"norm_ffn{layer}", j))

                def squared(i, j):
                    r = slot(4)[:, 512 * j:512 * (j + 1)]
                    sq = slot(4)[:, 1024 + 512 * j:1024 + 512 * (j + 1)]
                    fh, fl = Fh[:, 512 * j:512 * (j + 1)], Fl[:, 512 * j:512 * (j + 1)]
                    dve.wait_ge(sem("ffn_relu"), i * 2 + (16 * layer + j + 1))
                    dve.tensor_tensor(sq, r, r, ALU.mult).then_inc(sem("ffn_sq"), 1)
                    dve.wait_ge(sem("ffn_sq"), i * 4 + (32 * layer + 2 * j + 1))
                    dve.tensor_copy(fh, sq).then_inc(sem("ffn_sq"), 1)
                    dve.wait_ge(sem("ffn_sq"), i * 4 + (32 * layer + 2 * j + 2))
                    dve.tensor_tensor(fl, sq, fh.bitcast(F32), ALU.subtract).then_inc(sem("ffn_hid"), 1)

                if layer == 1:
                    dve.memset(scr[:, 0:1], 0.0).then_inc(sem("ada_used"), 3)
                    dve.wait_ge(sem("c_sigmoid"), 1)
                    do(dve.tensor_tensor(cact, cact, col[:, COL["c"]:COL["c"] + KT], ALU.mult))
                    settle()

                def ada(i, j):
                    buf = slot(8 + j)
                    dve.wait_ge(sem(f"ada_in{j}"), i * 16 + 16)
                    dve.tensor_tensor(tiles(buf), tiles(buf), cact.unsqueeze(2).to_broadcast([P, KT, 256]),
                                      ALU.mult).then_inc(sem("ada_prod"), 1)
                    dve.wait_ge(sem("ada_prod"), i * 3 + (j + 1))
                    dve.tensor_reduce(macc[:, bass.ds(i * 768 + 256 * j, 256)], buf.rearrange("p (k n) -> p n k", k=KT),
                                      AX.X, ALU.add).then_inc(sem("ada_used"), 1)

                with dve.Fori(0, FFN // 512) as i:
                    for j in range(2):
                        squared(i, j)
                        if layer == 1:
                            ada(i, j)
                    if layer == 1:
                        ada(i, 2)
                add_to_x(used, FIRST["rwkv_k"] if layer == 0 else FIRST["in2"], x_ready)

            def mixed(dst, p):
                for j in range(KT):
                    ins = dve.scalar_tensor_tensor(dst[:, j, :], r_xx[:, j, :], colv("mu", 8 * p + j),
                                                   r_h[:, j, :], ALU.mult, ALU.add)
                return ins

            def split(src, ready):
                for q in range(4):
                    both = slice(2 * q, 2 * q + 2)
                    do(dve.tensor_copy(HhT[:, both, :], src[:, both, :]))
                    settle()
                    dve.tensor_tensor(HlT[:, both, :], src[:, both, :], HhT[:, both, :].bitcast(F32),
                                      ALU.subtract).then_inc(ready, 1)

            def flat(t):
                return t.rearrange("p k t -> p (k t)")

            def rwkv():
                norm(2, lambda j: colv("norm_mix1", j), split=False)
                do(dve.tensor_tensor(r_xx[:, :, 1:SEQ], r_h[:, :, 0:SEQ - 1], r_h[:, :, 1:SEQ], ALU.subtract))
                do(dve.tensor_scalar(r_xx[:, :, 0:1], r_h[:, :, 0:1], -1.0, None, ALU.mult))
                settle()
                mixed(r_xs, 3).then_inc(sem("xs"), 1)
                mixed(r_xsa, 4).then_inc(sem("xs"), 1)
                mixed(r_xsg, 5).then_inc(sem("xs"), 1)
                dve.wait_ge(sem("lora_mm"), 1)
                do(mixed(r_xs, 1))
                settle()
                dve.wait_ge(sem("lora2_mm"), 8)
                split(r_xs, sem("xs"))
                dve.wait_ge(sem("lora_sigmoid"), 4)
                for j in range(KT):
                    do(dve.tensor_tensor_scan(r_cum[:, j, :], cc("not_chunk_start"), r_sg[:, j, :], 0.0,
                                              ALU.mult, ALU.add))
                settle()
                dve.tensor_tensor(slot(5), slot(6), slot(5), ALU.subtract).then_inc(sem("cum_excl"), 1)
                dve.wait_ge(sem("lora_mm"), 3)
                for c in range(4):
                    dve.wait_ge(sem("rwkv_copied"), c + 1)
                    for j in (2 * c, 2 * c + 1):
                        do(dve.tensor_scalar(r_kk[:, j, :], r_k[:, j, :], colv("k_k", j), None, ALU.mult))
                settle()
                dve.tensor_tensor(slot(4), slot(10), slot(10), ALU.mult).then_inc(sem("kk_sq"), 1)
                dve.wait_ge(sem("kk_norm"), 1)
                do(dve.tensor_scalar(r_norm, r_norm, 1e-12, None, ALU.max))
                settle()
                dve.reciprocal(r_norm, r_norm).then_inc(sem("kk_rinv"), 1)
                do(mixed(r_xs, 0))
                settle()
                dve.wait_ge(used, FIRST["rwkv_r"])
                split(r_xs, sem("xs"))
                for q in range(4):
                    dve.wait_ge(sem("rinv_mm"), q + 1)
                    two = slot(10)[:, 512 * q:512 * (q + 1)]
                    do(dve.tensor_tensor(two, ps[:, q, :], two, ALU.mult))
                dve.wait_ge(sem("lora_sigmoid"), 8)
                settle()
                dve.wait_ge(sem("W_excl"), 1)
                do(dve.scalar_tensor_tensor(slot(5), slot(10), -1.0, slot(5), ALU.mult, ALU.mult))
                settle()
                do(dve.tensor_tensor(slot(10), slot(10), slot(7), ALU.mult))
                settle()
                for j in range(KT):
                    do(dve.tensor_scalar(r_a[:, j, :], r_a[:, j, :], 1.0, colv("k_a", j), ALU.subtract, ALU.mult))
                settle()
                dve.scalar_tensor_tensor(slot(9), slot(7), 1.0, slot(9), ALU.add, ALU.mult
                                         ).then_inc(sem("k_new"), 1)
                do(mixed(r_xs, 2))
                settle()
                dve.wait_ge(used, FIRST["rwkv_v"])
                split(r_xs, sem("xs"))
                dve.wait_ge(sem("xs"), 15)
                dve.memset(scr[:, 0:1], 0.0).then_inc(sem("tmp_free"), 1)
                dve.wait_ge(sem("rwkv_copied"), 8)
                dve.wait_ge(sem("k_new"), 1)
                for j in range(KT):
                    ins = dve.scalar_tensor_tensor(r_prod[:, j, :], r_r[:, j, :], colv("r_k", j), r_k[:, j, :],
                                                   ALU.mult, ALU.mult)
                ins.then_inc(sem("bonus_prod"), 1)
                dve.wait_ge(sem("bonus_prod"), 1)
                dve.wait_ge(sem("W_inv"), 1)
                do(dve.tensor_tensor(slot(10), slot(10), slot(4), ALU.mult))
                do(dve.tensor_tensor(slot(9), slot(9), slot(4), ALU.mult))
                dve.wait_ge(sem("W"), 1)
                do(dve.tensor_copy(wend.rearrange("p (j c) -> p j c", c=NCH), r_cum[:, :, CH - 1:SEQ:CH]))
                do(dve.tensor_tensor(slot(7), slot(7), slot(6), ALU.mult))
                settle()
                dve.memset(scr[:, 1:2], 0.0).then_inc(sem("scaled"), 1)
                dve.wait_ge(sem("bonus_mm"), 1)
                dve.tensor_copy(bonus, ps[:, 3, 0:32]).then_inc(sem("bonus_copied"), 1)
                for m, (name, _, _, mask) in enumerate(MATRICES):
                    for g in range(4):
                        idx = 4 * m + g
                        dve.wait_ge(sem("mat_mm"), idx + 1)
                        dve.tensor_tensor(
                            MATRIX_OUT[name][:, g // 2, g % 2::2, :],
                            ps[:, idx % 4, :].rearrange("p (h s) -> p h s", h=8),
                            cc(mask).unsqueeze(1).to_broadcast([P, 8, CH]), ALU.mult).then_inc(sem("mat_done"), 1)

                def per_head(t, i):
                    return t[:, i // 2, 8 * (i % 2):8 * (i % 2 + 1), :]

                def wide(ap):
                    return ap.unsqueeze(1).to_broadcast([P, 8, CH])
                dve.wait_ge(sem("mat_done"), 20)
                dve.wait_ge(sem("token_major_mm"), 8)
                for g in range(4):
                    do(dve.tensor_tensor(per_head(r_X, g), per_head(r_M, g), wide(cc("level1_lower")), ALU.mult))
                    do(dve.tensor_tensor(per_head(r_Y, g), per_head(r_Y, g), wide(cc("level_upper", 0, CH)), ALU.mult))
                settle()
                for g in range(4):
                    do(dve.tensor_tensor(per_head(r_X, g), per_head(r_X, g), wide(cc("ident64")), ALU.add))
                    do(dve.tensor_tensor(per_head(r_Y, g), per_head(r_Y, g), wide(cc("ident64")), ALU.add))
                settle()
                dve.memset(scr[:, 2:3], 0.0).then_inc(sem("inv_start"), 1)
                for lv in range(1, 6):
                    def q_part(g):
                        dve.wait_ge(sem("invQ_mm"), 4 * (lv - 1) + g + 1)
                        dve.tensor_tensor(r_Q[:, g % 2, :, :], ps[:, g % 2, :].rearrange("p (h s) -> p h s", h=8),
                                          wide(cc("level_upper", CH * lv, CH)), ALU.mult).then_inc(sem("invQ"), 1)

                    def y_part(g):
                        dve.wait_ge(sem("invY_mm"), 4 * (lv - 1) + g + 1)
                        ins = dve.tensor_tensor(per_head(r_Y, g), ps[:, 2 + g % 2, :].rearrange("p (h s) -> p h s", h=8),
                                                per_head(r_Y, g), ALU.add)
                        if lv < 5:
                            ins = dve.tensor_tensor(per_head(r_X, g),
                                                    ps[:, 4 + g % 2, :].rearrange("p (h s) -> p h s", h=8),
                                                    per_head(r_X, g), ALU.add)
                        ins.then_inc(sem("invY"), 1)
                    q_part(0)
                    for g in range(1, 4):
                        q_part(g)
                        y_part(g - 1)
                    y_part(3)

                for g in range(4):
                    dve.wait_ge(sem("U_mm"), g + 1)
                    dve.tensor_copy(per_head(r_U, g), ps[:, 4 + g, :].rearrange("p (h s) -> p h s", h=8)
                                    ).then_inc(sem("U"), 1)
                dve.wait_ge(sem("U"), 4)
                for c in range(NCH):
                    rows, t = slice(CH * (c % 2), CH * (c % 2 + 1)), c // 2

                    def bank(b):
                        return ps[rows, b, :].rearrange("p (j s) -> p j s", j=KT)
                    for g in range(2):
                        if c > 0:
                            dve.wait_ge(sem("R_mm"), 2 * (c - 1) + g + 1)
                            dve.tensor_tensor(r_RS[rows, 0, g::2, :], bank(g), r_U[rows, t, g::2, :],
                                              ALU.add).then_inc(sem("R"), 1)
                    for g in range(2):
                        dve.wait_ge(sem("SA_mm"), 2 * c + g + 1)
                        dve.tensor_copy(r_RS[rows, 1, g::2, :], bank(2 + g)).then_inc(sem("SA"), 1)
                    if c < NCH - 1:
                        dve.wait_ge(sem("Z_mm"), c + 1)
                        new, old = r_Z[:, (c + 1) % 2, :, :], r_Z[:, c % 2, :, :]
                        src = ps[:, 6, :].rearrange("p (j v) -> p j v", j=KT)
                        decay = wend.rearrange("p (j c) -> p j c", c=NCH)[:, :, c:c + 1].to_broadcast([P, KT, HD])
                        if c > 0:
                            do(dve.tensor_tensor(new, src, old, ALU.add))
                            settle()
                            dve.tensor_tensor(new, new, decay, ALU.mult).then_inc(sem("Z"), 1)
                        else:
                            dve.tensor_tensor(new, src, decay, ALU.mult).then_inc(sem("Z"), 1)
                        dve.wait_ge(sem("Z"), c + 1)
                    for g in range(2):
                        dve.wait_ge(sem("y_mm"), 2 * c + g + 1)
                        y = r_y[rows, t, g::2, :]
                        if c > 0:
                            dve.wait_ge(sem("y_state"), 2 * (c - 1) + g + 1)
                            dve.tensor_tensor(y, bank(4 + g), y, ALU.add).then_inc(sem("y_done"), 1)
                        else:
                            dve.tensor_copy(y, bank(4 + g)).then_inc(sem("y_done"), 1)

                y, y2 = slot(3).rearrange("p (g v) -> p g v", v=HD), slot(2).rearrange("p (g v) -> p g v", v=HD)
                mean, var = gst[:, 0:32], gst[:, 32:64]

                def per_group(ap):
                    return ap.unsqueeze(2).to_broadcast([P, 32, HD])
                dve.wait_ge(sem("y_done"), 2 * NCH)
                do(dve.tensor_reduce(mean, y, AX.X, ALU.add))
                settle()
                do(dve.tensor_scalar(mean, mean, 1.0 / HD, None, ALU.mult))
                settle()
                do(dve.tensor_tensor(y, y, per_group(mean), ALU.subtract))
                settle()
                dve.wait_ge(sem("y_mm"), 2 * NCH)
                do(dve.tensor_tensor(y2, y, y, ALU.mult))
                settle()
                do(dve.tensor_reduce(var, y2, AX.X, ALU.add))
                settle()
                do(dve.tensor_scalar(var, var, 1.0 / HD, GN_EPS, ALU.mult, ALU.add))
                settle()
                dve.reciprocal(var, var).then_inc(sem("gn_rec"), 1)
                do(dve.tensor_tensor(y2, slot(0).rearrange("p (g v) -> p g v", v=HD), per_group(bonus), ALU.mult))
                dve.wait_ge(sem("gn_rstd"), 1)
                do(dve.tensor_tensor(y, y, per_group(var), ALU.mult))
                settle()
                dve.wait_ge(sem("ln_in"), 32)
                y3 = tiles(slot(3), TT)
                do(dve.tensor_tensor(y3, y3, r_lnrow[:, 0:1, :].to_broadcast([P, TT, D]), ALU.mult))
                settle()
                do(dve.tensor_tensor(y3, y3, r_lnrow[:, 1:2, :].to_broadcast([P, TT, D]), ALU.add))
                settle()
                do(dve.tensor_tensor(slot(3), slot(3), slot(2), ALU.add))
                settle()
                for t in range(TT):
                    dve.wait_ge(sem("g_mm"), t + 1)
                    for half in range(2):
                        o = y3[:, t, 512 * half:512 * (half + 1)]
                        ins = dve.tensor_tensor(o, ps[:, 2 * t + half, :], o, ALU.mult)
                    ins.then_inc(sem("y_out"), 1)
                transposed_split("rwkv", ChT, ClT)
                add_to_x(used, FIRST["ffn1"], x_ready)

            def ada_columns():
                dve.wait_ge(sem("gate_in"), 32)
                dve.wait_ge(sem("gate_mm"), 9)
                for m in range(2):
                    at = 3 * KT * m
                    do(dve.tensor_tensor(modcol[:, at:at + 2 * KT], ps[:, 7, at:at + 2 * KT],
                                         col[:, COL["b_ada"] + at:COL["b_ada"] + at + 2 * KT], ALU.add))
                for b in range(4):
                    row = gates[:, b // 2, 512 * (b % 2):512 * (b % 2 + 1)]
                    do(dve.tensor_tensor(row, ps[:, b, :], row, ALU.add))
                settle()
                for m, name in enumerate(("norm_mix2", "norm_ffn2")):
                    do(dve.scalar_tensor_tensor(gain2[:, 8 * m:8 * m + 8], modcol[:, 24 * m + 8:24 * m + 16], 1.0,
                                                col[:, COL[name]:COL[name] + 8], ALU.add, ALU.mult))
                settle()
                dve.memset(scr[:, 0:1], 0.0).then_inc(sem("gates_done"), 1)

            def final_norm(m, count, row, ready):
                dve.wait_ge(sem("norm_ss"), nth(m))
                do(dve.tensor_scalar(rec, ss, 1.0 / D, EPS, ALU.mult, ALU.add))
                settle()
                dve.reciprocal(rec, rec).then_inc(sem("norm_rec"), 1)
                dve.wait_ge(sem("fin_in"), count)
                dve.wait_ge(sem("norm_rstd"), nth(m))
                for t in range(TT):
                    dve.scalar_tensor_tensor(Xv[:, t, :], Xv[:, t, :], rstd[:, t:t + 1], row, ALU.mult, ALU.mult
                                             ).then_inc(ready, 1)

            def gated_add(m, done, count, ready):
                dve.wait_ge(done, count)
                tmp = slot(4)
                for t in range(TT):
                    for b in (2 * t, 2 * t + 1):
                        do(dve.tensor_tensor(tmp[:, 512 * b:512 * (b + 1)], ps[:, b, :],
                                             gates[:, m, 512 * (b % 2):512 * (b % 2 + 1)], ALU.mult))
                    settle()
                    dve.tensor_tensor(Xv[:, t, :], Xv[:, t, :], tiles(tmp, TT)[:, t, :], ALU.add).then_inc(ready, 1)

            def mixer2():
                final_norm("f", 16, finrow_first, x_ready)
                dve.wait_ge(x_ready, TT * 5)
                norm(4, lambda j: gain2[:, j:j + 1], lambda j: modcol[:, j:j + 1], before_gain=ada_columns)
                z = f_tmp[:, 0:16].rearrange("p (t n) -> p t n", t=TT)
                e = f_tmp[:, 16:32].rearrange("p (t n) -> p t n", t=TT)
                dve.wait_ge(sem("small_in"), 48)
                dve.wait_ge(sem("f_mm"), 1)
                do(dve.memset(lf2, 0.0))
                do(dve.tensor_tensor(z, ps[:, 3, 0:16].rearrange("p (t n) -> p t n", t=TT),
                                     s_b[:, 0:AH].unsqueeze(1).to_broadcast([P, TT, AH]), ALU.add))
                settle()
                do(dve.tensor_scalar(e, z, -1.0, None, ALU.mult))
                settle()
                dve.tensor_tensor(e, e, z, ALU.min).then_inc(sem("f_negabs"), 1)
                do(dve.tensor_scalar(z, z, 0.0, None, ALU.min))
                settle()
                dve.wait_ge(sem("f_ln"), 2)
                do(dve.tensor_tensor(lf2[:, :, 0:AH], z, e, ALU.subtract))
                dve.tensor_tensor(lf2[:, :, 24:32], e, z, ALU.subtract).then_inc(sem("f_log"), 1)
                dve.wait_ge(sem("F_mm"), 1)
                do(dve.tensor_scalar(f_a, ps[0:16, 3, 0:SEQ], f_cols[0:16, 0:1], None, ALU.add))
                do(dve.tensor_scalar(f_b, ps[0:16, 2, 0:SEQ], f_cols[0:16, 1:2], None, ALU.add))
                settle()
                for h in range(AH):
                    ins = dve.tensor_scalar(f_bh[:, h, :], f_b, f_cols[0:16, 2 + h:3 + h], None, ALU.mult)
                ins.then_inc(sem("F_rows"), 1)
                for g in range(PG):
                    dve.wait_ge(sem("pool_mm"), g + 1)
                    if g >= 2:
                        dve.wait_ge(sem("pmix_mm"), g - 1)
                    dve.tensor_copy(pdiff[:, g % 2, :], ps[:, 4 + g % 2, 0:SEQ]).then_inc(sem("pdiff"), 1)
                    dve.wait_ge(sem("pmix_mm"), g + 1)
                    do(dve.tensor_scalar(pmix[:, g % 2, :], ps[:, 6 + g % 2, 0:SEQ], colv("pool_scale", g), None,
                                         ALU.mult))
                    settle()
                    do(dve.tensor_copy(C2hT[:, 4 + g, :], pmix[:, g % 2, :]))
                    settle()
                    dve.tensor_tensor(C2lT[:, 4 + g, :], pmix[:, g % 2, :], C2hT[:, 4 + g, :].bitcast(F32),
                                      ALU.subtract).then_inc(sem("pool_done"), 1)

                def softmax_in(h):
                    p_, st = prob[:, h % 2, :], att_stat[:, h % 2, :]
                    dve.wait_ge(sem("score_mm"), h + 1)
                    if h >= 2:
                        dve.wait_ge(sem("probT_mm"), h - 1)
                    do(dve.tensor_tensor(p_, ps[:, h % 2, 0:3 * P], causal, ALU.add))
                    settle()
                    do(dve.tensor_tensor(p_, ps[:, 2 + h % 2, 0:3 * P], p_, ALU.add))
                    settle()
                    do(dve.tensor_reduce(st[:, 0:1], p_[:, 0:P], AX.X, ALU.max, negate=True))
                    dve.tensor_reduce(st[:, 1:2], p_[:, P:3 * P], AX.X, ALU.max, negate=True
                                      ).then_inc(sem("att_max"), 1)

                def softmax_scale(h):
                    p_, st = prob[:, h % 2, :], att_stat[:, h % 2, :]
                    dve.wait_ge(sem("att_exp"), h + 1)
                    do(dve.reciprocal(st[:, 2:4], st[:, 2:4]))
                    settle()
                    do(dve.tensor_scalar(p_[:, 0:P], p_[:, 0:P], st[:, 2:3], None, ALU.mult))
                    dve.tensor_scalar(p_[:, P:3 * P], p_[:, P:3 * P], st[:, 3:4], None, ALU.mult
                                      ).then_inc(sem("prob"), 1)

                def softmax_out(h):
                    dve.wait_ge(sem("probT_mm"), h + 1)
                    if h >= 2:
                        dve.wait_ge(sem("av_mm"), h - 1)
                    dve.tensor_copy(probT[:, h % 2, :], ps[:, 4 + h % 2, 0:3 * P]).then_inc(sem("probT"), 1)
                    if h % 2:
                        dve.wait_ge(sem("av_mm"), h + 1)
                        j = h // 2
                        src = ps[:, 6 + j % 2, 0:SEQ]
                        do(dve.tensor_copy(C2hT[:, j, :], src))
                        settle()
                        dve.tensor_tensor(C2lT[:, j, :], src, C2hT[:, j, :].bitcast(F32),
                                          ALU.subtract).then_inc(sem("att_done"), 1)
                dve.wait_ge(sem("pool_done"), PG)
                softmax_in(0)
                for h in range(AH):
                    softmax_scale(h)
                    if h + 1 < AH:
                        softmax_in(h + 1)
                    softmax_out(h)
                gated_add(0, used, PIECES, x_ready)

            def moe():
                norm(5, lambda j: gain2[:, 8 + j:9 + j], lambda j: modcol[:, 24 + j:25 + j], split=False)
                logits = ro[:, 0:72].rearrange("p (t n) -> p t n", t=TT)
                lg, le = logits[:, :, 0:NG], logits[:, :, NG:].rearrange("p t (g e) -> p t g e", g=NG)

                def field(at, n):
                    return ro[:, at:at + TT * n].rearrange("p (t n) -> p t n", t=TT)
                gexp, gone, gmax, top = field(72, NG), field(80, NG), field(88, 1), field(90, 1)
                sel, one1, one2, work = field(92, NE), field(108, NE), field(124, NE), field(140, NE)
                m1, m2, e2, w1 = field(156, 1), field(158, 1), field(200, 1), field(204, 1)
                w2, rank = field(206, 1), field(208, 1)
                prod = ro[:, 256:256 + TT * EXPERTS].rearrange("p (t g e) -> p t g e", t=TT, g=NG)
                comb = ro[:, 384:384 + TT * EXPERTS].rearrange("p (t g e) -> p t g e", t=TT, g=NG)

                def spread(ap, n):
                    return ap.to_broadcast([P, TT, n])

                def step(*args, **kw):
                    do(dve.tensor_tensor(*args, **kw))
                    settle()

                def first_max(dst, src, top_value, n):
                    desc = cc("descending", 8 - n, n).unsqueeze(1).to_broadcast([P, TT, n])
                    step(dst, src, spread(top_value, n), ALU.is_equal)
                    step(dst, dst, desc, ALU.mult)
                    do(dve.tensor_reduce(rank, dst, AX.X, ALU.max))
                    settle()
                    step(dst, dst, spread(rank, n), ALU.is_equal)

                dve.wait_ge(sem("ro_mm"), 1)
                step(logits, ps[:, 6, 0:72].rearrange("p (t n) -> p t n", t=TT),
                     s_b[:, AH:].unsqueeze(1).to_broadcast([P, TT, NR]), ALU.add)
                do(dve.tensor_reduce(gmax, lg, AX.X, ALU.max))
                settle()
                dve.tensor_tensor(gexp, lg, spread(gmax, NG), ALU.subtract).then_inc(sem("ro_logits"), 1)
                first_max(gone, lg, gmax, NG)
                step(prod, le, gone.unsqueeze(3).to_broadcast([P, TT, NG, NE]), ALU.mult)
                do(dve.tensor_reduce(sel, prod.rearrange("p t g e -> p t e g"), AX.X, ALU.add))
                settle()
                do(dve.tensor_reduce(m1, sel, AX.X, ALU.max))
                settle()
                first_max(one1, sel, m1, NE)
                do(dve.scalar_tensor_tensor(work, one1, NEG, sel, ALU.mult, ALU.add))
                settle()
                do(dve.tensor_reduce(m2, work, AX.X, ALU.max))
                settle()
                dve.tensor_tensor(e2, m2, m1, ALU.subtract).then_inc(sem("ro_logits"), 1)
                first_max(one2, work, m2, NE)
                dve.wait_ge(sem("ro_exp"), 1)
                do(dve.tensor_reduce(top, gexp, AX.X, ALU.add))
                settle()
                do(dve.reciprocal(top, top))
                dve.wait_ge(sem("ro_exp"), 2)
                do(dve.tensor_scalar(w1, e2, 1.0, None, ALU.add))
                settle()
                do(dve.reciprocal(w1, w1))
                settle()
                step(w1, w1, top, ALU.mult)
                step(w2, w1, e2, ALU.mult)
                sel1, sel2, chosen, at_slot = (ro[:, 256 + 64 * n:320 + 64 * n].rearrange("p (t e) -> p t e", t=TT)
                                               for n in range(4))
                beyond = ro[:, 512:576].rearrange("p (t e) -> p t e", t=TT)
                count, extra, upto, first, base = (ro[:, 576 + 32 * n:608 + 32 * n] for n in range(5))
                table = ro[:, 736:736 + EXTRA * EXPERTS].rearrange("p (o e) -> p o e", e=EXPERTS)
                index = ro[:, 992:992 + EXTRA]
                for dst, one in ((sel1, one1), (sel2, one2)):
                    dst4 = dst.rearrange("p t (g e) -> p t g e", g=NG)
                    do(dve.tensor_copy(dst4, gone.unsqueeze(3).to_broadcast([P, TT, NG, NE])))
                    settle()
                    do(dve.tensor_tensor(dst4, dst4, one.unsqueeze(2).to_broadcast([P, TT, NG, NE]), ALU.mult))
                settle()
                dve.tensor_tensor(chosen, sel1, sel2, ALU.add).then_inc(sem("chosen"), 1)
                dve.wait_ge(sem("iota_in"), 16)
                do(dve.tensor_scalar(base, iota[:, 0:EXPERTS], float(CAP), None, ALU.mult))
                do(dve.tensor_copy(Hh[:, :], slot(4)))
                settle()
                do(dve.tensor_tensor(Hl[:, :], slot(4), Hh[:, :].bitcast(F32), ALU.subtract))
                dve.wait_ge(sem("position_mm"), 1)
                place = ps[:, 7, 0:64].rearrange("p (t e) -> p t e", t=TT)
                do(dve.tensor_copy(count, ps[:, 7, 64:96]))
                do(dve.tensor_copy(at_slot, place))
                settle()
                do(dve.tensor_scalar(beyond, at_slot, float(CAP), None, ALU.is_gt))
                do(dve.tensor_scalar(extra, count, float(CAP), None, ALU.is_gt))
                settle()
                for n in (2, 3):
                    do(dve.scalar_tensor_tensor(extra, count, float(n * CAP), extra, ALU.is_gt, ALU.add))
                    settle()
                do(dve.tensor_tensor_scan(upto, cc("ones", 0, EXPERTS), extra, 0.0, ALU.mult, ALU.add))
                settle()
                do(dve.tensor_tensor(first, upto, extra, ALU.subtract))
                settle()
                do(dve.tensor_scalar(first, first, float(CAP), float(EXPERTS * CAP - CAP), ALU.mult, ALU.add))
                settle()
                do(dve.tensor_tensor(first, first, base, ALU.subtract))
                settle()
                def per_token(ap):
                    return ap.unsqueeze(1).to_broadcast([P, TT, EXPERTS])
                step(beyond, beyond, per_token(first), ALU.mult)
                step(at_slot, at_slot, per_token(base), ALU.add)
                step(at_slot, at_slot, beyond, ALU.add)
                step(sel1, sel1, at_slot, ALU.mult)
                step(sel2, sel2, at_slot, ALU.mult)
                for n, dst in enumerate((sel1, sel2)):
                    do(dve.tensor_reduce(slots12[:, n, :], dst, AX.X, ALU.add))
                settle()
                do(dve.tensor_scalar(slots12, slots12, 1.0, None, ALU.subtract))
                settle()

                def one_hots():
                    for n in range(2):
                        for t in range(TT):
                            do(dve.tensor_scalar(G12[:, n, t, :], iota, slots12[:, n, t:t + 1], None, ALU.is_equal))
                    settle()
                    dve.tensor_tensor(Gr[:, :], G12[:, 0].rearrange("p t n -> p (t n)"),
                                      G12[:, 1].rearrange("p t n -> p (t n)"), ALU.add).then_inc(sem("one_hot"), 1)
                    do(dve.tensor_scalar(slots12, slots12, float(QUAD), None, ALU.subtract))

                one_hots()
                do(dve.tensor_copy(Yh[:, :], zeros_bf[:, 0:1].to_broadcast([P, D])))
                dve.tensor_copy(Yl[:, :], zeros_bf[:, 0:1].to_broadcast([P, D])).then_inc(sem("Y_lo"), 1)
                def split_picked(buf, part):
                    src = picked_raw[:, :].rearrange("p (k e n) -> p k e n", k=2, e=4)
                    k = 2 * (part % 2)
                    dst = picked[buf][part // 2][:, k:k + 2]
                    return src, dst[:, :, :, 0, :], dst[:, :, :, 1, :]

                do(dve.tensor_tensor(table, upto.unsqueeze(1).to_broadcast([P, EXTRA, EXPERTS]),
                                     iota[:, 0:EXTRA].unsqueeze(2).to_broadcast([P, EXTRA, EXPERTS]), ALU.is_le))
                settle()
                do(dve.tensor_reduce(index, table, AX.X, ALU.add))
                settle()
                do(dve.tensor_scalar(index, index, float(EXPERTS - 1), None, ALU.min))
                settle()
                do(dve.tensor_copy(moe_index[:, 0:EXTRA], index))
                dve.tensor_copy(moe_index[:, EXTRA:EXTRA + 1], upto[:, EXPERTS - 1:EXPERTS]).then_inc(sem("moe_index"), 1)
                dve.wait_ge(sem("expert_hi"), 2)
                dve.tensor_tensor(wlo[1][:, :], raw[1][:, :], whi[1][:, :].bitcast(F32), ALU.subtract
                                  ).then_inc(sem("up_lo"), 1)
                for part in range(4):
                    dve.wait_ge(sem("picked_raw"), part + 1)
                    src, hi_, lo_ = split_picked(0, part)
                    do(dve.tensor_copy(hi_, src))
                    settle()
                    dve.tensor_tensor(lo_, src, hi_.bitcast(F32), ALU.subtract).then_inc(sem("picked"), 1)
                dve.wait_ge(sem("wslot_mm"), 1)
                dve.tensor_copy(wslot[:, 0, :], ps[:, 2, 0:2]).then_inc(sem("wslot"), 1)
                dve.wait_ge(sem("scatter_tp"), 1)
                settle()
                one_hots()

                def lower(i, q, pair):
                    dve.wait_ge(sem("Y_hi"), i * 4 + (2 * q + pair + 1))
                    for half in range(2):
                        h = slice(512 * half, 512 * (half + 1))
                        ins = dve.scalar_tensor_tensor(Yl[:, h], ps[:, 4 + half, :], wslot[:, q, pair:pair + 1],
                                                       Yh[:, h].bitcast(F32), ALU.mult, ALU.subtract)
                    ins.then_inc(sem("Y_lo"), 1)

                def two_quads(i):
                    for q in range(2):
                        for e in range(4):
                            if e == 2:
                                lower(i, q, 0)
                            n = 4 * q + e
                            dve.wait_ge(sem("e_silu"), i * 8 + (n + 1))
                            if e == 1:
                                dve.tensor_copy(wslot[:, 1 - q, :], ps[:, 6, 4 * CAP:4 * CAP + 2]).then_inc(sem("wslot"), 1)
                            dve.tensor_tensor(e_hid, ps[:, 6, 2 * CAP:4 * CAP], e_silu, ALU.mult
                                              ).then_inc(sem("e_hid"), 1)
                            dve.wait_ge(sem("picked_raw"), i * 8 + (n + 5))
                            src, hi_, lo_ = split_picked(1 - q, e)
                            dve.tensor_copy(hi_, src).then_inc(sem("picked_hi"), 1)
                            dve.wait_ge(sem("picked_hi"), i * 8 + (n + 1))
                            dve.tensor_tensor(lo_, src, hi_.bitcast(F32), ALU.subtract).then_inc(sem("picked"), 1)
                            dve.wait_ge(sem("expert_hi"), i * 16 + (2 * n + 4))
                            dve.tensor_tensor(wlo[1][:, :], raw[2 * ((n + 1) % 2) + 1][:, :], whi[1][:, :].bitcast(F32),
                                              ALU.subtract).then_inc(sem("up_lo"), 1)
                        lower(i, q, 1)
                        dve.wait_ge(sem("scatter_tp"), i * 2 + (q + 2))
                        for w in range(2):
                            for t in range(TT):
                                ins = dve.tensor_scalar(G12[:, w, t, :], iota, slots12[:, w, t:t + 1], None, ALU.is_equal)
                        ins.then_inc(sem("G12"), 1)
                        dve.wait_ge(sem("G12"), i * 2 + (q + 1))
                        dve.tensor_scalar(slots12, slots12, float(QUAD), None, ALU.subtract).then_inc(sem("slots12"), 1)
                        dve.tensor_tensor(Gr[:, :], G12[:, 0].rearrange("p t n -> p (t n)"),
                                          G12[:, 1].rearrange("p t n -> p (t n)"), ALU.add).then_inc(sem("one_hot"), 1)
                        dve.wait_ge(sem("slots12"), i * 2 + (q + 1))
                settle()
                with dve.Fori(0, EXPERTS // 8) as i:
                    two_quads(i)
                dve.wait_ge(sem("moe_index"), 1)
                more = dve.value_load(moe_index[0:1, EXTRA:EXTRA + 1], min_val=0, max_val=EXTRA)
                with dve.If(more > 0):
                    with dve.Fori(EXPERTS // 8, (EXPERTS + EXTRA) // 8) as i:
                        two_quads(i)
                gated_add(1, sem("moe_done"), 1, x_ready)
                final_norm("g", 32, finrow, x_ready)

            def transposed_split(name, dh, dl):
                for q in range(4):
                    dve.wait_ge(sem(f"{name}_tp"), q + 1)
                    both = slice(2 * q, 2 * q + 2)
                    src = ps[:, 4 + q, :].rearrange("p (f t) -> p f t", f=2)
                    do(dve.tensor_copy(dh[:, both, :], src))
                    settle()
                    dve.tensor_tensor(dl[:, both, :], src, dh[:, both, :].bitcast(F32),
                                      ALU.subtract).then_inc(sem(f"{name}_T"), 1)

            ffn(0)
            rwkv()
            ffn(1)
            mixer2()
            moe()
            dve.wait_ge(x_ready, TT * 8)
            dve.memset(scr[:, 1:2], 0.0).then_inc(sem("out_ready"), 1)

        @block.tensor
        def _(pe):
            def mm3(o, sh, sl, mh, ml, start, stop):
                pe.matmul(o, sh, mh, start=start, stop=False, skip_group_check=True)
                pe.matmul(o, sh, ml, start=False, stop=False, skip_group_check=True)
                return pe.matmul(o, sl, mh, start=False, stop=stop, skip_group_check=True)

            def have(n, i=None, per=0):
                pe.wait_ge(lo_done, n + 1 if i is None else i * per + (n + 1))
                return n

            def feature_tiles(n, bank, xh, xl, wait_k=None):
                wh, wl = piece(whi, n, KT), piece(wlo, n, KT)
                for f in range(2):
                    for k in range(KT):
                        if wait_k and f == 0:
                            wait_k(k)
                        c = slice(P * f, P * (f + 1))
                        ins = mm3(ps[:, bank, 256 * f:256 * (f + 1)], wh[:, k, c], wl[:, k, c],
                                  xh[:, k, :], xl[:, k, :], k == 0, k == KT - 1)
                return ins

            def token_tiles(n, bank, xh, xl, wait_k=None):
                wh, wl = piece(whi, n, KT), piece(wlo, n, KT)
                for t in range(TT):
                    for k in range(KT):
                        if wait_k and t == 0:
                            wait_k(k)
                        c = slice(P * t, P * (t + 1))
                        ins = mm3(ps[:, bank, 256 * t:256 * (t + 1)], xh[:, k, c], xl[:, k, c],
                                  wh[:, k, :], wl[:, k, :], k == 0, k == KT - 1)
                return ins

            def accumulate(n, xh, xl, first, last, wait_k=None):
                wh, wl = piece(whi, n, 2), piece(wlo, n, 2)
                for k in range(2):
                    if wait_k:
                        wait_k(k)
                    for t in range(TT):
                        for half in range(2):
                            c = slice(P * t, P * (t + 1))
                            w = slice(512 * half, 512 * (half + 1))
                            ins = mm3(ps[:, 2 * t + half, :], xh[:, k, c], xl[:, k, c], wh[:, k, w], wl[:, k, w],
                                      first and k == 0, last and k == 1)
                ins.then_inc(used, 1)

            def norm(m):
                pe.wait_ge(sem("norm_xn"), TT * (m + 1))
                for q in range(4):
                    for j in (2 * q, 2 * q + 1):
                        for t in range(TT):
                            ins = pe.transpose(ps[:, 4 + q, 256 * (j % 2) + P * t:256 * (j % 2) + P * (t + 1)],
                                               tiles(slot(4), 2)[:, t, P * j:P * (j + 1)], ident)
                    ins.then_inc(sem("norm_tp"), 1)
                return lambda k: pe.wait_ge(sem("norm_h"), 4 * m + k // 2 + 1) if k % 2 == 0 else None

            pe.wait_ge(sem("cst_in"), 16)
            pe.wait_ge(sem("zeros"), 1)
            h_ready = norm(0)
            for c in range(8):
                n = have(FIRST["sgu_v"] + c)
                if c >= 4:
                    pe.wait_ge(sem("v_biased"), c - 3)
                token_tiles(n, c % 4, HhT, HlT, h_ready if c == 0 else None).then_inc(used, 1)
            for c in range(8):
                n = have(FIRST["sgu_u"] + c)
                if c >= 4:
                    pe.wait_ge(sem("u_gelu"), c - 3)
                feature_tiles(n, 4 + c % 4, HhT, HlT).then_inc(used, 1)
            pe.wait_ge(sem("ws_masked"), 1)
            pe.wait_ge(sem("v_biased"), 8)
            for q in range(4):
                ins = pe.matmul(ps[:, q, :], cc("ones"), slot(10)[:, 512 * q:512 * (q + 1)], start=True, stop=True)
            ins.then_inc(sem("rowsum_mm"), 1)
            v = slot(5, 2).rearrange("p (t d) -> p t d", t=TT)

            def gate(q):
                for g in (2 * q, 2 * q + 1):
                    for t in range(TT):
                        o = ps[:, 4 + q % 4, 256 * (g % 2) + P * t:256 * (g % 2) + P * (t + 1)]
                        ins = pe.matmul(o, v[:, t, P * g:P * (g + 1)], slot(10)[:, P * g:P * (g + 1)],
                                        start=True, stop=True)
                ins.then_inc(sem("gate_mm"), 1)
            pe.wait_ge(sem("v_norm"), TT)
            pe.wait_ge(sem("u_gelu"), 8)
            for q in range(4):
                gate(q)
            pe.wait_ge(sem("gate_b"), 1)
            for q in range(8):
                n = have(FIRST["sgu_out"] + q)
                pe.wait_ge(sem("gate_y"), q + 1)
                at = slice(512 * (q % 2), 512 * (q % 2) + 512)
                accumulate(n, tiles(Ah[:, at], 2), tiles(Al[:, at], 2), q == 0, q == 7)
                if q + 4 < 8:
                    gate(q + 4)

            def ffn(layer, base):
                m = 1 if layer == 0 else 3
                h_ready = norm(m)
                for b in range(4):
                    pe.matmul(ps[:, b, :], zeros, zero_cols, start=True, stop=False, skip_group_check=True)
                for k in range(0, KT, 2):
                    h_ready(k)
                with pe.Fori(0, FFN // 512) as i:
                    for j in range(2):
                        n = have(base + j, i, 4)
                        feature_tiles(n, 4 + j, HhT, HlT).then_inc(used, 1)
                    for j in range(2):
                        n = have(base + 2 + j, i, 4)
                        pe.wait_ge(sem("ffn_hid"), i * 2 + (16 * layer + j + 1))
                        at = slice(512 * j, 512 * (j + 1))
                        accumulate(n, tiles(Fh[:, at], 2), tiles(Fl[:, at], 2), False, False)

            def transposes(name, src):
                for q in range(4):
                    for j in (2 * q, 2 * q + 1):
                        for t in range(TT):
                            ins = pe.transpose(ps[:, 4 + q, 256 * (j % 2) + P * t:256 * (j % 2) + P * (t + 1)],
                                               src[:, t, P * j:P * (j + 1)], ident)
                    ins.then_inc(sem(f"{name}_tp"), 1)

            def fp32_k(o, w, x, k_tiles=KT):
                for k in range(k_tiles):
                    ins = pe.matmul(o, w[:, k, :], x[:, k, :], start=k == 0, stop=k == k_tiles - 1)
                return ins

            def rwkv():
                norm(2)
                pe.wait_ge(sem("lora_in"), 80)
                pe.wait_ge(sem("xs"), 1)
                fp32_k(ps[0:64, 0, 0:SEQ], r_la[:, :, 0:64], r_xs).then_inc(sem("lora_mm"), 1)
                pe.wait_ge(sem("xs"), 2)
                fp32_k(ps[64:128, 1, 0:SEQ], r_la[:, :, 64:128], r_xsa).then_inc(sem("lora_mm"), 1)
                pe.wait_ge(sem("xs"), 3)
                fp32_k(ps[:, 2, 0:SEQ], r_la[:, :, 128:256], r_xsg).then_inc(sem("lora_mm"), 1)
                for m, what in enumerate("wa"):
                    rows = slice(64 * m, 64 * (m + 1))
                    pe.wait_ge(sem("lora_mid"), m + 1)
                    for q in range(4):
                        if m:
                            pe.wait_ge(sem("lora_sigmoid"), q + 1)
                        for j in (2 * q, 2 * q + 1):
                            ins = pe.matmul(ps[:, 4 + q, 256 * (j % 2):256 * (j % 2 + 1)],
                                            r_lb[rows, P * j:P * (j + 1)], r_mid[rows, :], start=True, stop=True)
                        ins.then_inc(sem("lora2_mm"), 1)

                def xs_ready(before):
                    return lambda k: pe.wait_ge(sem("xs"), before + k // 2 + 1) if k % 2 == 0 else None
                for c in range(4):
                    n = have(FIRST["rwkv_k"] + c)
                    pe.wait_ge(sem("lora_sigmoid"), 4 + c + 1)
                    feature_tiles(n, 4 + c, HhT, HlT, xs_ready(3) if c == 0 else None).then_inc(used, 1)
                pe.wait_ge(sem("kk_sq"), 1)
                for j in range(KT):
                    ins = pe.matmul(ps[0:HEADS, 3, 0:SEQ], cc("head16", 14 - 2 * j, HEADS), r_tmp[:, j, :],
                                    start=j == 0, stop=j == KT - 1)
                ins.then_inc(sem("kk_sum_mm"), 1)
                pe.wait_ge(sem("headrows_in"), 16)
                pe.wait_ge(sem("kk_rinv"), 1)
                for q in range(4):
                    for j in (2 * q, 2 * q + 1):
                        ins = pe.matmul(ps[:, q, 256 * (j % 2):256 * (j % 2 + 1)], r_headrows[:, P * j:P * (j + 1)],
                                        r_norm, start=True, stop=True)
                    ins.then_inc(sem("rinv_mm"), 1)
                for c in range(4):
                    n = have(FIRST["rwkv_r"] + c)
                    pe.wait_ge(sem("rwkv_copied"), c + 1)
                    feature_tiles(n, 4 + c, HhT, HlT, xs_ready(7) if c == 0 else None).then_inc(used, 1)
                for c in range(4):
                    n = have(FIRST["rwkv_v"] + c)
                    pe.wait_ge(sem("rwkv_copied"), 4 + c + 1)
                    token_tiles(n, 4 + c, HhT, HlT, xs_ready(11) if c == 0 else None).then_inc(used, 1)
                pe.wait_ge(sem("bonus_prod"), 1)
                for j in range(KT):
                    for t in range(TT):
                        ins = pe.matmul(ps[:, 3, 16 * t + 2 * j:16 * t + 2 * j + 2], r_prod[:, j, P * t:P * (t + 1)],
                                        cc("head2"), start=True, stop=True)
                ins.then_inc(sem("bonus_mm"), 1)

                pe.wait_ge(sem("scaled"), 1)

                def matrix(idx):
                    _, left, right, _ = MATRICES[idx // 4]
                    t, g = idx % 4 // 2, idx % 2
                    if idx == 3:
                        pe.wait_ge(sem("bonus_copied"), 1)
                    if idx >= 4:
                        pe.wait_ge(sem("mat_done"), idx - 3)
                    f = slice(HD * g, HD * (g + 1))
                    for j in range(KT):
                        for c in (2 * t, 2 * t + 1):
                            tok = slice(CH * c, CH * (c + 1))
                            ins = pe.matmul(ps[CH * (c % 2):CH * (c % 2 + 1), idx % 4, CH * j:CH * (j + 1)],
                                            left[f, j, tok], right[f, j, tok], start=True, stop=True)
                    ins.then_inc(sem("mat_mm"), 1)

                def token_major(src, before):
                    for q in range(4):
                        pe.wait_ge(sem("rwkv_copied"), before + q + 1)
                        for j in range(4 * (q % 2), 4 * (q % 2) + 4):
                            ins = pe.transpose(ps[:, 4 + q, P * (j % 4):P * (j % 4 + 1)],
                                               src[:, j, P * (q // 2):P * (q // 2 + 1)], ident)
                        ins.then_inc(sem("token_major_mm"), 1)
                for idx in range(12):
                    matrix(idx)
                token_major(r_bt, 8)
                for idx in range(12, 20):
                    matrix(idx)
                token_major(r_kt, 12)

                def units(g):
                    for h in range(8 * (g % 2), 8 * (g % 2) + 8):
                        for half in range(2):
                            yield h, slice(CH * half, CH * (half + 1)), slice(CH * (h % 8), CH * (h % 8 + 1))
                pe.wait_ge(sem("inv_start"), 1)
                pe.wait_ge(sem("rwkv_copied"), 20)
                for lv in range(1, 6):
                    def q_part(g):
                        if lv > 1:
                            pe.wait_ge(sem("invY"), 4 * (lv - 2) + g + 1)
                        for h, rows, at in units(g):
                            ins = pe.matmul(ps[rows, g % 2, at], r_M[rows, g // 2, h, :], r_Y[rows, g // 2, h, :],
                                            start=True, stop=True)
                        ins.then_inc(sem("invQ_mm"), 1)

                    def y_part(g):
                        pe.wait_ge(sem("invQ"), 4 * (lv - 1) + g + 1)
                        if lv > 1 or g >= 2:
                            pe.wait_ge(sem("invY"), 4 * (lv - 1) + g - 1)
                        for h, rows, at in units(g):
                            ins = pe.matmul(ps[rows, 2 + g % 2, at], r_X[rows, g // 2, h, :], r_Q[rows, g % 2, h % 8, :],
                                            start=True, stop=True)
                        if lv < 5:
                            for h, rows, at in units(g):
                                ins = pe.matmul(ps[rows, 4 + g % 2, at], r_Q[rows, g % 2, h % 8, :],
                                                r_X[rows, g // 2, h, :], start=True, stop=True)
                        ins.then_inc(sem("invY_mm"), 1)
                    q_part(0)
                    for g in range(1, 4):
                        q_part(g)
                        y_part(g - 1)
                    y_part(3)

                pe.wait_ge(sem("invY"), 20)
                for g in range(4):
                    for h, rows, at in units(g):
                        ins = pe.matmul(ps[rows, 4 + g, at], r_Aak[rows, g // 2, h, :],
                                        r_v[rows, g // 2, HD * h:HD * (h + 1)], start=True, stop=True)
                    ins.then_inc(sem("U_mm"), 1)

                for c in range(NCH):
                    t, rows, tok = c // 2, slice(CH * (c % 2), CH * (c % 2 + 1)), slice(CH * c, CH * (c + 1))
                    Z = r_Z[:, c % 2, :, :]

                    def bank_heads(g):
                        for j in range(KT):
                            yield 2 * j + g, j, slice(HD * g, HD * (g + 1)), slice(CH * j, CH * (j + 1))
                    if c > 0:
                        pe.wait_ge(sem("Z"), c)
                        pe.wait_ge(sem("y_state"), 2 * (c - 1)) if c > 1 else None
                        for g in range(2):
                            for h, j, f, at in bank_heads(g):
                                ins = pe.matmul(ps[rows, g, at], r_at[f, j, tok], Z[f, j, :], start=True, stop=True)
                            ins.then_inc(sem("R_mm"), 1)
                    for g in range(2):
                        if c > 0:
                            pe.wait_ge(sem("R"), 2 * (c - 1) + g + 1)
                        else:
                            pe.wait_ge(sem("U"), 4)
                        for h, j, f, at in bank_heads(g):
                            R = r_RS[rows, 0, h, :] if c > 0 else r_U[rows, 0, h, :]
                            ins = pe.matmul(ps[rows, 2 + g, at], r_Y[rows, t, h, :], R, start=True, stop=True)
                        ins.then_inc(sem("SA_mm"), 1)
                    if c > 0:
                        for g in range(2):
                            for h, j, f, at in bank_heads(g):
                                ins = pe.matmul(ps[rows, g, at], r_rt[f, j, tok], Z[f, j, :], start=True, stop=True)
                            ins.then_inc(sem("ystate_mm"), 1)
                    pe.wait_ge(sem("SA"), 2 * c + 2)
                    if c < NCH - 1:
                        for h in range(HEADS):
                            f, j = slice(HD * (h % 2), HD * (h % 2 + 1)), h // 2
                            o = ps[f, 6, HD * j:HD * (j + 1)]
                            pe.matmul(o, r_btm[rows, t, h, :], r_RS[rows, 1, h, :], start=True, stop=False)
                            ins = pe.matmul(o, r_ktm[rows, t, h, :], r_v[rows, t, HD * h:HD * (h + 1)],
                                            start=False, stop=True)
                        ins.then_inc(sem("Z_mm"), 1)
                    for g in range(2):
                        if c > 0:
                            pe.wait_ge(sem("y_done"), 2 * (c - 1) + g + 1)
                        for h, j, f, at in bank_heads(g):
                            pe.matmul(ps[rows, 4 + g, at], r_Arb[rows, t, h, :], r_RS[rows, 1, h, :],
                                      start=True, stop=False)
                            ins = pe.matmul(ps[rows, 4 + g, at], r_Ark[rows, t, h, :],
                                            r_v[rows, t, HD * h:HD * (h + 1)], start=False, stop=True)
                        ins.then_inc(sem("y_mm"), 1)
                pe.wait_ge(sem("gb_in"), 16)
                pe.wait_ge(sem("g_sigmoid"), 1)
                pe.wait_ge(sem("y_state"), 2 * (NCH - 1))
                for t in range(TT):
                    for half in range(2):
                        ins = pe.matmul(ps[:, 2 * t + half, :], gsig[:, P * t:P * (t + 1)],
                                        r_gb[:, 512 * half:512 * (half + 1)], start=True, stop=True)
                    ins.then_inc(sem("g_mm"), 1)
                pe.wait_ge(sem("y_out"), TT)
                transposes("rwkv", tiles(slot(3), TT))
                for c in range(4):
                    n = have(FIRST["rwkv_o"] + c)
                    pe.wait_ge(sem("rwkv_T"), c + 1)
                    accumulate(n, ChT[:, 2 * c:2 * c + 2, :], ClT[:, 2 * c:2 * c + 2, :], c == 0, c == 3)

            def mixer2():
                pe.wait_ge(sem("ada_used"), 27)
                ones = cc("ones")
                for j in (*range(2 * KT), *range(3 * KT, 5 * KT)):
                    ins = pe.matmul(ps[:, 7, j:j + 1], macc[:, P * j:P * (j + 1)], ones[:, 0:1], start=True, stop=True)
                pe.wait_ge(x_ready, TT * 4)
                for b in range(4):
                    at = (2 if b < 2 else 5) * D + 512 * (b % 2)
                    ins = pe.matmul(ps[:, b, :], ones, macc[:, at:at + 512], start=True, stop=True)
                ins.then_inc(sem("gate_mm"), 1)
                pe.wait_ge(sem("gates_done"), 1)
                h_ready = norm(4)
                pe.wait_ge(sem("small_in"), 48)
                pe.wait_ge(sem("norm_h"), 20)
                for t in range(TT):
                    for k in range(KT):
                        ins = pe.matmul(ps[:, 3, AH * t:AH * (t + 1)], r_h[:, k, P * t:P * (t + 1)], w_f[:, k, :],
                                        start=k == 0, stop=k == KT - 1)
                ins.then_inc(sem("f_mm"), 1)
                for c in range(8):
                    n = have(FIRST["in2"] + c)
                    if c >= 4:
                        pe.wait_ge(sem("in2_copied"), c - 3)
                    (feature_tiles if c < 4 else token_tiles)(n, 4 + c % 4, HhT, HlT).then_inc(used, 1)
                    if c == 5:
                        pe.wait_ge(sem("f_log"), 1)
                        for b, at in ((3, 0), (2, 16)):
                            for t in range(TT):
                                ins = pe.matmul(ps[0:16, b, 0:SEQ], lf2[:, t, at:at + 16], cum[:, t, :],
                                                start=t == 0, stop=t == TT - 1)
                        ins.then_inc(sem("F_mm"), 1)
                pe.wait_ge(sem("in2_copied"), 8)
                pe.wait_ge(sem("pool_in"), 16)

                def pool_mean(g):
                    for t in range(TT):
                        ins = pe.matmul(ps[:, 4 + g % 2, 0:SEQ], utm[:, t, P * g:P * (g + 1)], poolm[:, t, g, :],
                                        start=t == 0, stop=t == TT - 1)
                    ins.then_inc(sem("pool_mm"), 1)

                def pool_mix(g):
                    pe.wait_ge(sem("pdiff"), g + 1)
                    pe.matmul(ps[:, 6 + g % 2, 0:SEQ], w_pool[:, g, :], pdiff[:, g % 2, :],
                              start=True, stop=True).then_inc(sem("pmix_mm"), 1)
                pool_mean(0)
                pool_mean(1)
                for g in range(PG):
                    if g >= 2:
                        pe.wait_ge(sem("pool_done"), g - 1)
                    pool_mix(g)
                    if g + 2 < PG:
                        pool_mean(g + 2)
                pe.wait_ge(sem("F_rows"), 1)

                def scores(h):
                    f, j = slice(HD * (h % 2), HD * (h % 2 + 1)), h // 2
                    if h >= 2:
                        pe.wait_ge(sem("att_max"), h - 1)
                    for o, t, s_ in ((slice(0, P), 0, P), (slice(P, 3 * P), 1, SEQ)):
                        tok = slice(P * t, P * (t + 1))
                        pe.matmul(ps[:, h % 2, o], qT[f, j, tok], kT[f, j, 0:s_], start=True, stop=True)
                    for o, t, s_ in ((slice(0, P), 0, P), (slice(P, 3 * P), 1, SEQ)):
                        tok = slice(P * t, P * (t + 1))
                        ins = pe.matmul(ps[:, 2 + h % 2, o], f_a[:, tok], f_bh[:, h, 0:s_], start=True, stop=True)
                    ins.then_inc(sem("score_mm"), 1)
                pe.wait_ge(sem("pool_done"), PG)
                scores(0)
                scores(1)
                for h in range(AH):
                    pe.wait_ge(sem("prob"), h + 1)
                    if h >= 2:
                        pe.wait_ge(sem("probT"), h - 1)
                    for b in range(3):
                        ins = pe.transpose(ps[:, 4 + h % 2, P * b:P * (b + 1)], prob[:, h % 2, P * b:P * (b + 1)], ident)
                    ins.then_inc(sem("probT_mm"), 1)
                    if h + 2 < AH:
                        scores(h + 2)
                    pe.wait_ge(sem("probT"), h + 1)
                    j, f = h // 2, slice(HD * (h % 2), HD * (h % 2 + 1))
                    if j >= 2:
                        pe.wait_ge(sem("att_done"), j - 1)
                    V = [vtm[:, t, HD * h:HD * (h + 1)] for t in range(TT)]
                    o, pT = ps[f, 6 + j % 2, 0:SEQ], probT[:, h % 2, :]
                    pe.matmul(o[:, 0:P], V[0], pT[:, 0:P], start=True, stop=True)
                    pe.matmul(o[:, P:SEQ], V[0], pT[:, P:2 * P], start=True, stop=False)
                    pe.matmul(o[:, P:SEQ], V[1], pT[:, 2 * P:3 * P], start=False, stop=True).then_inc(sem("av_mm"), 1)
                for c in range(4):
                    n = have(FIRST["out2"] + c)
                    if c < 2:
                        pe.wait_ge(sem("att_done"), 4)
                    accumulate(n, C2hT[:, 2 * c:2 * c + 2, :], C2lT[:, 2 * c:2 * c + 2, :], c == 0, c == 3)

            def moe():
                norm(5)
                pe.wait_ge(sem("norm_h"), 24)
                for t in range(TT):
                    for k in range(KT):
                        ins = pe.matmul(ps[:, 6, NR * t:NR * (t + 1)], r_h[:, k, P * t:P * (t + 1)], w_r[:, k, :],
                                        start=k == 0, stop=k == KT - 1)
                ins.then_inc(sem("ro_mm"), 1)
                pe.wait_ge(sem("chosen"), 1)
                chosen = ro[:, 384:448].rearrange("p (t e) -> p t e", t=TT)
                for t in range(TT):
                    for s_ in range(TT):
                        pe.matmul(ps[:, 7, EXPERTS * t:EXPERTS * (t + 1)], cum[:, s_, P * t:P * (t + 1)],
                                  chosen[:, s_, :], start=s_ == 0, stop=s_ == TT - 1)
                for s_ in range(TT):
                    ins = pe.matmul(ps[:, 7, 64:64 + EXPERTS], cc("ones"), chosen[:, s_, :],
                                    start=s_ == 0, stop=s_ == TT - 1)
                ins.then_inc(sem("position_mm"), 1)

                def gather(part, bank, halves=(0, 1)):
                    for f in halves:
                        k = 2 * part + f
                        n = 0
                        for x in (XhT, XlT):
                            for t in range(TT):
                                ins = pe.matmul(ps[:, bank, QUAD * f:QUAD * (f + 1)], x[:, t, P * k:P * (k + 1)],
                                                GrT[:, t, :], start=n == 0, stop=n == 3)
                                n += 1
                    if f == 1:
                        ins.then_inc(sem("gather_mm"), 1)

                def slot_weights(bank, at):
                    token_weight = [ro[:, 204:206], ro[:, 206:208]]
                    for pair in range(2):
                        n = 0
                        for w in range(2):
                            for t in range(TT):
                                ins = pe.matmul(ps[:, bank, at + pair:at + pair + 1],
                                                G12[:, w, t, P * pair:P * (pair + 1)], token_weight[w][:, t:t + 1],
                                                start=n == 0, stop=n == 3)
                                n += 1
                    return ins

                def scatter_transposes(bank):
                    for pair in range(2):
                        for t in range(TT):
                            ins = pe.transpose(ps[:, bank, SEQ * pair + P * t:SEQ * pair + P * (t + 1)],
                                               GrT[:, t, P * pair:P * (pair + 1)].bitcast(F32), ident)
                    ins.then_inc(sem("scatter_tp"), 1)

                def scatter_add(buf, pair):
                    for t in range(TT):
                        w = scatter[buf][:, SEQ * pair + P * t:SEQ * pair + P * (t + 1)]
                        for half in range(2):
                            h = slice(512 * half, 512 * (half + 1))
                            pe.matmul(ps[:, 2 * t + half, :], w, Yh[:, h], start=False, stop=False,
                                      skip_group_check=True)
                            pe.matmul(ps[:, 2 * t + half, :], w, Yl[:, h], start=False, stop=False,
                                      skip_group_check=True)

                pe.wait_ge(sem("one_hot"), 1)
                for part in range(4):
                    gather(part, 4 + part)
                slot_weights(2, 0).then_inc(sem("wslot_mm"), 1)
                scatter_transposes(3)
                pe.wait_ge(sem("wslot"), 1)
                pe.wait_ge(sem("scatter_copied"), 1)
                for b in range(4):
                    pe.matmul(ps[:, b, :], zeros, zero_cols, start=True, stop=False, skip_group_check=True)
                pe.wait_ge(sem("Y_lo"), 1)

                def two_quads(i):
                    for q in range(2):
                        for e in range(4):
                            n = 4 * q + e
                            if e == 0:
                                pe.wait_ge(sem("picked"), i * 8 + (4 * q + 4))
                            for m, ready, done in ((0, "gate_lo", "expert_gate_mm"), (1, "up_lo", "gate_up_mm")):
                                pe.wait_ge(sem(ready), i * 8 + (n + 1))
                                wh, wl = piece(whi, m, KT), piece(wlo, m, KT)
                                for k in range(KT):
                                    x = picked[q][k // 4][:, k % 4, e, :, :]
                                    at = slice(DE * m, DE * (m + 1))
                                    pe.matmul(ps[:, 6, at], x.rearrange("p s n -> p (s n)"), wh[:, k, :],
                                              start=k == 0, stop=False, skip_group_check=True)
                                    ins = pe.matmul(ps[0:CAP, 6, at], x[:, 0, :], wl[:, k, :],
                                                    start=False, stop=k == KT - 1, skip_group_check=True)
                                ins.then_inc(sem(done), 1)
                            if e == 0:
                                pe.wait_ge(sem("one_hot"), i * 2 + (q + 2))
                                pe.wait_ge(sem("scatter_copied"), i * 2 + (q + 1))
                            else:
                                pe.wait_ge(sem("picked_raw"), i * 8 + (4 * q + 4 + e))
                            gather(e, 7, (0,))
                            pe.wait_ge(sem("e_parts"), i * 8 + (n + 1))
                            for f in range(4):
                                ins = pe.matmul(ps[:, 6, CAP * f:CAP * (f + 1)], e_parts[:, P * f:P * (f + 1)],
                                                cc("ident64"), start=True, stop=True)
                            if e == 1:
                                ins = slot_weights(6, 4 * CAP)
                            ins.then_inc(sem("e_sum_mm"), 1)
                            gather(e, 7, (1,))
                            if e % 2 == 0:
                                pe.wait_ge(sem("Y_lo"), i * 4 + (2 * q + e // 2 + 1))
                                scatter_add(q if e else 1 - q, 0 if e else 1)
                            pe.wait_ge(sem("e_hid"), i * 8 + (4 * q + e + 1))
                            pe.wait_ge(sem(f"down_in{e % 2}"), i * 64 + 16 * (n // 2 + 1))
                            w = w_down_in[e % 2][:, :].rearrange("p (k n) -> p k n", k=2)
                            rows = slice(CAP * (e % 2), CAP * (e % 2 + 1))
                            for half in range(2):
                                for k in range(2):
                                    ins = pe.matmul(ps[rows, 4 + half, :], e_hid[:, CAP * k:CAP * (k + 1)],
                                                    w[:, k, 512 * half:512 * (half + 1)], start=k == 0, stop=k == 1)
                            ins.then_inc(sem("expert_done"), 1)
                        pe.wait_ge(sem("picked_raw"), i * 8 + (4 * q + 8))
                        scatter_transposes(7)
                with pe.Fori(0, EXPERTS // 8) as i:
                    two_quads(i)
                pe.wait_ge(sem("Y_lo"), EXPERTS // 2 + 1)
                pe.wait_ge(sem("moe_index"), 1)
                more = pe.value_load(moe_index[0:1, EXTRA:EXTRA + 1], min_val=0, max_val=EXTRA)
                with pe.If(more > 0):
                    with pe.Fori(EXPERTS // 8, (EXPERTS + EXTRA) // 8) as i:
                        two_quads(i)
                    pe.wait_ge(sem("Y_lo"), (EXPERTS + EXTRA) // 2 + 1)
                scatter_add(1, 1)
                for b in range(4):
                    ins = pe.matmul(ps[:, b, :], zeros, zero_cols, start=False, stop=True, skip_group_check=True)
                ins.then_inc(sem("moe_done"), 1)

            ffn(0, FIRST["ffn0"])
            rwkv()
            ffn(1, FIRST["ffn1"])
            mixer2()
            moe()


def kernel(**inputs):
    import concourse.bacc as bacc
    from concourse.bass_utils import run_bass_kernel_spmd

    def columns(v):
        return np.asarray(v, np.float32).reshape(-1, P).T

    g = {k: np.asarray(v) for k, v in inputs.items()}
    parts = {"norm_mix0": g["norm_mix_g"][0], "norm_mix1": g["norm_mix_g"][1],
             "norm_ffn0": g["norm_ffn_g"][0], "norm_ffn1": g["norm_ffn_g"][1],
             "b_in_u": g["sgu_b_in"][0, :SGU], "sgu_ln_g": g["sgu_ln_g"], "sgu_ln_b": g["sgu_ln_b"],
             "mu": g["rwkv_mu"], "w0": g["rwkv_w0"], "a0": g["rwkv_a0"], "k_k": g["rwkv_k_k"],
             "k_a": g["rwkv_k_a"], "r_k": g["rwkv_r_k"], "norm_mix2": g["norm_mix_g_2"],
             "norm_ffn2": g["norm_ffn_g_2"], "pool_scale": g["pool_scale_2"], "c": g["c_2"], "b_ada": g["b_ada_2"]}
    arrays = {name: np.ascontiguousarray(g[name]) for name in DIRECT}
    arrays["cols"] = np.ascontiguousarray(np.concatenate([columns(parts[name]) for name, _ in COLS], 1))
    arrays["consts"] = shape_constants()
    arrays["iota"] = np.ascontiguousarray(np.broadcast_to(np.arange(QUAD, dtype=np.float32), (P, QUAD)))
    arrays["head_rows"] = head_rows()
    arrays["attention_consts"] = attention_constants()
    arrays["pool_matrices"] = pool_matrices().reshape(P, TT * PG * SEQ)

    def rows(w):
        return w.reshape(KT, P, -1).transpose(1, 0, 2)
    router = np.concatenate([g["w_router_group_2"][0], *g["w_router_expert_2"][0]], 1)
    arrays["w_small"] = np.ascontiguousarray(np.concatenate(
        [rows(g["w_in_2"][0][:, 3 * AW:3 * AW + AH]).reshape(P, -1), rows(router).reshape(P, -1),
         g["w_pool_2"][0].transpose(1, 0, 2).reshape(P, -1)], 1))
    arrays["b_small"] = np.concatenate([g["b_fgate_2"].reshape(1, -1), g["b_router_group_2"].reshape(1, -1),
                                        g["b_router_expert_2"].reshape(1, -1)], 1)
    arrays["sgu_w_sT"] = np.ascontiguousarray(g["sgu_w_s"][0].transpose(2, 0, 1).reshape(P, SG * P))

    nc = bacc.Bacc("TRN2", target_bir_lowering=False, num_devices=1)
    dram = {name: nc.dram_tensor(f"in_{name}", v.shape, mybir.dt.from_np(v.dtype), kind="ExternalInput").ap()
            for name, v in arrays.items()}
    out = nc.dram_tensor("out", (1, SEQ, D), F32, kind="ExternalOutput").ap()
    build(nc, dram, out)
    r = run_bass_kernel_spmd(nc, [{f"in_{name}": v for name, v in arrays.items()}], core_ids=[0])
    return r.results[0]["out"]
```
